# Optimizing a Trainium2 kernel written in Bass

```python
import numpy as np
import jax, jax.numpy as jnp
from jax import lax
import jax
import jax.numpy as jnp

D_MODEL = 1024
BATCH = 1
SEQ = 512
DEPTH = 2

ROPE_THETA = 500000.0
NORM_EPS = 1e-6
Q_BLOCK = 128
MLA_HEADS = 8
MLA_NOPE_DIM = 64
MLA_ROPE_DIM = 32
MLA_QK_DIM = MLA_NOPE_DIM + MLA_ROPE_DIM
MLA_V_DIM = 64
MLA_Q_RANK = 384
MLA_KV_RANK = 256
CONV_CH = 512
CONV_WIDTH = 31
NSA_HEADS = 8
NSA_KV_GROUPS = 2
NSA_HEAD_DIM = 64
NSA_ROPE_DIM = NSA_HEAD_DIM // 4
NSA_N_BRANCH = 3
CMP_BLOCK = 32
CMP_STRIDE = 16
CMP_HIDDEN = 128
SLC_BLOCK = 64
SLC_TOP_N = 16
WINDOW = 512
NSA_Q_BLOCK = 64
FORCED_BLOCK_SCORE = 1e6
N_MIXERS = 3
D_FF = 4 * D_MODEL

IN_SPLITS = (
    MLA_Q_RANK,
    MLA_KV_RANK,
    MLA_ROPE_DIM,
    2 * CONV_CH,
    NSA_HEADS * NSA_HEAD_DIM,
    2 * NSA_N_BRANCH * NSA_KV_GROUPS * NSA_HEAD_DIM,
    NSA_N_BRANCH * NSA_HEADS,
    N_MIXERS * D_MODEL,
)
D_IN = sum(IN_SPLITS)
SPLIT_IDX = tuple(int(v) for v in np.cumsum(IN_SPLITS)[:-1])


def rms_norm(x, g):
    xf = x.astype(jnp.float32)
    y = xf * lax.rsqrt(jnp.mean(xf * xf, axis=-1, keepdims=True) + NORM_EPS)
    return (y * g.astype(jnp.float32)).astype(x.dtype)

def layer_norm(x, g, b):
    xf = x.astype(jnp.float32)
    mu = jnp.mean(xf, axis=-1, keepdims=True)
    var = jnp.mean(jnp.square(xf - mu), axis=-1, keepdims=True)
    y = (xf - mu) * lax.rsqrt(var + NORM_EPS)
    return (y * g.astype(jnp.float32) + b.astype(jnp.float32)).astype(x.dtype)

def rope(x, pos, rot_dim):
    half = rot_dim // 2
    inv = jnp.power(jnp.float32(ROPE_THETA), -jnp.arange(half, dtype=jnp.float32) * (2.0 / rot_dim))
    ang = pos.astype(jnp.float32)[:, None] * inv
    cos = jnp.cos(ang)[:, None, :]
    sin = jnp.sin(ang)[:, None, :]
    xf = x.astype(jnp.float32)
    x1, x2 = xf[..., :half], xf[..., half:rot_dim]
    out = jnp.concatenate([x1 * cos - x2 * sin, x2 * cos + x1 * sin, xf[..., rot_dim:]], axis=-1)
    return out.astype(x.dtype)

def masked_softmax(s, mask):
    s = jnp.where(mask, s.astype(jnp.float32), -jnp.inf)
    m = jnp.max(s, axis=-1, keepdims=True)
    m = jnp.where(jnp.isfinite(m), m, 0.0)
    p = jnp.exp(s - m)
    return p / jnp.maximum(jnp.sum(p, axis=-1, keepdims=True), 1e-30)

def mla_mixer(c_q, c_kv, k_rope, g_cq, g_ckv, w_uq, w_ukv, g_q, g_k, w_o, pos):
    B, S, _ = c_q.shape
    dt = c_q.dtype
    q = (rms_norm(c_q, g_cq) @ w_uq).reshape(B, S, MLA_HEADS, MLA_QK_DIM)
    kv = (rms_norm(c_kv, g_ckv) @ w_ukv).reshape(B, S, MLA_HEADS, MLA_NOPE_DIM + MLA_V_DIM)
    k_nope, v = kv[..., :MLA_NOPE_DIM], kv[..., MLA_NOPE_DIM:]
    k_r = jnp.broadcast_to(k_rope[:, :, None, :], (B, S, MLA_HEADS, MLA_ROPE_DIM))
    k = jnp.concatenate([k_r, k_nope], axis=-1)
    q = rope(rms_norm(q, g_q), pos, MLA_ROPE_DIM)
    k = rope(rms_norm(k, g_k), pos, MLA_ROPE_DIM)
    scale = MLA_QK_DIM ** -0.5

    def block(i):
        qb = lax.dynamic_slice_in_dim(q, i * Q_BLOCK, Q_BLOCK, axis=1)
        t = i * Q_BLOCK + jnp.arange(Q_BLOCK)
        s = jnp.einsum('bqhd,bkhd->bhqk', qb, k) * scale
        p = masked_softmax(s, pos[None, :] <= t[:, None])
        return jnp.einsum('bhqk,bkhd->bqhd', p.astype(dt), v)

    o = lax.map(block, jnp.arange(S // Q_BLOCK))
    o = jnp.moveaxis(o, 0, 1).reshape(B, S, MLA_HEADS * MLA_V_DIM)
    return o @ w_o

def conv_mixer(u2, b_glu, w_dw, b_dw, g_ln, b_ln, w_out, b_out):
    a, gate = jnp.split(u2 + b_glu, 2, axis=-1)
    u = a * jax.nn.sigmoid(gate)
    u = lax.conv_general_dilated(u, w_dw[:, None, :], (1,), [(CONV_WIDTH - 1, 0)],
                                 dimension_numbers=('NWC', 'WIO', 'NWC'),
                                 feature_group_count=CONV_CH) + b_dw
    u = jax.nn.silu(layer_norm(u, g_ln, b_ln))
    return u @ w_out + b_out

def compress(tok, pe, w1, w2):
    B, S, G, dh = tok.shape
    n_cmp = (S - CMP_BLOCK) // CMP_STRIDE + 1
    idx = (jnp.arange(n_cmp) * CMP_STRIDE)[:, None] + jnp.arange(CMP_BLOCK)[None, :]
    blocks = tok[:, idx] + pe[None, None, :, None, :]
    blocks = jnp.moveaxis(blocks, 2, 3).reshape(B, n_cmp, G, CMP_BLOCK * dh)
    return jax.nn.silu(blocks @ w1) @ w2

def nsa_mixer(q_raw, kv_raw, gate_logits, pe_k, pe_v, w_ck1, w_ck2, w_cv1, w_cv2, g_q, g_k, w_o, pos):
    B, S, _ = q_raw.shape
    dt = q_raw.dtype
    H, G, dh = NSA_HEADS, NSA_KV_GROUPS, NSA_HEAD_DIM
    hpg = H // G
    QB = NSA_Q_BLOCK
    q = rope(rms_norm(q_raw.reshape(B, S, H, dh), g_q), pos, NSA_ROPE_DIM)
    kv = kv_raw.reshape(B, S, 2 * NSA_N_BRANCH, G, dh)
    kc, vc, ks, vs, kw, vw = [kv[:, :, j] for j in range(2 * NSA_N_BRANCH)]
    n_cmp = (S - CMP_BLOCK) // CMP_STRIDE + 1
    cmp_pos = jnp.arange(n_cmp) * CMP_STRIDE + CMP_BLOCK - 1
    k_cmp = rope(rms_norm(compress(kc, pe_k, w_ck1, w_ck2), g_k), cmp_pos, NSA_ROPE_DIM)
    v_cmp = compress(vc, pe_v, w_cv1, w_cv2)
    n_slc = S // SLC_BLOCK
    top_n = min(SLC_TOP_N, n_slc)
    k_slc = rope(rms_norm(ks, g_k), pos, NSA_ROPE_DIM)
    k_slc_blk = k_slc.reshape(B, n_slc, SLC_BLOCK, G, dh).transpose(0, 3, 1, 2, 4)
    v_slc_blk = vs.reshape(B, n_slc, SLC_BLOCK, G, dh).transpose(0, 3, 1, 2, 4)
    c_start = jnp.arange(n_cmp) * CMP_STRIDE
    s_start = jnp.arange(n_slc) * SLC_BLOCK
    overlap = ((c_start[:, None] < s_start[None, :] + SLC_BLOCK)
               & (c_start[:, None] + CMP_BLOCK > s_start[None, :])).astype(jnp.float32)
    k_win = rope(rms_norm(kw, g_k), pos, NSA_ROPE_DIM)
    k_win_pad = jnp.pad(k_win, ((0, 0), (WINDOW, 0), (0, 0), (0, 0)))
    v_win_pad = jnp.pad(vw, ((0, 0), (WINDOW, 0), (0, 0), (0, 0)))
    scale = dh ** -0.5
    bi = jnp.arange(B)[:, None, None, None]
    gi = jnp.arange(G)[None, :, None, None]
    j_blk = jnp.arange(n_slc)

    def block(i):
        q0 = i * QB
        t = q0 + jnp.arange(QB)
        qb = lax.dynamic_slice_in_dim(q, q0, QB, axis=1).reshape(B, QB, G, hpg, dh)
        s_c = jnp.einsum('bqghd,bcgd->bghqc', qb, k_cmp) * scale
        p_c = masked_softmax(s_c, cmp_pos[None, :] <= t[:, None])
        o_c = jnp.einsum('bghqc,bcgd->bqghd', p_c.astype(dt), v_cmp)
        imp = jnp.einsum('bghqc,cn->bgqn', p_c, overlap)
        blk_t = t // SLC_BLOCK
        forced = ((j_blk[None, :] == 0) | (j_blk[None, :] == blk_t[:, None])
                  | (j_blk[None, :] == blk_t[:, None] - 1))
        imp = jnp.where(forced, FORCED_BLOCK_SCORE, imp)
        imp = jnp.where(j_blk[None, :] > blk_t[:, None], -jnp.inf, imp)
        _, idx = lax.top_k(imp, top_n)
        k_sel = k_slc_blk[bi, gi, idx]
        v_sel = v_slc_blk[bi, gi, idx]
        s_s = jnp.einsum('bqghd,bgqnkd->bghqnk', qb, k_sel) * scale
        kpos = idx[..., None] * SLC_BLOCK + jnp.arange(SLC_BLOCK)
        m_s = (kpos <= t[None, None, :, None, None])[:, :, None]
        p_s = masked_softmax(s_s.reshape(B, G, hpg, QB, top_n * SLC_BLOCK),
                             m_s.reshape(B, G, 1, QB, top_n * SLC_BLOCK))
        o_s = jnp.einsum('bghqnk,bgqnkd->bqghd', p_s.reshape(s_s.shape).astype(dt), v_sel)
        k_w = lax.dynamic_slice_in_dim(k_win_pad, q0, WINDOW + QB, axis=1)
        v_w = lax.dynamic_slice_in_dim(v_win_pad, q0, WINDOW + QB, axis=1)
        wpos = q0 - WINDOW + jnp.arange(WINDOW + QB)
        m_w = ((wpos[None, :] <= t[:, None]) & (wpos[None, :] > t[:, None] - WINDOW)
               & (wpos[None, :] >= 0))
        s_w = jnp.einsum('bqghd,bkgd->bghqk', qb, k_w) * scale
        p_w = masked_softmax(s_w, m_w)
        o_w = jnp.einsum('bghqk,bkgd->bqghd', p_w.astype(dt), v_w)
        return jnp.stack([o_c, o_s, o_w], axis=-2)

    o = lax.map(block, jnp.arange(S // QB))
    o = jnp.moveaxis(o, 0, 1).reshape(B, S, H, NSA_N_BRANCH, dh)
    g = jax.nn.sigmoid(gate_logits.reshape(B, S, H, NSA_N_BRANCH).astype(jnp.float32)).astype(dt)
    o = jnp.einsum('bshnd,bshn->bshd', o, g).reshape(B, S, H * dh)
    return o @ w_o

def hybrid_layer(x, pos, g_mix, w_in, g_cq, g_ckv, w_uq, w_ukv, g_q_mla, g_k_mla, w_o_mla,
                 b_glu, w_dw, b_dw, g_conv_ln, b_conv_ln, w_conv_out, b_conv_out,
                 pe_cmp_k, pe_cmp_v, w_cmp_k1, w_cmp_k2, w_cmp_v1, w_cmp_v2,
                 g_q_nsa, g_k_nsa, w_o_nsa, w_out, g_ffn, w_ff1, w_ff2):
    dt = x.dtype
    h = rms_norm(x, g_mix)
    z = h @ w_in
    c_q, c_kv, k_rope, u2, q_nsa, kv_nsa, gate_nsa, gate_mix = jnp.split(z, SPLIT_IDX, axis=-1)
    o_a = mla_mixer(c_q, c_kv, k_rope, g_cq, g_ckv, w_uq, w_ukv, g_q_mla, g_k_mla, w_o_mla, pos)
    o_b = conv_mixer(u2, b_glu, w_dw, b_dw, g_conv_ln, b_conv_ln, w_conv_out, b_conv_out)
    o_c = nsa_mixer(q_nsa, kv_nsa, gate_nsa, pe_cmp_k, pe_cmp_v, w_cmp_k1, w_cmp_k2,
                    w_cmp_v1, w_cmp_v2, g_q_nsa, g_k_nsa, w_o_nsa, pos)
    g_a, g_b, g_c = jnp.split(jax.nn.sigmoid(gate_mix.astype(jnp.float32)).astype(dt), N_MIXERS, axis=-1)
    x = x + (g_a * o_a + g_b * o_b + g_c * o_c) @ w_out
    h = rms_norm(x, g_ffn)
    x = x + jnp.square(jax.nn.relu(h @ w_ff1)) @ w_ff2
    return x

def first_inputs(seed: int = 0) -> dict:
    key = jax.random.key(seed)
    ks = iter(jax.random.split(key, 40))
    L = DEPTH
    res = (2.0 * DEPTH) ** -0.5

    def nrm(shape, scale):
        return jax.random.normal(next(ks), shape, jnp.float32) * scale

    def gain(shape):
        return 1.0 + nrm(shape, 0.02)

    return {
        "x": nrm((BATCH, SEQ, D_MODEL), 1.0),
        "g_mix": gain((L, D_MODEL)),
        "w_in": nrm((L, D_MODEL, D_IN), D_MODEL ** -0.5),
        "g_cq": gain((L, MLA_Q_RANK)),
        "g_ckv": gain((L, MLA_KV_RANK)),
        "w_uq": nrm((L, MLA_Q_RANK, MLA_HEADS * MLA_QK_DIM), MLA_Q_RANK ** -0.5),
        "w_ukv": nrm((L, MLA_KV_RANK, MLA_HEADS * (MLA_NOPE_DIM + MLA_V_DIM)), MLA_KV_RANK ** -0.5),
        "g_q_mla": gain((L, MLA_QK_DIM)),
        "g_k_mla": gain((L, MLA_QK_DIM)),
        "w_o_mla": nrm((L, MLA_HEADS * MLA_V_DIM, D_MODEL), (MLA_HEADS * MLA_V_DIM) ** -0.5),
        "b_glu": nrm((L, 2 * CONV_CH), 0.01),
        "w_dw": nrm((L, CONV_WIDTH, CONV_CH), CONV_WIDTH ** -0.5),
        "b_dw": nrm((L, CONV_CH), 0.01),
        "g_conv_ln": gain((L, CONV_CH)),
        "b_conv_ln": nrm((L, CONV_CH), 0.01),
        "w_conv_out": nrm((L, CONV_CH, D_MODEL), CONV_CH ** -0.5),
        "b_conv_out": nrm((L, D_MODEL), 0.01),
        "pe_cmp_k": nrm((L, CMP_BLOCK, NSA_HEAD_DIM), 0.1),
        "pe_cmp_v": nrm((L, CMP_BLOCK, NSA_HEAD_DIM), 0.1),
        "w_cmp_k1": nrm((L, CMP_BLOCK * NSA_HEAD_DIM, CMP_HIDDEN), (CMP_BLOCK * NSA_HEAD_DIM) ** -0.5),
        "w_cmp_k2": nrm((L, CMP_HIDDEN, NSA_HEAD_DIM), CMP_HIDDEN ** -0.5),
        "w_cmp_v1": nrm((L, CMP_BLOCK * NSA_HEAD_DIM, CMP_HIDDEN), (CMP_BLOCK * NSA_HEAD_DIM) ** -0.5),
        "w_cmp_v2": nrm((L, CMP_HIDDEN, NSA_HEAD_DIM), CMP_HIDDEN ** -0.5),
        "g_q_nsa": gain((L, NSA_HEAD_DIM)),
        "g_k_nsa": gain((L, NSA_HEAD_DIM)),
        "w_o_nsa": nrm((L, NSA_HEADS * NSA_HEAD_DIM, D_MODEL), (NSA_HEADS * NSA_HEAD_DIM) ** -0.5),
        "w_out": nrm((L, D_MODEL, D_MODEL), D_MODEL ** -0.5 * res),
        "g_ffn": gain((L, D_MODEL)),
        "w_ff1": nrm((L, D_MODEL, D_FF), D_MODEL ** -0.5),
        "w_ff2": nrm((L, D_FF, D_MODEL), D_FF ** -0.5 * res),
    }

def first_block(x, g_mix, w_in, g_cq, g_ckv, w_uq, w_ukv, g_q_mla, g_k_mla, w_o_mla,
              b_glu, w_dw, b_dw, g_conv_ln, b_conv_ln, w_conv_out, b_conv_out,
              pe_cmp_k, pe_cmp_v, w_cmp_k1, w_cmp_k2, w_cmp_v1, w_cmp_v2,
              g_q_nsa, g_k_nsa, w_o_nsa, w_out, g_ffn, w_ff1, w_ff2):
    pos = jnp.arange(x.shape[1])
    for l in range(DEPTH):
        x = hybrid_layer(x, pos, g_mix[l], w_in[l], g_cq[l], g_ckv[l], w_uq[l], w_ukv[l],
                         g_q_mla[l], g_k_mla[l], w_o_mla[l], b_glu[l], w_dw[l], b_dw[l],
                         g_conv_ln[l], b_conv_ln[l], w_conv_out[l], b_conv_out[l],
                         pe_cmp_k[l], pe_cmp_v[l], w_cmp_k1[l], w_cmp_k2[l], w_cmp_v1[l], w_cmp_v2[l],
                         g_q_nsa[l], g_k_nsa[l], w_o_nsa[l], w_out[l], g_ffn[l], w_ff1[l], w_ff2[l])
    return x


CHUNK = 64
HEAD_DIM = 64
H_SPARSE = 8
H_FOX = 8
H_IDX = 8
D_IDX = 64
TOPK_MAX = 256
ROT_DIM = HEAD_DIM // 4
ROT_DIM_IDX = D_IDX // 4
D_FF_2 = 2816
CONV_W = 3
N_BRANCH = 2
EPS = 1e-6
NEG_INF = -1e30

W_SPARSE = H_SPARSE * HEAD_DIM
W_FOX = H_FOX * HEAD_DIM
IN_SPLITS_2 = (W_SPARSE, HEAD_DIM, HEAD_DIM, H_IDX * D_IDX, D_IDX, H_IDX,
             W_FOX, W_FOX, W_FOX, H_FOX, N_BRANCH * D_MODEL)
N_IN = W_SPARSE + 2 * HEAD_DIM + H_IDX * D_IDX + D_IDX + H_IDX + 3 * W_FOX + H_FOX + N_BRANCH * D_MODEL


def _rmsnorm(x, g):
    xf = x.astype(jnp.float32)
    y = xf * lax.rsqrt(jnp.mean(xf * xf, axis=-1, keepdims=True) + EPS)
    return (y * g.astype(jnp.float32)).astype(x.dtype)

def _partial_rope(x, positions, rot_dim):
    half = rot_dim // 2
    inv_freq = ROPE_THETA ** (-jnp.arange(0, rot_dim, 2, dtype=jnp.float32) / rot_dim)
    ang = positions.astype(jnp.float32)[..., None] * inv_freq
    cos = jnp.cos(ang)[:, :, None, :]
    sin = jnp.sin(ang)[:, :, None, :]
    xf = x.astype(jnp.float32)
    x1, x2, rest = xf[..., :half], xf[..., half:rot_dim], xf[..., rot_dim:]
    out = jnp.concatenate([x1 * cos - x2 * sin, x2 * cos + x1 * sin, rest], axis=-1)
    return out.astype(x.dtype)

def _to_blocks(a, nb):
    b = a.shape[0]
    return jnp.moveaxis(a.reshape((b, nb, Q_BLOCK) + a.shape[2:]), 1, 0)

def _from_blocks(a):
    a = jnp.moveaxis(a, 0, 1)
    return a.reshape((a.shape[0], a.shape[1] * a.shape[2]) + a.shape[3:])

def _sparse_attention(q, k, v, q_idx, k_idx, w_idx):
    S = q.shape[1]
    nb = S // Q_BLOCK
    topk = min(TOPK_MAX, S // 4)
    key_chunk = jnp.arange(S) // CHUNK
    idx_scale = D_IDX ** -0.5
    att_scale = HEAD_DIM ** -0.5

    def block(args):
        qb, qib, wb, q_start = args
        q_chunk = (q_start + jnp.arange(Q_BLOCK)) // CHUNK
        admissible = key_chunk[None, :] <= q_chunk[:, None]
        s = jnp.einsum("bqhd,bsd->bqhs", qib, k_idx).astype(jnp.float32) * idx_scale
        score = jnp.einsum("bqh,bqhs->bqs", wb.astype(jnp.float32), jax.nn.relu(s))
        score = jnp.where(admissible[None], score, NEG_INF)
        top_val, top_idx = lax.top_k(score, topk)
        valid = top_val > 0.5 * NEG_INF
        k_sel = jax.vmap(lambda kk, ii: kk[ii])(k, top_idx)
        v_sel = jax.vmap(lambda vv, ii: vv[ii])(v, top_idx)
        logits = jnp.einsum("bqhd,bqkd->bqhk", qb, k_sel).astype(jnp.float32) * att_scale
        logits = jnp.where(valid[:, :, None, :], logits, NEG_INF)
        p = jax.nn.softmax(logits, axis=-1).astype(v.dtype)
        return jnp.einsum("bqhk,bqkd->bqhd", p, v_sel)

    starts = jnp.arange(nb) * Q_BLOCK
    out = lax.map(block, (_to_blocks(q, nb), _to_blocks(q_idx, nb), _to_blocks(w_idx, nb), starts))
    return _from_blocks(out)

def _forgetting_attention(q, k, v, log_f):
    S = q.shape[1]
    nb = S // Q_BLOCK
    cum = jnp.cumsum(log_f, axis=1)
    cum_k = jnp.moveaxis(cum, 1, 2)
    key_pos = jnp.arange(S)
    scale = HEAD_DIM ** -0.5

    def block(args):
        qb, cq, q_start = args
        causal = key_pos[None, :] <= (q_start + jnp.arange(Q_BLOCK))[:, None]
        logits = jnp.einsum("bqhd,bshd->bhqs", qb, k).astype(jnp.float32) * scale
        logits = logits + jnp.moveaxis(cq, 1, 2)[..., None] - cum_k[:, :, None, :]
        logits = jnp.where(causal[None, None], logits, NEG_INF)
        p = jax.nn.softmax(logits, axis=-1).astype(v.dtype)
        return jnp.einsum("bhqs,bshd->bqhd", p, v)

    starts = jnp.arange(nb) * Q_BLOCK
    out = lax.map(block, (_to_blocks(q, nb), _to_blocks(cum, nb), starts))
    return _from_blocks(out)

def _mixer(h, positions, w_in, forget_bias, w_branch_a, w_branch_b, w_out):
    B, S, _ = h.shape
    proj = h @ w_in
    offs = np.cumsum(IN_SPLITS_2)[:-1].tolist()
    q_a, k_a, v_a, q_i, k_i, w_i, q_f, k_f, v_f, f_f, gates = jnp.split(proj, offs, axis=-1)
    q_a = _partial_rope(q_a.reshape(B, S, H_SPARSE, HEAD_DIM), positions, ROT_DIM)
    k_a = _partial_rope(k_a[:, :, None, :], positions, ROT_DIM)[:, :, 0]
    q_i = _partial_rope(q_i.reshape(B, S, H_IDX, D_IDX), positions, ROT_DIM_IDX)
    k_i = _partial_rope(k_i[:, :, None, :], positions, ROT_DIM_IDX)[:, :, 0]
    w_i = w_i * (H_IDX ** -0.5)
    o_a = _sparse_attention(q_a, k_a, v_a, q_i, k_i, w_i)
    y_a = o_a.reshape(B, S, W_SPARSE) @ w_branch_a
    log_f = jax.nn.log_sigmoid(f_f.astype(jnp.float32) + forget_bias.astype(jnp.float32))
    o_b = _forgetting_attention(q_f.reshape(B, S, H_FOX, HEAD_DIM),
                                k_f.reshape(B, S, H_FOX, HEAD_DIM),
                                v_f.reshape(B, S, H_FOX, HEAD_DIM), log_f)
    y_b = o_b.reshape(B, S, W_FOX) @ w_branch_b
    g_a, g_b = jnp.split(jax.nn.sigmoid(gates.astype(jnp.float32)).astype(h.dtype), N_BRANCH, axis=-1)
    return (g_a * y_a + g_b * y_b) @ w_out

def _conv_ffn(h, w_up, conv_w, conv_b, w_down):
    S = h.shape[1]
    u = h @ w_up
    up = jnp.pad(u, ((0, 0), (CONV_W - 1, 0), (0, 0)))
    u = conv_b + sum(conv_w[i] * up[:, i:i + S] for i in range(CONV_W))
    a, b = jnp.split(u, 2, axis=-1)
    return (jax.nn.silu(a) * b) @ w_down

def second_inputs(seed: int = 0) -> dict:
    key = jax.random.key(seed)
    ks = jax.random.split(key, 17)
    f32 = jnp.float32

    def nrm(k, shape, fan_in, mult=1.0):
        return jax.random.normal(k, shape, f32) * (mult * fan_in ** -0.5)

    x = jax.random.normal(ks[0], (BATCH, SEQ, D_MODEL), f32)
    c = jax.random.normal(ks[1], (BATCH, D_MODEL), f32)
    offset = jax.random.randint(ks[2], (BATCH, 1), 0, 4096, dtype=jnp.int32)
    positions = offset + jnp.arange(SEQ, dtype=jnp.int32)[None, :]
    mod_w = nrm(ks[3], (DEPTH, D_MODEL, 6 * D_MODEL), D_MODEL, 0.5)
    mod_b = 0.01 * jax.random.normal(ks[4], (DEPTH, 6 * D_MODEL), f32)
    norm1_g = 1.0 + 0.02 * jax.random.normal(ks[5], (DEPTH, D_MODEL), f32)
    norm2_g = 1.0 + 0.02 * jax.random.normal(ks[6], (DEPTH, D_MODEL), f32)
    w_in = nrm(ks[7], (DEPTH, D_MODEL, N_IN), D_MODEL)
    forget_bias = 4.0 + 0.5 * jax.random.normal(ks[8], (DEPTH, H_FOX), f32)
    w_branch_a = nrm(ks[9], (DEPTH, W_SPARSE, D_MODEL), W_SPARSE)
    w_branch_b = nrm(ks[10], (DEPTH, W_FOX, D_MODEL), W_FOX)
    w_out = nrm(ks[11], (DEPTH, D_MODEL, D_MODEL), D_MODEL)
    w_up = nrm(ks[12], (DEPTH, D_MODEL, 2 * D_FF_2), D_MODEL)
    conv_w = nrm(ks[13], (DEPTH, CONV_W, 2 * D_FF_2), CONV_W)
    conv_b = 0.01 * jax.random.normal(ks[14], (DEPTH, 2 * D_FF_2), f32)
    w_down = nrm(ks[15], (DEPTH, D_FF_2, D_MODEL), D_FF_2)
    final_g = 1.0 + 0.02 * jax.random.normal(ks[16], (D_MODEL,), f32)
    return {"x": x, "c": c, "positions": positions, "mod_w": mod_w, "mod_b": mod_b,
            "norm1_g": norm1_g, "norm2_g": norm2_g, "w_in": w_in, "forget_bias": forget_bias,
            "w_branch_a": w_branch_a, "w_branch_b": w_branch_b, "w_out": w_out,
            "w_up": w_up, "conv_w": conv_w, "conv_b": conv_b, "w_down": w_down,
            "final_g": final_g}

def second_block(x, c, positions, mod_w, mod_b, norm1_g, norm2_g, w_in, forget_bias,
              w_branch_a, w_branch_b, w_out, w_up, conv_w, conv_b, w_down, final_g):
    for l in range(DEPTH):
        mod = c @ mod_w[l] + mod_b[l]
        sh1, sc1, g1, sh2, sc2, g2 = [m[:, None, :] for m in jnp.split(mod, 6, axis=-1)]
        h = _rmsnorm(x, norm1_g[l]) * (1.0 + sc1) + sh1
        x = x + g1 * _mixer(h, positions, w_in[l], forget_bias[l], w_branch_a[l], w_branch_b[l], w_out[l])
        h = _rmsnorm(x, norm2_g[l]) * (1.0 + sc2) + sh2
        x = x + g2 * _conv_ffn(h, w_up[l], conv_w[l], conv_b[l], w_down[l])
    return _rmsnorm(x, final_g)


def setup_inputs(seed=0):
    out = dict(first_inputs(seed))
    for name, value in second_inputs(seed + 1).items():
        if name != "x":
            out[name + "_2"] = value
    return out


def reference(
    x, g_mix, w_in, g_cq, g_ckv, w_uq, w_ukv, g_q_mla, g_k_mla, w_o_mla, b_glu, w_dw, b_dw,
    g_conv_ln, b_conv_ln, w_conv_out, b_conv_out, pe_cmp_k, pe_cmp_v, w_cmp_k1, w_cmp_k2,
    w_cmp_v1, w_cmp_v2, g_q_nsa, g_k_nsa, w_o_nsa, w_out, g_ffn, w_ff1, w_ff2, c_2, positions_2,
    mod_w_2, mod_b_2, norm1_g_2, norm2_g_2, w_in_2, forget_bias_2, w_branch_a_2, w_branch_b_2,
    w_out_2, w_up_2, conv_w_2, conv_b_2, w_down_2, final_g_2,
):
    x = first_block(
        x, g_mix, w_in, g_cq, g_ckv, w_uq, w_ukv, g_q_mla, g_k_mla, w_o_mla, b_glu, w_dw, b_dw,
        g_conv_ln, b_conv_ln, w_conv_out, b_conv_out, pe_cmp_k, pe_cmp_v, w_cmp_k1, w_cmp_k2,
        w_cmp_v1, w_cmp_v2, g_q_nsa, g_k_nsa, w_o_nsa, w_out, g_ffn, w_ff1, w_ff2,
    )
    return second_block(
        x, c_2, positions_2, mod_w_2, mod_b_2, norm1_g_2, norm2_g_2, w_in_2, forget_bias_2,
        w_branch_a_2, w_branch_b_2, w_out_2, w_up_2, conv_w_2, conv_b_2, w_down_2, final_g_2,
    )


_drawn_inputs = setup_inputs


def setup_inputs(seed=0):
    import zlib

    import numpy as np

    out = dict(_drawn_inputs(seed))
    spreads = {}
    factors = {'g_mix': 6.67,
     'g_cq': 8.0,
     'g_ckv': 8.0,
     'g_q_mla': 8.0,
     'g_k_mla': 8.0,
     'b_glu': 8.0,
     'b_dw': 8.0,
     'g_conv_ln': 7.523,
     'b_conv_ln': 8.0,
     'b_conv_out': 8.0,
     'pe_cmp_k': 8.0,
     'pe_cmp_v': 4.383,
     'g_q_nsa': 8.0,
     'g_k_nsa': 8.0,
     'g_ffn': 3.004,
     'mod_b_2': 3.553,
     'norm1_g_2': 5.742,
     'norm2_g_2': 4.446,
     'conv_b_2': 8.0,
     'final_g_2': 2.706}
    for name, (base, spread) in spreads.items():
        noise = np.random.default_rng([zlib.crc32(name.encode()), seed]).standard_normal(out[name].shape)
        drawn = base * np.exp(spread * noise) if base else spread * noise
        out[name] = jnp.asarray(drawn.astype(out[name].dtype))
    for name, factor in factors.items():
        out[name] = (out[name] * factor).astype(out[name].dtype)
    return out
```

```python
from contextlib import ExitStack, contextmanager

import numpy as np
import concourse.bass as bass
from concourse import mybir

F32 = mybir.dt.float32
BF16 = mybir.dt.bfloat16
I32 = mybir.dt.int32
ALU = mybir.AluOpType
ACT = mybir.ActivationFunctionType
AX = mybir.AxisListType.X

P = 128
T = 512
TT = T // P
D = 1024
KD = D // P
DEPTH = 2
EPS = 1e-6
NEG = -1e30

NH, DH = 8, 64
MQK, MNOPE, MROPE = 96, 64, 32
QRANK, KVRANK = 384, 256
CONV_CH, TAPS = 512, 31
CCH = CONV_CH // P
NCMP, CSTRIDE, CBLOCK = 31, 16, 32
FF1 = 4096
TOPK = 128
FF2 = 2816
NF2 = FF2 // P

RING = 4
CHUNK = 8 * P
C1 = {}
n = 0
for name, count in (("raw", 20), ("misc", 4), ("mla", 6), ("cmp", 6), ("gate", 24), ("merge", 12),
                    ("wout", 8), ("ff_up", 32), ("ff_down", 32)):
    C1[name] = n
    n += count
NC1 = n
C2 = {}
n = 0
for name, count in (("mod", 48), ("raw", 8), ("misc", 4), ("fox", 12), ("gate", 16), ("merge", 8),
                    ("wout", 8), ("ff_up", 44), ("ff_down", 24)):
    C2[name] = n
    n += count
NC2 = n
BASE2 = DEPTH * NC1
NCHUNKS = DEPTH * (NC1 + NC2)
assert NC1 % RING == 0 and NC2 % RING == 0

def columns(spec):
    at, off = {}, 0
    for name, w in spec:
        at[name] = off
        off += w
    return at, off


PAR1, NPAR1 = columns((("g_mix", 8), ("g_ffn", 8), ("g_cq", 3), ("g_ckv", 2), ("gq_mla", 1), ("gk_mla", 1),
                       ("gq_nsa", 1), ("gk_nsa", 1), ("b_glu", 8), ("w_dw", CCH * TAPS), ("b_dw", 4),
                       ("g_ln", 4), ("b_ln", 4), ("b_out", 8), ("pe_k", 16), ("pe_v", 16)))
PAR2, NPAR2 = columns((("mod_b", 48), ("g1", 8), ("g2", 8), ("fbias", 32), ("conv_w", 3 * 44), ("conv_b", 44)))
NPAR = max(NPAR1, NPAR2)

CON, NCON = columns((("ident", 128), ("ones", 128), ("bd64", 128), ("chunkmask", 128),
                     ("cos_m", 512), ("sin_m", 512), ("cos_n", 512), ("sin_n", 512),
                     ("cos_c", 62), ("sin_c", 62), ("mask_c", 124), ("rowok", 4), ("invf", 1), ("sgn", 1), ("rotm", 1),
                     ("unrot", 1), ("eps", 1), ("eps_mla", 1), ("eps_nsa", 1), ("final_g", 8), ("cvec", 8)))

AR = {}
n = 0
for name, w in (("ring", RING * CHUNK), ("x", KD * T), ("h", KD * T), ("raw", 21 * T), ("g", 24 * T),
                ("p", 8 * T), ("pt", 1280), ("qs", 4 * T), ("vs", 8 * 256), ("o", 8 * T),
                ("par", NPAR), ("con", NCON), ("idb", 64), ("caub", 64), ("extra", 640), ("small", 256)):
    AR[name] = n
    n += w
NARENA = n

SWAP32 = [(i + 16) % 32 for i in range(32)]
SWAP16 = [(i + 8) % 16 if i < 16 else i for i in range(32)]


class Program:
    pass


@contextmanager
def stage(m, names):
    nc = m.nc
    with ExitStack() as ctx:
        sems = [ctx.enter_context(nc.semaphore(s)) for s in names.split()]
        yield sems
        with nc.Block() as block:
            @block.gpsimd
            def _(pool):
                for s in sems:
                    pool.sem_clear(s)


@contextmanager
def loop(eng, count):
    if count == 1:
        yield 0
    else:
        with eng.Fori(0, count) as i:
            yield i


def chunk_flat(m, c):
    return m.layer * m.per_layer + (m.stream_base + c)


def hold(eng, m):
    eng.sem_inc(m.passed, 1)


def use_log_exp(m):
    m.nc.scalar.preload_act_table_set("natural_log_exp_and_others")


def wait_chunk(pe, m, c, i=0, body=0):
    rounds = (m.stream_base + c) // RING + 1
    pe.wait_ge(m.landed[c % RING], m.layer * (16 * m.per_layer // RING) + i * (16 * body // RING) + 16 * rounds)


def slab(m, c):
    return m.ring[:, c % RING, :]


def load_ahead(sp, m, c, done, j):
    sp.wait_ge(done, j)
    sp.dma_start(slab(m, c), m.wstream[chunk_flat(m, c) + RING]).then_inc(m.landed[c % RING], 16)


def load_ahead_loop(sp, m, base, done, iters, body):
    with loop(sp, iters) as i:
        for j in range(body):
            sp.wait_ge(done, i * body + j + 1)
            sp.dma_start(slab(m, base + j), m.wstream[m.layer * m.per_layer + i * body + (m.stream_base + base + j + RING)])\
                .then_inc(m.landed[(base + j) % RING], 16)


def linear_stage(m, base, iters, units, rhs, evac, post=None, extra="", act_first=None, dve_side=None, pool_side=None):
    body = sum(len(u) for u in units)
    ng = len(units)
    assert body % RING == 0 or iters == 1
    with stage(m, "chunk_done act_evac dve_evac " + extra) as (chunk_done, act_evac, dve_evac, *side):
        counters = {"act": act_evac, "dve": dve_evac}
        mine = {e: [g for g in range(ng) if evac[g][0] == e] for e in ("act", "dve")}
        upto = []
        for u in units:
            upto.append((upto[-1] if upto else 0) + len(u))
        nbanks = min(ng, 8)
        assert ng <= 8
        with m.nc.Block() as block:
            @block.sync
            def _(sp):
                load_ahead_loop(sp, m, base, chunk_done, iters, body)

            @block.tensor
            def _(pe):
                with loop(pe, iters) as i:
                    c = 0
                    for g in range(ng):
                        who = evac[g][0]
                        pe.wait_ge(counters[who], i * len(mine[who]) + mine[who].index(g) + 1)
                        total, done = sum(len(u) for u in units[g]), 0
                        for u in units[g]:
                            wait_chunk(pe, m, base + c, i, body)
                            for k, r in enumerate(u):
                                mm = m.nc.tensor.matmul(m.ps[:, g, :], slab(m, base + c)[:, k * P:(k + 1) * P], rhs(r),
                                                        start=(done == 0), stop=(done == total - 1))
                                done += 1
                            mm.then_inc(chunk_done, 1)
                            c += 1

            def drain(eng, name):
                counter = counters[name]
                if mine[name]:
                    eng.sem_inc(counter, len(mine[name]))
                    with loop(eng, iters) as i:
                        for g in mine[name]:
                            eng.wait_ge(chunk_done, i * body + upto[g])
                            evac[g][1](eng, m.ps[:, g, :], i * ng + g).then_inc(counter, 1)

            @block.scalar
            def _(act):
                if act_first:
                    act_first(act, *side)
                drain(act, "act")

            @block.vector
            def _(dve):
                if dve_side:
                    dve_side(dve, *side)
                drain(dve, "dve")
                if post:
                    with loop(dve, iters) as i:
                        for g in range(ng):
                            dve.wait_ge(act_evac, i * ng + g + 1 + ng)
                            post(dve, i * ng + g)

            @block.gpsimd
            def _(pool):
                if pool_side:
                    pool_side(pool, *side)


def refined_rsqrt(m, dve, step, done, v, root, out, tmp):
    nc = m.nc
    nc.vector.reciprocal(out, root).then_inc(step, 1)
    dve.wait_ge(step, done + 1)
    nc.vector.tensor_tensor(tmp, v, out, ALU.mult).then_inc(step, 1)
    dve.wait_ge(step, done + 2)
    nc.vector.tensor_tensor(tmp, tmp, out, ALU.mult).then_inc(step, 1)
    dve.wait_ge(step, done + 3)
    nc.vector.tensor_scalar(tmp, tmp, -0.5, 1.5, ALU.mult, ALU.add).then_inc(step, 1)
    dve.wait_ge(step, done + 4)
    return nc.vector.tensor_tensor(out, out, tmp, ALU.mult)


def norm_stage(m, src, n_src, dst, gain, width, shift=None):
    nc = m.nc
    sq = m.p[:, 0:8 * T].rearrange("p (k t) -> p k t", t=T)
    var, rstd = m.pt[:, 0:T], m.pt[:, T:2 * T]
    with stage(m, "squared summed rooted step rstd_done scaled") as (squared, summed, rooted, step, rstd_done, scaled):
        with nc.Block() as block:
            @block.scalar
            def _(act):
                for k in range(n_src):
                    nc.scalar.activation(sq[:, k, :], src(k), ACT.Square).then_inc(squared, 1)
                act.wait_ge(summed, 1)
                nc.scalar.activation(var, m.ps[:, 0, :], ACT.Identity, bias=m.eps, scale=1.0 / width).then_inc(rooted, 1)
                nc.scalar.activation(rstd, m.ps[:, 0, :], ACT.Sqrt, bias=m.eps, scale=1.0 / width).then_inc(rooted, 1)

            @block.tensor
            def _(pe):
                for k in range(n_src):
                    pe.wait_ge(squared, k + 1)
                    mm = nc.tensor.matmul(m.ps[:, 0, :], m.ones, sq[:, k, :], start=(k == 0), stop=(k == n_src - 1))
                mm.then_inc(summed, 1)

            @block.vector
            def _(dve):
                dve.wait_ge(rooted, 2)
                refined_rsqrt(m, dve, step, 0, var, rstd, rstd, sq[:, 0, :]).then_inc(rstd_done, 1)
                dve.wait_ge(rstd_done, 1)
                for k in range(n_src):
                    nc.vector.scalar_tensor_tensor(dst(k), src(k), gain(k), rstd, ALU.mult, ALU.mult).then_inc(scaled, 1)
                    if shift is not None:
                        dve.wait_ge(scaled, 2 * k + 1)
                        nc.vector.tensor_scalar(dst(k), dst(k), shift(k), None, ALU.add).then_inc(scaled, 1)


def rotate_stage(m, jobs):
    nc = m.nc
    buf = m.scratch[:, 0:10 * T].rearrange("p (b s t) -> p b s t", b=5, t=T)
    with stage(m, "squared summed rooted step rstd_done normed swapped swap_sin turned") as (
            squared, summed, rooted, step_, rstd_done, normed, swapped, swap_sin, turned):
        with nc.Block() as block:
            @block.scalar
            def _(act):
                t0 = 0
                for tile, count, rows, cols, ones, gain, width, eps, cos, sin, mask in jobs:
                    step = min(2, count)
                    if gain is None:
                        continue
                    with loop(act, count // step) as i:
                        for s in range(step):
                            nc.scalar.activation(buf[0:rows, 0, s, 0:cols], tile(i * 2 + s), ACT.Square).then_inc(squared, 1)
                        for s in range(step):
                            act.wait_ge(summed, t0 + i * 2 + s + 1)
                            act.wait_ge(normed, t0 + i * 2 + s + 1)
                            nc.scalar.activation(buf[0:rows, 1, s, 0:cols], m.ps[0:rows, s, 0:cols], ACT.Sqrt, bias=eps[0:rows],
                                                 scale=1.0 / width).then_inc(rooted, 1)
                            nc.scalar.activation(buf[0:rows, 4, s, 0:cols], m.ps[0:rows, s, 0:cols], ACT.Identity,
                                                 bias=eps[0:rows], scale=1.0 / width).then_inc(rooted, 1)
                    t0 += count

            @block.tensor
            def _(pe):
                pe.sem_inc(rooted, 4)
                t0 = 0
                for tile, count, rows, cols, ones, gain, width, eps, cos, sin, mask in jobs:
                    step = min(2, count)
                    if gain is None:
                        continue
                    with loop(pe, count // step) as i:
                        for s in range(step):
                            pe.wait_ge(squared, t0 + i * 2 + s + 1)
                            pe.wait_ge(rooted, 2 * t0 + i * 4 + 2 * s + 2)
                            nc.tensor.matmul(m.ps[0:rows, s, 0:cols], ones, buf[0:rows, 0, s, 0:cols], start=True, stop=True)\
                                .then_inc(summed, 1)
                    t0 += count

            @block.vector
            def _(dve):
                dve.sem_inc(normed, 2)
                t0 = 0
                for tile, count, rows, cols, ones, gain, width, eps, cos, sin, mask in jobs:
                    step = min(2, count)
                    with loop(dve, count // step) as i:
                        for s in range(step):
                            n_, sw = buf[0:rows, 2, s, 0:cols], buf[0:rows, 3, s, 0:cols]
                            if gain is None:
                                nc.vector.tensor_copy(n_, tile(i * 2 + s)).then_inc(normed, 1)
                            else:
                                dve.wait_ge(rooted, 2 * t0 + i * 4 + 2 * s + 6)
                                rstd, var, tmp = buf[0:rows, 1, s, 0:cols], buf[0:rows, 4, s, 0:cols], buf[0:rows, 3, s, 0:cols]
                                refined_rsqrt(m, dve, step_, i * 8 + (4 * t0 + 4 * s), var, rstd, rstd, tmp).then_inc(rstd_done, 1)
                                dve.wait_ge(rstd_done, t0 + i * 2 + s + 1)
                                nc.vector.scalar_tensor_tensor(n_, tile(i * 2 + s), gain, buf[0:rows, 1, s, 0:cols],
                                                               ALU.mult, ALU.mult).then_inc(normed, 1)
                        for s in range(step):
                            n_, sw = buf[0:rows, 2, s, 0:cols], buf[0:rows, 3, s, 0:cols]
                            dve.wait_ge(normed, t0 + i * 2 + s + 3)
                            nc.vector.tensor_tensor(tile(i * 2 + s), n_, cos, ALU.mult).then_inc(turned, 1)
                        for s in range(step):
                            n_, sw = buf[0:rows, 2, s, 0:cols], buf[0:rows, 3, s, 0:cols]
                            nc.vector.stream_shuffle(sw, n_, mask).then_inc(swapped, 1)
                        for s in range(step):
                            n_, sw = buf[0:rows, 2, s, 0:cols], buf[0:rows, 3, s, 0:cols]
                            dve.wait_ge(swap_sin, t0 + i * 2 + s + 1)
                            dve.wait_ge(turned, 2 * (t0 + i * 2) + s + 1)
                            nc.vector.tensor_tensor(tile(i * 2 + s), tile(i * 2 + s), sw, ALU.add).then_inc(turned, 1)
                    t0 += count

            @block.gpsimd
            def _(pool):
                t0 = 0
                for tile, count, rows, cols, ones, gain, width, eps, cos, sin, mask in jobs:
                    step = min(2, count)
                    with loop(pool, count // step) as i:
                        for s in range(step):
                            sw = buf[0:rows, 3, s, 0:cols]
                            pool.wait_ge(swapped, t0 + i * 2 + s + 1)
                            nc.gpsimd.tensor_tensor(sw, sw, sin, ALU.mult).then_inc(swap_sin, 1)
                    t0 += count


SCORE_BANKS = ((0, ((3, 0),)), (1, ((0, 0), (2, 128))), (2, ((1, 0),)))
PT_BANKS = ((3, ((0, 0),), "dve"), (4, ((1, 0), (3, 384)), "act"), (5, ((2, 0),), "dve"))
PT_AT = {0: 0, 1: 512, 3: 896, 2: 1024}
PT_SPAN = {3: (0, 512), 4: (512, 512), 5: (1024, 256)}
SCORE_AT = {qt: (bank, c) for bank, parts in SCORE_BANKS for qt, c in parts}


def attention_stage(m, iters, heads, stage_in, keys, krows, values, biases, weights, out, zero=(), add=False):
    nc = m.nc
    nb = heads
    NU = 4 * nb
    prob = m.p.rearrange("p (s q t) -> p s q t", s=2, t=T)
    pt = m.pt
    mx, sums, rinv = m.small[:, 0:8], m.small[:, 8:16], m.small[:, 16:24]
    with stage(m, "q_staged v_staged scores maxed exped summed inverted scaled transposed pt_dve pt_act pv_done o_out zeroed") as (
            q_staged, v_staged, scores, maxed, exped, summed, inverted, scaled, transposed, pt_dve, pt_act, pv_done, o_out, zeroed):
        with nc.Block() as block:
            @block.gpsimd
            def _(pool):
                for part in zero:
                    nc.gpsimd.memset(part, 0.0).then_inc(zeroed, 1)
                if zero:
                    pool.wait_ge(zeroed, len(zero))
                with loop(pool, iters) as i:
                    for j in range(4):
                        pool.wait_ge(pv_done, i * NU + (j + 1) * nb)
                        hold(pool, m)
                        src, dst = stage_in(i, j)
                        nc.gpsimd.tensor_copy(dst, src).then_inc(q_staged, 1)
                        pool.wait_ge(q_staged, i * 4 + j + 1)
                        hold(pool, m)
                        for b in range(nb):
                            nc.gpsimd.tensor_copy(m.vstage(j, b), values(i, j, b)).then_inc(v_staged, 1)
                        pool.wait_ge(v_staged, i * 4 * nb + (j + 1) * nb)

            @block.tensor
            def _(pe):
                pe.sem_inc(pv_done, NU)
                if zero:
                    pe.wait_ge(zeroed, len(zero))
                with loop(pe, iters) as i:
                    def score(u):
                        j, b = divmod(u, nb)
                        if b == 0:
                            pe.wait_ge(q_staged, i * 4 + j + 1)
                        for g, (bank, parts) in enumerate(SCORE_BANKS):
                            pe.wait_ge(exped, i * 3 * NU + 3 * u + g + 1)
                            for qt, c in parts:
                                w = P * (qt + 1)
                                o = m.ps[:, bank, c:c + w]
                                bias, c0 = biases(b, qt)
                                nc.tensor.matmul(o, m.qstage(j)[0:krows, qt * P:(qt + 1) * P], keys(i, j, b)[:, 0:w],
                                                 start=True, stop=False)
                                mm = nc.tensor.matmul(o[:, c0:w], m.ident_bf, bias, start=False, stop=True)
                            mm.then_inc(scores, 1)

                    def turn(u):
                        pe.wait_ge(scaled, i * NU + u + 1)
                        for g, (bank, parts, who) in enumerate(PT_BANKS):
                            pe.wait_ge(*((pt_dve, i * 2 * NU + 2 * u + g // 2 + 1) if who == "dve" else (pt_act, i * NU + u + 1)))
                            for kt, c in parts:
                                for qt in range(kt, TT):
                                    mm = nc.tensor.transpose(m.ps[:, bank, c + (qt - kt) * P:c + (qt - kt + 1) * P],
                                                             prob[:, u % 2, qt, kt * P:(kt + 1) * P], m.ident)
                            mm.then_inc(transposed, 1)

                    def product(u):
                        j, b = divmod(u, nb)
                        half = j % 2
                        if b == 0:
                            pe.wait_ge(v_staged, i * 4 * nb + (j + 1) * nb)
                            pe.wait_ge(o_out, i * 2 + j // 2 + 1)
                        pe.wait_ge(pt_dve, i * 2 * NU + 2 * u + 2 + 2)
                        pe.wait_ge(pt_act, i * NU + u + 1 + 1)
                        for kt in range(TT):
                            mm = nc.tensor.matmul(m.ps[64 * half:64 * half + 64, 6 + j // 2, kt * P:T], m.vstage(j, b)[:, kt, :],
                                                  pt[:, PT_AT[kt]:PT_AT[kt] + T - kt * P],
                                                  start=(b == 0 and kt == 0), stop=(b == nb - 1 and kt == TT - 1))
                        mm.then_inc(pv_done, 1)

                    score(0)
                    for u in range(NU):
                        if u + 1 < NU:
                            score(u + 1)
                        turn(u)
                        product(u)

            @block.vector
            def _(dve):
                dve.sem_inc(pt_dve, 2)
                with loop(dve, iters) as i:
                    def rowmax(u):
                        for g, (bank, parts) in enumerate(SCORE_BANKS):
                            dve.wait_ge(scores, i * 3 * NU + 3 * u + g + 1)
                            for qt, c in parts:
                                r = nc.vector.tensor_reduce(mx[:, 4 * (u % 2) + qt:4 * (u % 2) + qt + 1],
                                                            m.ps[:, bank, c:c + P * (qt + 1)], AX, ALU.max, negate=True)
                            r.then_inc(maxed, 1)

                    def scale(u):
                        j, b = divmod(u, nb)
                        s = 4 * (u % 2)
                        dve.wait_ge(exped, i * 3 * NU + 3 * u + 6)
                        nc.vector.reciprocal(rinv[:, s:s + 4], sums[:, s:s + 4]).then_inc(inverted, 1)
                        w = weights(i, j, b)
                        if w is not None:
                            dve.wait_ge(inverted, i * 2 * NU + 2 * u + 1)
                            nc.vector.tensor_tensor(rinv[:, s:s + 4], rinv[:, s:s + 4], w.rearrange("p t o -> p (t o)"), ALU.mult).then_inc(inverted, 1)
                            dve.wait_ge(inverted, i * 2 * NU + 2 * u + 2)
                        else:
                            dve.wait_ge(inverted, i * NU + u + 1)
                        for qt in range(TT):
                            v = prob[:, u % 2, qt, 0:P * (qt + 1)]
                            r = nc.vector.tensor_scalar(v, v, rinv[:, s + qt:s + qt + 1], None, ALU.mult)
                        r.then_inc(scaled, 1)

                    def copy_pt(u):
                        for g, (bank, parts, who) in enumerate(PT_BANKS):
                            if who == "dve":
                                at, w = PT_SPAN[bank]
                                dve.wait_ge(transposed, i * 3 * NU + 3 * u + g + 1)
                                dve.wait_ge(pv_done, i * NU + u + NU)
                                nc.vector.tensor_copy(pt[:, at:at + w], m.ps[:, bank, 0:w]).then_inc(pt_dve, 1)

                    rowmax(0)
                    for u in range(NU):
                        scale(u)
                        if u + 1 < NU:
                            rowmax(u + 1)
                        copy_pt(u)
                        j, b = divmod(u, nb)
                        if j % 2 and b == nb - 1 and add:
                            dve.wait_ge(pv_done, i * NU + u + 1 + NU)
                            nc.vector.tensor_tensor(out(i, j // 2), out(i, j // 2), m.ps[:, 6 + j // 2, :], ALU.add)\
                                .then_inc(o_out, 1)

            @block.scalar
            def _(act):
                act.sem_inc(exped, 3)
                act.sem_inc(pt_act, 1)
                act.sem_inc(o_out, 2)
                with loop(act, iters) as i:
                    def exps(u):
                        for g, (bank, parts) in enumerate(SCORE_BANKS):
                            act.wait_ge(maxed, i * 3 * NU + 3 * u + g + 1)
                            if g == 0 and u >= 2:
                                act.wait_ge(transposed, i * 3 * NU + 3 * (u - 1))
                            elif g == 0:
                                act.wait_ge(pv_done, i * NU + NU)
                            for qt, c in parts:
                                s = 4 * (u % 2) + qt
                                a = nc.scalar.activation(prob[:, u % 2, qt, 0:P * (qt + 1)], m.ps[:, bank, c:c + P * (qt + 1)],
                                                         ACT.Exp, bias=mx[:, s:s + 1], accum_out=sums[:, s:s + 1])
                            a.then_inc(exped, 1)

                    exps(0)
                    for u in range(NU):
                        if u + 1 < NU:
                            exps(u + 1)
                        for g, (bank, parts, who) in enumerate(PT_BANKS):
                            if who == "act":
                                at, w = PT_SPAN[bank]
                                act.wait_ge(transposed, i * 3 * NU + 3 * u + g + 1)
                                act.wait_ge(pv_done, i * NU + u + NU)
                                nc.scalar.activation(pt[:, at:at + w], m.ps[:, bank, 0:w], ACT.Copy).then_inc(pt_act, 1)
                        j, b = divmod(u, nb)
                        if j % 2 and b == nb - 1 and not add:
                            act.wait_ge(pv_done, i * NU + u + 1 + NU)
                            nc.scalar.activation(out(i, j // 2), m.ps[:, 6 + j // 2, :], ACT.Copy).then_inc(o_out, 1)


def params_stage(m, src):
    with stage(m, "loaded") as (loaded,):
        with m.nc.Block() as block:
            @block.sync
            def _(sp):
                sp.dma_start(m.par[:, 0:NPAR], src[m.layer]).then_inc(loaded, 16)
                sp.wait_ge(loaded, 16)


def merge_stage(m, base, branches, schedule, n_chunks, sources, gates, bias):
    nc = m.nc
    with stage(m, "chunk_done half_done gated added") as (chunk_done, half_done, gated, added):
        with nc.Block() as block:
            @block.sync
            def _(sp):
                load_ahead_loop(sp, m, base, chunk_done, 1, n_chunks)

            @block.tensor
            def _(pe):
                seen = -1
                for at, (n, b, c, u0, ends) in enumerate(schedule):
                    if c > seen:
                        wait_chunk(pe, m, base + c)
                        seen = c
                    if n >= 2:
                        pe.wait_ge(gated, branches * (n - 2) + b + 1)
                    for k in range(4):
                        mm = nc.tensor.matmul(m.ps[:, (n % 2) * 4 + b, :], slab(m, base + c)[:, (u0 + k) * P:(u0 + k + 1) * P],
                                              sources(b, k), start=(k == 0), stop=(k == 3))
                    mm.then_inc(chunk_done if ends else half_done, 1)

            @block.vector
            def _(dve):
                full = half = adds = 0
                for at, (n, b, c, u0, ends) in enumerate(schedule):
                    if ends:
                        full += 1
                        dve.wait_ge(chunk_done, full)
                    else:
                        half += 1
                        dve.wait_ge(half_done, half)
                    g = m.p[:, ((n % 2) * 3 + b) * T:((n % 2) * 3 + b + 1) * T]
                    if bias is not None and b == 1:
                        nc.vector.scalar_tensor_tensor(g, m.ps[:, (n % 2) * 4 + b, :], bias(n), gates(b, n), ALU.add, ALU.mult)\
                            .then_inc(gated, 1)
                    else:
                        nc.vector.tensor_tensor(g, m.ps[:, (n % 2) * 4 + b, :], gates(b, n), ALU.mult).then_inc(gated, 1)
                    if b == branches - 1:
                        g0 = m.p[:, (n % 2) * 3 * T:((n % 2) * 3 + 1) * T]
                        first = g0
                        for bb in range(1, branches):
                            gb = m.p[:, ((n % 2) * 3 + bb) * T:((n % 2) * 3 + bb + 1) * T]
                            dve.wait_ge(gated, branches * n + bb + 1)
                            if adds and bb > 1:
                                dve.wait_ge(added, adds)
                            nc.vector.tensor_tensor(m.raw[:, n, :], first, gb, ALU.add).then_inc(added, 1)
                            adds += 1
                            first = m.raw[:, n, :]


def mla_project_stage(m):
    nc = m.nc
    base = C1["mla"]
    qm, km, vm = m.q_mla, m.k_mla, m.v_mla
    with stage(m, "chunk_done head_done q_out k_out v_done v_out") as (chunk_done, head_done, q_out, k_out, v_done, v_out):
        with nc.Block() as block:
            @block.sync
            def _(sp):
                load_ahead_loop(sp, m, base, chunk_done, 1, 6)

            @block.tensor
            def _(pe):
                for h in range(NH):
                    if h % 2 == 0:
                        wait_chunk(pe, m, base + h // 2)
                    if h >= 4:
                        pe.wait_ge(q_out, h - 3)
                    for k in range(3):
                        u = (h % 2) * 3 + k
                        mm = nc.tensor.matmul(m.ps[0:MQK, h % 4, :], slab(m, base + h // 2)[:, u * P:u * P + MQK], m.raw[:, k, :],
                                              start=(k == 0), stop=(k == 2))
                    mm.then_inc(chunk_done if h % 2 else head_done, 1)
                wait_chunk(pe, m, base + 4)
                for p in range(4):
                    for k in range(2):
                        mm = nc.tensor.matmul(m.ps[:, 4 + p, :], slab(m, base + 4)[:, (2 * p + k) * P:(2 * p + k + 1) * P],
                                              m.raw[:, 3 + k, :], start=(k == 0), stop=(k == 1))
                    mm.then_inc(chunk_done if p == 3 else head_done, 1)
                wait_chunk(pe, m, base + 5)
                pe.wait_ge(q_out, NH)
                for t in range(TT):
                    for k in range(2):
                        mm = nc.tensor.matmul(m.ps[:, t, :], m.raw[:, 3 + k, t * P:(t + 1) * P],
                                              slab(m, base + 5)[:, k * T:(k + 1) * T], start=(k == 0), stop=(k == 1))
                    mm.then_inc(chunk_done if t == TT - 1 else v_done, 1)

            @block.scalar
            def _(act):
                for h in range(NH):
                    act.wait_ge(*((chunk_done, h // 2 + 1) if h % 2 else (head_done, h // 2 + 1)))
                    nc.scalar.activation(qm[0:MQK, h, :], m.ps[0:MQK, h % 4, :], ACT.Copy).then_inc(q_out, 1)
                for t in range(TT):
                    act.wait_ge(*((chunk_done, 6) if t == TT - 1 else (v_done, t + 1)))
                    nc.scalar.activation(vm[:, t, :], m.ps[:, t, :], ACT.Copy)

            @block.vector
            def _(dve):
                for p in range(4):
                    dve.wait_ge(*((chunk_done, 5) if p == 3 else (head_done, 4 + p + 1)))
                    for half in range(2):
                        nc.vector.tensor_copy(km[0:MNOPE, 2 * p + half, :], m.ps[64 * half:64 * half + 64, 4 + p, :])

            @block.gpsimd
            def _(pool):
                for h in range(NH):
                    nc.gpsimd.tensor_copy(km[MNOPE:MQK, h, :], m.krope[MNOPE:MQK, :])


def misc1_stage(m):
    nc = m.nc
    base = C1["misc"]
    with stage(m, "chunk_done kr_done gates_done v_done gates_exp gates_sig") as (
            chunk_done, kr_done, gates_done, v_done, gates_exp, gates_sig):
        with nc.Block() as block:
            @block.sync
            def _(sp):
                load_ahead_loop(sp, m, base, chunk_done, 1, 4)

            @block.tensor
            def _(pe):
                wait_chunk(pe, m, base)
                for k in range(KD):
                    mm = nc.tensor.matmul(m.ps[:, 0, :], slab(m, base)[:, k * P:(k + 1) * P], m.h[:, k, :],
                                          start=(k == 0), stop=(k == KD - 1))
                mm.then_inc(chunk_done, 1)
                wait_chunk(pe, m, base + 1)
                for k in range(KD):
                    mm = nc.tensor.matmul(m.ps[64:96, 1, :], slab(m, base + 1)[:, k * P:k * P + MROPE], m.h[:, k, :],
                                          start=(k == 0), stop=(k == KD - 1))
                mm.then_inc(kr_done, 1)
                for t in range(TT):
                    for k in range(KD):
                        mm = nc.tensor.matmul(m.ps[:, 2, t * 24:(t + 1) * 24], m.h[:, k, t * P:(t + 1) * P],
                                              slab(m, base + 1)[:, k * P + 32:k * P + 56], start=(k == 0), stop=(k == KD - 1))
                mm.then_inc(chunk_done, 1)
                wait_chunk(pe, m, base + 2)
                wait_chunk(pe, m, base + 3)
                for t in range(TT):
                    for k in range(KD):
                        w = slab(m, base + 2 + k // 4)[:, (k % 4) * 256:(k % 4 + 1) * 256]
                        mm = nc.tensor.matmul(m.ps[:, 3 + t, 0:256], m.h[:, k, t * P:(t + 1) * P], w,
                                              start=(k == 0), stop=(k == KD - 1))
                        if t == TT - 1 and k == 3:
                            mm.then_inc(chunk_done, 1)
                    mm.then_inc(chunk_done if t == TT - 1 else v_done, 1)

            @block.scalar
            def _(act):
                act.wait_ge(chunk_done, 1)
                nc.scalar.activation(m.raw[:, 20, :], m.ps[:, 0, :], ACT.Copy)
                act.wait_ge(kr_done, 1)
                nc.scalar.activation(m.krope[64:96, :], m.ps[64:96, 1, :], ACT.Copy)
                act.wait_ge(chunk_done, 2)
                nc.scalar.activation(m.gn, m.ps[:, 2, 0:96], ACT.Sigmoid).then_inc(gates_sig, 1)

            @block.vector
            def _(dve):
                dve.wait_ge(gates_sig, 1)
                gn = m.gn.rearrange("p (t h n) -> p t h n", t=TT, n=3)
                gm = m.gcmp.rearrange("p (t h) -> p t h", t=TT)
                for t in range(TT):
                    nc.vector.tensor_scalar(gm[:, t, :], gn[:, t, :, 0], m.con("rowok", 4)[:, t:t + 1], None, ALU.mult)
                for t in range(TT):
                    dve.wait_ge(*((chunk_done, 4) if t == TT - 1 else (v_done, t + 1)))
                    nc.vector.tensor_copy(m.v_nsa[:, t, :], m.ps[:, 3 + t, 0:256])


def compress_stage(m):
    nc = m.nc
    base = C1["cmp"]
    kc2 = m.kc2
    with stage(m, "chunk_done shifted hidden sig silu kcmp_done copied") as (
            chunk_done, shifted, hidden, sig, silu, kcmp_done, copied):
        with nc.Block() as block:
            @block.sync
            def _(sp):
                load_ahead_loop(sp, m, base, chunk_done, 1, 6)

            @block.vector
            def _(dve):
                for which in range(2):
                    src = m.raw[:, 19 + which, :]
                    if which == 1:
                        dve.wait_ge(chunk_done, 2)
                    for g in range(2):
                        nc.vector.tensor_copy(kc2[0:64, g, :], src[64 * g:64 * g + 64, :])
                        r = nc.vector.tensor_copy(kc2[64:128, g, 0:T - 1], src[64 * g:64 * g + 64, 1:T])
                    r.then_inc(shifted, 1)
                for which in range(2):
                    dve.wait_ge(sig, which + 1)
                    nc.vector.tensor_tensor(m.hid[:, which, :], m.ps[:, which, 0:62], m.hsig[:, which, :], ALU.mult).then_inc(silu, 1)
                dve.wait_ge(chunk_done, 6)
                for g in range(2):
                    nc.vector.tensor_copy(m.vcmp[0:NCMP, g, :], m.ps[0:NCMP, 3 + g, 0:64])

            @block.tensor
            def _(pe):
                for which, pe_col in enumerate(("pe_k", "pe_v")):
                    pe.wait_ge(shifted, which + 1)
                    for p in range(16):
                        if p % 8 == 0:
                            wait_chunk(pe, m, base + 2 * which + p // 8)
                        w = slab(m, base + 2 * which + p // 8)[:, (p % 8) * P:(p % 8 + 1) * P]
                        v = kc2.rearrange("p g (j s) -> p g j s", s=CSTRIDE)
                        o = 2 * p // CSTRIDE
                        tok = v[:, :, o:o + NCMP, 2 * p % CSTRIDE]
                        nc.tensor.matmul(m.ps[:, which, 0:62].rearrange("p (g j) -> p g j", g=2), w, tok, start=(p == 0), stop=False)
                        mm = nc.tensor.matmul(m.ps[:, which, 0:62], w, m.param(pe_col, 16)[:, p:p + 1].to_broadcast([P, 62]),
                                              start=False, stop=(p == 15))
                        if p % 8 == 7:
                            mm.then_inc(chunk_done, 1)
                for which in range(2):
                    pe.wait_ge(silu, which + 1)
                    wait_chunk(pe, m, base + 4 + which)
                    if which == 0:
                        nc.tensor.matmul(m.ps[0:64, 2, 0:62], slab(m, base + 4)[:, 0:64], m.hid[:, 0, :], start=True, stop=True)\
                            .then_inc(chunk_done, 1)
                    else:
                        for g in range(2):
                            mm = nc.tensor.matmul(m.ps[0:NCMP, 3 + g, 0:64], m.hid[:, 1, g * NCMP:(g + 1) * NCMP],
                                                  slab(m, base + 5)[:, 0:64], start=True, stop=True)
                        mm.then_inc(chunk_done, 1)

            @block.scalar
            def _(act):
                for which in range(2):
                    act.wait_ge(chunk_done, 2 * which + 2)
                    nc.scalar.activation(m.hsig[:, which, :], m.ps[:, which, 0:62], ACT.Sigmoid).then_inc(sig, 1)
                act.wait_ge(chunk_done, 5)
                nc.scalar.activation(m.kcmp[0:64, :], m.ps[0:64, 2, 0:62], ACT.Copy)


def compressed_attention_stage(m):
    nc = m.nc
    W = TT * NCMP
    with stage(m, "dup scores masked maxed centred exped summed inverted weighted scaled transposed copied pv_done") as (
            dup, scores, masked, maxed, centred, exped, summed, inverted, weighted, scaled, transposed, copied, pv_done):
        sc = m.p[:, 0:2 * 128].rearrange("p (s w) -> p s w", s=2)
        st = m.small[:, 32:64]
        ptc = m.p[:, 512:512 + 2 * T].rearrange("p (s t) -> p s t", s=2)
        mask = m.con("mask_c", W)

        def three(ap):
            return ap[:, 0:W].rearrange("p (t j) -> p t j", t=TT)

        with nc.Block() as block:
            @block.scalar
            def _(act):
                nc.scalar.activation(m.kcmp[64:128, :], m.kcmp[0:64, :], ACT.Copy).then_inc(dup, 1)
                for h in range(NH):
                    act.wait_ge(centred, h + 1)
                    nc.scalar.activation(sc[:, h % 2, 0:W], sc[:, h % 2, 0:W], ACT.Exp).then_inc(exped, 1)
                    act.wait_ge(transposed, h + 1)
                    nc.scalar.activation(ptc[0:NCMP, h % 2, :], m.ps[0:NCMP, 2 + h % 2, :], ACT.Copy).then_inc(copied, 1)
                    if h % 2:
                        act.wait_ge(pv_done, h + 1)
                        nc.scalar.activation(m.o_nsa[:, h // 2, :], m.ps[:, 4 + (h // 2) % 2, :], ACT.Copy).then_inc(dup, 1)

            @block.tensor
            def _(pe):
                pe.wait_ge(dup, 1)

                def score(h):
                    r0 = 64 * (h % 2)
                    if h >= 2:
                        pe.wait_ge(masked, h - 1)
                    for t in range(TT):
                        mm = nc.tensor.matmul(m.ps[:, h % 2, t * NCMP:(t + 1) * NCMP],
                                              m.raw[r0:r0 + 64, 13 + h // 2, t * P:(t + 1) * P],
                                              m.kcmp[r0:r0 + 64, (h // 4) * NCMP:(h // 4 + 1) * NCMP], start=True, stop=True)
                    mm.then_inc(scores, 1)

                score(0)
                for h in range(NH):
                    if h + 1 < NH:
                        score(h + 1)
                    pe.wait_ge(scaled, h + 1)
                    if h >= 2:
                        pe.wait_ge(copied, h - 1)
                    for t in range(TT):
                        mm = nc.tensor.transpose(m.ps[0:NCMP, 2 + h % 2, t * P:(t + 1) * P],
                                                 sc[:, h % 2, t * NCMP:(t + 1) * NCMP], m.ident)
                    mm.then_inc(transposed, 1)
                    pe.wait_ge(copied, h + 1)
                    if h >= 4:
                        pe.wait_ge(dup, 1 + h // 2 - 1)
                    r0 = 64 * (h % 2)
                    nc.tensor.matmul(m.ps[r0:r0 + 64, 4 + (h // 2) % 2, :], m.vcmp[0:NCMP, h // 4, :], ptc[0:NCMP, h % 2, :],
                                     start=True, stop=True).then_inc(pv_done, 1)

            @block.vector
            def _(dve):
                for h in range(NH):
                    s, a = sc[:, h % 2, :], st[:, 16 * (h % 2):16 * (h % 2) + 16]
                    dve.wait_ge(scores, h + 1)
                    if h >= 2:
                        dve.wait_ge(transposed, h - 1)
                    nc.vector.tensor_tensor(s[:, 0:W], m.ps[:, h % 2, 0:W], mask, ALU.add).then_inc(masked, 1)
                    dve.wait_ge(masked, h + 1)
                    nc.vector.tensor_reduce(a[:, 0:4], three(s), AX, ALU.max).then_inc(maxed, 1)
                    dve.wait_ge(maxed, h + 1)
                    nc.vector.tensor_tensor(three(s), three(s), a[:, 0:4].rearrange("p (t o) -> p t o", o=1).to_broadcast([P, TT, NCMP]),
                                            ALU.subtract).then_inc(centred, 1)
                    dve.wait_ge(exped, h + 1)
                    nc.vector.tensor_reduce(a[:, 4:8], three(s), AX, ALU.add).then_inc(summed, 1)
                    dve.wait_ge(summed, h + 1)
                    nc.vector.reciprocal(a[:, 8:12], a[:, 4:8]).then_inc(inverted, 1)
                    dve.wait_ge(inverted, h + 1)
                    g = m.gcmp.rearrange("p (t h) -> p t h", t=TT)[:, :, h]
                    nc.vector.tensor_tensor(a[:, 12:16], a[:, 8:12], g, ALU.mult).then_inc(weighted, 1)
                    dve.wait_ge(weighted, h + 1)
                    nc.vector.tensor_tensor(three(s), three(s), a[:, 12:16].rearrange("p (t o) -> p t o", o=1).to_broadcast([P, TT, NCMP]),
                                            ALU.mult).then_inc(scaled, 1)


def conv_prepare(m, act, glu_sig, *rest):
    for c in range(CCH):
        act_i = m.nc.scalar.activation(m.raw[:, 6 + 2 * c, :], m.raw[:, 6 + 2 * c, :], ACT.Sigmoid,
                                       bias=m.param("b_glu", 8)[:, 4 + c:5 + c])
        act_i.then_inc(glu_sig, 1)


def conv_taps(m, dve, glu_sig, padded, tapped):
    nc = m.nc
    up = m.p[:, 0:CCH * 544].rearrange("p (c t) -> p c t", c=CCH)
    w = m.param("w_dw", CCH * TAPS).rearrange("p (c w) -> p c w", c=CCH)
    for c in range(CCH):
        nc.vector.memset(up[:, c, 0:TAPS - 1], 0.0)
    for c in range(CCH):
        dve.wait_ge(glu_sig, c + 1)
        nc.vector.scalar_tensor_tensor(up[:, c, TAPS - 1:TAPS - 1 + T], m.raw[:, 5 + 2 * c, :], m.param("b_glu", 8)[:, c:c + 1],
                                       m.raw[:, 6 + 2 * c, :], ALU.add, ALU.mult).then_inc(padded, 1)
    for c in range(CCH):
        dve.wait_ge(padded, c + 1)
        nc.vector.tensor_scalar(m.raw[:, 13 + c, :], up[:, c, 0:T], w[:, c, 0:1], m.param("b_dw", 4)[:, c:c + 1],
                                ALU.mult, ALU.add).then_inc(tapped, 1)
    with dve.Fori(1, TAPS) as i:
        for c in range(CCH):
            dve.wait_ge(tapped, i * CCH + (c + 1 - CCH))
            nc.vector.scalar_tensor_tensor(m.raw[:, 13 + c, :], up[:, c, bass.ds(i, T)], w[:, c, bass.ds(i, 1)], m.raw[:, 13 + c, :],
                                           ALU.mult, ALU.add).then_inc(tapped, 1)
    dve.wait_ge(tapped, CCH * TAPS)


def conv_norm_stage(m):
    nc = m.nc
    x = lambda c: m.raw[:, 13 + c, :]
    sq = m.p[:, 0:4 * T].rearrange("p (k t) -> p k t", t=T)
    mu, rstd, sig = m.pt[:, 0:T], m.pt[:, T:2 * T], m.p[:, 4 * T:8 * T].rearrange("p (k t) -> p k t", t=T)
    var = m.spare
    with stage(m, "summed mean centred squared varsum rooted step rstd_done scaled sig_done") as (
            summed, mean, centred, squared, varsum, rooted, step, rstd_done, scaled, sig_done):
        with nc.Block() as block:
            @block.tensor
            def _(pe):
                for c in range(CCH):
                    mm = nc.tensor.matmul(m.ps[:, 0, :], m.ones, x(c), start=(c == 0), stop=(c == CCH - 1))
                mm.then_inc(summed, 1)
                for c in range(CCH):
                    pe.wait_ge(squared, c + 1)
                    mm = nc.tensor.matmul(m.ps[:, 1, :], m.ones, sq[:, c, :], start=(c == 0), stop=(c == CCH - 1))
                mm.then_inc(varsum, 1)

            @block.scalar
            def _(act):
                act.wait_ge(summed, 1)
                nc.scalar.activation(mu, m.ps[:, 0, :], ACT.Copy, scale=1.0 / CONV_CH).then_inc(mean, 1)
                for c in range(CCH):
                    act.wait_ge(centred, c + 1)
                    nc.scalar.activation(sq[:, c, :], x(c), ACT.Square).then_inc(squared, 1)
                act.wait_ge(varsum, 1)
                nc.scalar.activation(rstd, m.ps[:, 1, :], ACT.Sqrt, bias=m.eps, scale=1.0 / CONV_CH).then_inc(rooted, 1)
                nc.scalar.activation(var, m.ps[:, 1, :], ACT.Identity, bias=m.eps, scale=1.0 / CONV_CH).then_inc(rooted, 1)
                for c in range(CCH):
                    act.wait_ge(scaled, c + 1)
                    nc.scalar.activation(sig[:, c, :], x(c), ACT.Sigmoid, bias=m.param("b_ln", 4)[:, c:c + 1]).then_inc(sig_done, 1)

            @block.vector
            def _(dve):
                dve.wait_ge(mean, 1)
                for c in range(CCH):
                    nc.vector.tensor_tensor(x(c), x(c), mu, ALU.subtract).then_inc(centred, 1)
                dve.wait_ge(rooted, 2)
                refined_rsqrt(m, dve, step, 0, var, rstd, rstd, sq[:, 0, :]).then_inc(rstd_done, 1)
                dve.wait_ge(rstd_done, 1)
                for c in range(CCH):
                    nc.vector.scalar_tensor_tensor(x(c), x(c), m.param("g_ln", 4)[:, c:c + 1], rstd, ALU.mult, ALU.mult).then_inc(scaled, 1)
                for c in range(CCH):
                    dve.wait_ge(sig_done, c + 1)
                    nc.vector.scalar_tensor_tensor(x(c), x(c), m.param("b_ln", 4)[:, c:c + 1], sig[:, c, :], ALU.add, ALU.mult)


def first_layer(m, par):
    nc = m.nc
    params_stage(m, par)
    K8 = [list(range(KD))]

    def copy_act(dst):
        return lambda eng, bank, n: m.nc.scalar.activation(dst(n), bank, ACT.Copy)

    def copy_dve(dst):
        return lambda eng, bank, n: m.nc.vector.tensor_copy(dst(n), bank)

    def add_x(eng, bank, n):
        return nc.vector.tensor_tensor(m.x[:, n, :], m.x[:, n, :], bank, ALU.add)

    X, H = (lambda k: m.x[:, k, :]), (lambda k: m.h[:, k, :])
    raw = lambda n: m.raw[:, n, :]
    norm_stage(m, X, KD, H, lambda k: m.param("g_mix", 8)[:, k:k + 1], D)
    linear_stage(m, C1["raw"], 5, [K8] * 4, H,
                 [("act", copy_act(raw)), ("dve", copy_dve(raw))] * 2)
    misc1_stage(m)
    norm_stage(m, raw, 3, raw, lambda k: m.param("g_cq", 3)[:, k:k + 1], QRANK)
    norm_stage(m, lambda k: raw(3 + k), 2, lambda k: raw(3 + k), lambda k: m.param("g_ckv", 2)[:, k:k + 1], KVRANK)
    mla_project_stage(m)
    compress_stage(m)
    rows96, rows128, rows64 = m.ones[0:MQK, 0:MQK], m.bd64, m.bd64[0:64, 0:64]
    rotate_stage(m, [
        (lambda i: m.q_mla[0:MQK, i, :], NH, MQK, T, rows96, m.param("gq_mla", 1)[0:MQK], 1, m.con("eps_mla", 1),
         m.con("cos_m", T)[0:MQK], m.con("sin_m", T)[0:MQK], SWAP32),
        (lambda i: m.k_mla[0:MQK, i, :], NH, MQK, T, rows96, m.param("gk_mla", 1)[0:MQK], MQK, m.eps,
         m.con("cos_m", T)[0:MQK], m.con("sin_m", T)[0:MQK], SWAP32),
        (lambda i: raw(i + 13), 4, P, T, rows128, m.param("gq_nsa", 1), 1, m.con("eps_nsa", 1),
         m.con("cos_n", T), m.con("sin_n", T), SWAP16),
        (lambda i: raw(i + 17), 2, P, T, rows128, m.param("gk_nsa", 1), DH, m.eps,
         m.con("cos_n", T), m.con("sin_n", T), SWAP16),
        (lambda i: m.kcmp[0:64, :], 1, 64, 62, rows64, m.param("gk_nsa", 1)[0:64], DH, m.eps,
         m.con("cos_c", 62)[0:64], m.con("sin_c", 62)[0:64], SWAP16),
    ])
    causal = lambda b, qt: (m.causal_bf, qt * P)
    attention_stage(m, 2, 1, lambda i, j: (m.q_mla[0:MQK, i * 4 + j, :], m.qstage(j)[0:MQK, :]),
                    lambda i, j, b: m.k_mla[0:MQK, i * 4 + j, :], MQK,
                    lambda i, j, b: m.v_mla[:, :, bass.ds(i * (4 * DH) + j * DH, DH)], causal,
                    lambda i, j, b: None, lambda i, p: m.o_mla[:, i * 2 + p, :])
    compressed_attention_stage(m)
    attention_stage(m, 2, 2, lambda i, j: (m.raw[64 * (j % 2):64 * (j % 2) + 64, i + (13 + 2 * (j // 2)), :],
                                           m.qstage(j)[64 * (j // 2):64 * (j // 2) + 64, :]),
                    lambda i, j, b: raw(17 + b), P,
                    lambda i, j, b: m.v_nsa[:, :, b * 128 + (j // 2) * 64:b * 128 + (j // 2) * 64 + 64], causal,
                    lambda i, j, b: m.gn.rearrange("p (t c) -> p t c", t=TT)[:, :, bass.ds(i * 6 + (12 * (j // 2) + 3 * (j % 2) + 1 + b), 1)],
                    lambda i, p: m.o_nsa[:, i + 2 * p, :],
                    zero=[m.qstage(j)[64 - 64 * (j // 2):128 - 64 * (j // 2), :] for j in range(4)], add=True)
    linear_stage(m, C1["gate"], 6, [K8] * 4, H,
                 [("act", lambda e, bank, n: nc.scalar.activation(m.g[:, n, :], bank, ACT.Sigmoid))] * 4,
                 extra="glu_sig padded tapped",
                 act_first=lambda act, *s: conv_prepare(m, act, *s), dve_side=lambda dve, *s: conv_taps(m, dve, *s))
    conv_norm_stage(m)
    schedule = [(2 * p + h, b, 3 * p + b, 4 * h, h == 1) for p in range(4) for h in range(2) for b in range(3)]
    merge_stage(m, C1["merge"], 3, schedule, 12,
                lambda b, k: (m.o_mla[:, k, :], raw(13 + k), m.o_nsa[:, k, :])[b],
                lambda b, n: m.g[:, 8 * b + n, :], lambda n: m.param("b_out", 8)[:, n:n + 1])
    linear_stage(m, C1["wout"], 2, [K8] * 4, raw, [("dve", add_x)] * 4)
    norm_stage(m, X, KD, H, lambda k: m.param("g_ffn", 8)[:, k:k + 1], D)
    linear_stage(m, C1["ff_up"], 8, [K8] * 4, H,
                 [("act", lambda e, bank, n: nc.scalar.activation(m.hidden[:, n, :], bank, ACT.Relu))] * 4,
                 post=lambda dve, n: nc.vector.tensor_tensor(m.hidden[:, n, :], m.hidden[:, n, :], m.hidden[:, n, :], ALU.mult))
    linear_stage(m, C1["ff_down"], 4, [[[8 * c + k for k in range(8)] for c in range(4)]] * 2,
                 lambda k: m.hidden[:, k, :], [("dve", add_x)] * 2)


def position_stage(m, tri, vecs, pos):
    nc = m.nc
    turn = 2 * np.pi
    c1 = 6.28125
    c2 = float(np.round((turn - c1) * 2.0 ** 21) / 2.0 ** 21)
    c3 = float(turn - c1 - c2)
    magic = 1.5 * 2.0 ** 23
    lim = 3.1415925
    ang, n_, r, rc = (m.p[:, k * T:(k + 1) * T] for k in range(4))
    posi = m.p[:, 4 * T:5 * T].bitcast(I32)
    cos, sin = m.con("cos_n", T), m.con("sin_n", T)
    with stage(m, "pos_loaded step args lut") as (pos_loaded, step, args, lut):
        with nc.Block() as block:
            @block.sync
            def _(sp):
                sp.dma_start(posi, pos.to_broadcast([P, T])).then_inc(pos_loaded, 16)
                sp.dma_start(m.con("cos_m", T), tri).then_inc(pos_loaded, 16)
                sp.dma_start(m.con("final_g", 16), vecs).then_inc(pos_loaded, 16)
                sp.wait_ge(pos_loaded, 48)

            @block.vector
            def _(dve):
                done = 0

                def then(ins):
                    nonlocal done
                    ins.then_inc(step, 1)
                    done += 1
                    dve.wait_ge(step, done)

                dve.wait_ge(pos_loaded, 48)
                then(nc.vector.tensor_copy(ang, posi))
                then(nc.vector.tensor_scalar(ang, ang, m.con("invf", 1), None, ALU.mult))
                then(nc.vector.tensor_scalar(n_, ang, 1.0 / turn, magic, ALU.mult, ALU.add))
                then(nc.vector.tensor_scalar(n_, n_, magic, None, ALU.subtract))
                then(nc.vector.scalar_tensor_tensor(r, n_, -c1, ang, ALU.mult, ALU.add))
                then(nc.vector.scalar_tensor_tensor(r, n_, -c2, r, ALU.mult, ALU.add))
                then(nc.vector.scalar_tensor_tensor(r, n_, -c3, r, ALU.mult, ALU.add))
                then(nc.vector.tensor_scalar(rc, r, np.pi / 2, None, ALU.add))
                then(nc.vector.tensor_scalar(ang, rc, np.pi, -turn, ALU.is_gt, ALU.mult))
                then(nc.vector.tensor_tensor(rc, rc, ang, ALU.add))
                then(nc.vector.tensor_scalar(rc, rc, lim, -lim, ALU.min, ALU.max))
                then(nc.vector.tensor_scalar(r, r, lim, -lim, ALU.min, ALU.max))
                nc.vector.tensor_scalar(r, r, 1.0, None, ALU.mult).then_inc(args, 1)
                dve.wait_ge(lut, 2)
                then(nc.vector.tensor_scalar(sin, sin, m.con("sgn", 1), None, ALU.mult))
                then(nc.vector.tensor_scalar(cos, cos, m.con("rotm", 1), m.con("unrot", 1), ALU.mult, ALU.add))

            @block.scalar
            def _(act):
                act.wait_ge(args, 1)
                nc.scalar.activation(sin, r, ACT.Sin).then_inc(lut, 1)
                nc.scalar.activation(cos, rc, ACT.Sin).then_inc(lut, 1)


def modulation_stage(m):
    nc = m.nc
    mod = m.mod
    with stage(m, "chunk_done added raised") as (chunk_done, added, raised):
        with nc.Block() as block:
            @block.sync
            def _(sp):
                load_ahead_loop(sp, m, C2["mod"], chunk_done, 12, 4)

            @block.tensor
            def _(pe):
                with pe.Fori(0, 12) as i:
                    for j in range(4):
                        wait_chunk(pe, m, C2["mod"] + j, i, 4)
                        for k in range(KD):
                            mm = nc.tensor.matmul(m.ps[:, 0, bass.ds(i * 4 + j, 1)], slab(m, C2["mod"] + j)[:, k * P:(k + 1) * P],
                                                  m.con("cvec", 8)[:, k:k + 1], start=(k == 0), stop=(k == KD - 1))
                        mm.then_inc(chunk_done, 1)

            @block.vector
            def _(dve):
                dve.wait_ge(chunk_done, 48)
                nc.vector.tensor_tensor(mod, m.ps[:, 0, 0:48], m.param("mod_b", 48), ALU.add).then_inc(added, 1)
                dve.wait_ge(added, 1)
                for a, (g, sc) in enumerate((("g1", 8), ("g2", 32))):
                    nc.vector.scalar_tensor_tensor(m.gains[:, 8 * a:8 * a + 8], mod[:, sc:sc + 8], 1.0, m.param(g, 8),
                                                   ALU.add, ALU.mult).then_inc(raised, 1)


def misc2_stage(m):
    nc = m.nc
    base = C2["misc"]
    with stage(m, "chunk_done") as (chunk_done,):
        with nc.Block() as block:
            @block.sync
            def _(sp):
                load_ahead_loop(sp, m, base, chunk_done, 1, 4)

            @block.tensor
            def _(pe):
                wait_chunk(pe, m, base)
                for k in range(KD):
                    mm = nc.tensor.matmul(m.ps[:, 0, :], slab(m, base)[:, k * P:(k + 1) * P], m.h[:, k, :],
                                          start=(k == 0), stop=(k == KD - 1))
                mm.then_inc(chunk_done, 1)
                for n_, w in ((1, 8), (2, 64), (3, 8)):
                    wait_chunk(pe, m, base + n_)
                    for t in range(TT):
                        for k in range(KD):
                            mm = nc.tensor.matmul(m.ps[:, n_, t * w:(t + 1) * w], m.h[:, k, t * P:(t + 1) * P],
                                                  slab(m, base + n_)[:, k * P:k * P + w], start=(k == 0), stop=(k == KD - 1))
                    mm.then_inc(chunk_done, 1)

            @block.scalar
            def _(act):
                act.wait_ge(chunk_done, 1)
                nc.scalar.activation(m.raw[:, 8, :], m.ps[:, 0, :], ACT.Copy)
                nc.scalar.activation(m.raw[64:128, 9, :], m.ps[64:128, 0, :], ACT.Copy)
                nc.scalar.activation(m.raw[0:64, 9, :], m.ps[64:128, 0, :], ACT.Copy)
                act.wait_ge(chunk_done, 4)
                nc.scalar.activation(m.wi, m.ps[:, 3, 0:32], ACT.Copy, scale=float(NH) ** -0.5)

            @block.vector
            def _(dve):
                dve.wait_ge(chunk_done, 2)
                nc.vector.tensor_tensor(m.logf, m.ps[:, 1, 0:32], m.param("fbias", 32), ALU.add)
                dve.wait_ge(chunk_done, 3)
                nc.vector.tensor_copy(m.va, m.ps[:, 2, 0:256])


def index_stage(m):
    nc = m.nc
    relu = m.p[:, 0:4 * T].rearrange("p (s t) -> p s t", s=4)
    cum = m.p[:, 4 * T:6 * T].rearrange("p (s t) -> p s t", s=2)
    neg, absx, low, ex = (m.small[:, 192 + 16 * 0:224], m.small[:, 224:256], m.small[:, 0:32], m.small[:, 32:64])
    work = m.work
    order = [(h, qt) for h in range(NH) for qt in range(1, TT)]
    with stage(m, "step log_exp logf_done summed cum_done filled rows_set started scored rectified") as (
            step, log_exp, logf_done, summed, cum_done, filled, rows_set, started, scored, rectified):
        with nc.Block() as block:
            @block.gpsimd
            def _(pool):
                nc.gpsimd.memset(m.qf[64:96, :, :], 0.0).then_inc(filled, 1)
                nc.gpsimd.memset(m.qf[96:97, :, :], 1.0).then_inc(filled, 1)
                nc.gpsimd.memset(m.kf[64:96, :, :], 0.0).then_inc(filled, 1)
                pool.wait_ge(filled, 3)
                nc.gpsimd.memset(m.kf[64:65, :, :], 1.0).then_inc(filled, 1)

            @block.sync
            def _(sp):
                sp.wait_ge(cum_done, 2)
                sp.wait_ge(filled, 4)
                for h in range(NH):
                    sp.dma_start(m.qf[64:65, h, :], cum[h:h + 1, 0, :]).then_inc(rows_set, 16)
                    sp.dma_start(m.kf[96:97, h, :], cum[h:h + 1, 1, :]).then_inc(rows_set, 16)
                sp.wait_ge(rows_set, 16 * 2 * NH)

            @block.scalar
            def _(act):
                use_log_exp(m)
                act.wait_ge(step, 2)
                nc.scalar.activation(ex, absx, ACT.Exp, scale=-1.0).then_inc(log_exp, 1)
                act.wait_ge(log_exp, 1)
                nc.scalar.activation(ex, ex, ACT.Ln, bias=1.0).then_inc(log_exp, 1)
                for n_, (h, qt) in enumerate(order):
                    w = P * (qt + 1)
                    act.wait_ge(scored, n_ + 1)
                    if n_ >= 4:
                        act.wait_ge(started, 3 + n_ - 3)
                    nc.scalar.activation(relu[:, n_ % 4, 0:w], m.ps[:, n_ % 4, 0:w], ACT.Relu, scale=float(DH) ** -0.5)\
                        .then_inc(rectified, 1)
                act.wait_ge(summed, 1)
                nc.scalar.activation(cum[0:NH, 0, :], m.ps[0:NH, 4, :], ACT.Copy).then_inc(cum_done, 1)
                nc.scalar.activation(cum[0:NH, 1, :], m.ps[0:NH, 4, :], ACT.Copy, scale=-1.0).then_inc(cum_done, 1)

            @block.vector
            def _(dve):
                nc.vector.tensor_scalar(neg, m.logf, -1.0, None, ALU.mult).then_inc(step, 1)
                dve.wait_ge(step, 1)
                nc.vector.tensor_tensor(absx, neg, m.logf, ALU.max).then_inc(step, 1)
                nc.vector.tensor_scalar(low, neg, 0.0, None, ALU.max).then_inc(step, 1)
                dve.wait_ge(log_exp, 2)
                dve.wait_ge(step, 3)
                nc.vector.tensor_tensor(low, low, ex, ALU.add).then_inc(step, 1)
                dve.wait_ge(step, 4)
                nc.vector.tensor_scalar(m.logf, low, -1.0, None, ALU.mult).then_inc(logf_done, 1)
                for qt in range(1, TT):
                    nc.vector.memset(work[qt][:, 0:qt * P], 0.0)
                    nc.vector.tensor_copy(work[qt][:, qt * P:(qt + 1) * P], m.con("chunkmask", P)).then_inc(started, 1)
                for n_, (h, qt) in enumerate(order):
                    w = P * (qt + 1)
                    dve.wait_ge(rectified, n_ + 1)
                    dve.wait_ge(started, n_ + 1)
                    nc.vector.scalar_tensor_tensor(work[qt], relu[:, n_ % 4, 0:w], m.wi[:, qt * NH + h:qt * NH + h + 1], work[qt],
                                                   ALU.mult, ALU.add).then_inc(started, 1)

            @block.tensor
            def _(pe):
                for n_, (h, qt) in enumerate(order):
                    w, r0 = P * (qt + 1), 64 * (h % 2)
                    if n_ >= 4:
                        pe.wait_ge(rectified, n_ - 3)
                    nc.tensor.matmul(m.ps[:, n_ % 4, 0:w], m.raw[r0:r0 + 64, 4 + h // 2, qt * P:(qt + 1) * P],
                                     m.raw[r0:r0 + 64, 9, 0:w], start=True, stop=True).then_inc(scored, 1)
                pe.wait_ge(logf_done, 1)
                for t in range(TT):
                    mm = nc.tensor.matmul(m.ps[0:NH, 4, t * P:T], m.logf[:, t * NH:(t + 1) * NH], m.tri[:, 0:T - t * P],
                                          start=(t == 0), stop=(t == TT - 1))
                mm.then_inc(summed, 1)


TAKEN = -3e38


def select_topk(m, dve, top8, replaced, marked):
    nc = m.nc
    best = m.small[:, 0:24]
    dve.sem_inc(replaced, 3)
    with dve.Fori(0, TOPK // 8) as r:
        dve.wait_ge(replaced, r * 3 + 3)
        hold(dve, m)
        for qt in range(1, TT):
            nc.vector.max(best[:, 8 * (qt - 1):8 * qt], m.work[qt]).then_inc(top8, 1)
        dve.wait_ge(top8, r * 3 + 3)
        hold(dve, m)
        for qt in range(1, TT):
            nc.vector.match_replace(m.work[qt], best[:, 8 * (qt - 1):8 * qt], m.work[qt], TAKEN).then_inc(replaced, 1)
    dve.wait_ge(replaced, 3 * (TOPK // 8) + 3)
    nc.vector.tensor_copy(m.select_bf[0], m.con("chunkmask", P)).then_inc(marked, 1)
    for qt in range(1, TT):
        nc.vector.tensor_scalar(m.select_bf[qt], m.work[qt], TAKEN / 2, NEG, ALU.is_ge, ALU.mult).then_inc(marked, 1)


def forget_values_stage(m):
    nc = m.nc
    base = C2["fox"] + 8
    with stage(m, "chunk_done") as (chunk_done,):
        with nc.Block() as block:
            @block.sync
            def _(sp):
                load_ahead_loop(sp, m, base, chunk_done, 1, 4)

            @block.tensor
            def _(pe):
                for c in range(4):
                    wait_chunk(pe, m, base + c)
                    for k in range(2):
                        for t in range(TT):
                            mm = nc.tensor.matmul(m.ps[:, t, :], m.h[:, 2 * c + k, t * P:(t + 1) * P],
                                                  slab(m, base + c)[:, k * T:(k + 1) * T], start=(c + k == 0), stop=(c == 3 and k == 1))
                    mm.then_inc(chunk_done, 1)

            @block.scalar
            def _(act):
                act.wait_ge(chunk_done, 4)
                for t in range(TT):
                    nc.scalar.activation(m.v_fox[:, t, :], m.ps[:, t, :], ACT.Copy)


def gated_up_stage(m):
    nc = m.nc
    base = C2["ff_up"]
    W = T + 2
    u = m.scratch[:, 0:4 * W].rearrange("p (s t) -> p s t", s=4)
    acc = m.scratch[:, 4 * W:4 * W + 4 * T].rearrange("p (s t) -> p s t", s=4)
    sig = m.scratch[:, 4 * W + 4 * T:4 * W + 6 * T].rearrange("p (s t) -> p s t", s=2)
    cw = m.param("conv_w", 132)
    cb = m.param("conv_b", 44)
    with stage(m, "chunk_done zeroed copied tap1 tap2 tap3 sig_done half_done pair_done") as (
            chunk_done, zeroed, copied, tap1, tap2, tap3, sig_done, half_done, pair_done):
        with nc.Block() as block:
            @block.sync
            def _(sp):
                load_ahead_loop(sp, m, base, chunk_done, 11, 4)

            @block.tensor
            def _(pe):
                with pe.Fori(0, 11) as i:
                    for s in range(4):
                        pe.wait_ge(copied, i * 4 + s + 1)
                        wait_chunk(pe, m, base + s, i, 4)
                        for k in range(KD):
                            mm = nc.tensor.matmul(m.ps[:, s, :], slab(m, base + s)[:, k * P:(k + 1) * P], m.h[:, k, :],
                                                  start=(k == 0), stop=(k == KD - 1))
                        mm.then_inc(chunk_done, 1)

            @block.scalar
            def _(act):
                act.sem_inc(copied, 4)
                act.wait_ge(zeroed, 1)
                with act.Fori(0, 11) as i:
                    for s in range(4):
                        act.wait_ge(chunk_done, i * 4 + s + 1)
                        act.wait_ge(tap3, i * 4 + s + 1)
                        nc.scalar.activation(u[:, s, 2:W], m.ps[:, s, :], ACT.Copy).then_inc(copied, 1)
                        if s % 2:
                            act.wait_ge(tap3, i * 4 + s + 4)
                            nc.scalar.activation(sig[:, s // 2, :], acc[:, s - 1, :], ACT.Sigmoid).then_inc(sig_done, 1)

            @block.vector
            def _(dve):
                dve.sem_inc(tap3, 4)
                nc.vector.memset(u[:, :, 0:2], 0.0).then_inc(zeroed, 1)
                with dve.Fori(0, 11) as i:
                    for p in range(2):
                        for s in (2 * p, 2 * p + 1):
                            f = i * 2 + (p + NF2 * (s % 2))
                            dve.wait_ge(copied, i * 4 + s + 5)
                            nc.vector.tensor_scalar(acc[:, s, :], u[:, s, 2:W], cw[:, bass.ds(f + 88, 1)], cb[:, bass.ds(f, 1)],
                                                    ALU.mult, ALU.add).then_inc(tap1, 1)
                        for s in (2 * p, 2 * p + 1):
                            f = i * 2 + (p + NF2 * (s % 2))
                            dve.wait_ge(tap1, i * 4 + s + 1)
                            nc.vector.scalar_tensor_tensor(acc[:, s, :], u[:, s, 1:W - 1], cw[:, bass.ds(f + 44, 1)], acc[:, s, :],
                                                           ALU.mult, ALU.add).then_inc(tap2, 1)
                        for s in (2 * p, 2 * p + 1):
                            f = i * 2 + (p + NF2 * (s % 2))
                            dve.wait_ge(tap2, i * 4 + s + 1)
                            nc.vector.scalar_tensor_tensor(acc[:, s, :], u[:, s, 0:T], cw[:, bass.ds(f, 1)], acc[:, s, :],
                                                           ALU.mult, ALU.add).then_inc(tap3, 1)
                        out = m.hidden[:, bass.ds(i * 2 + p, 1), :].rearrange("p o t -> p (o t)")
                        dve.wait_ge(tap3, i * 4 + 2 * p + 6)
                        nc.vector.tensor_tensor(out, acc[:, 2 * p, :], acc[:, 2 * p + 1, :], ALU.mult).then_inc(half_done, 1)
                        dve.wait_ge(sig_done, i * 2 + p + 1)
                        dve.wait_ge(half_done, i * 2 + p + 1)
                        nc.vector.tensor_tensor(out, out, sig[:, p, :], ALU.mult).then_inc(pair_done, 1)


def second_layer(m, par):
    nc = m.nc
    params_stage(m, par)
    modulation_stage(m)
    K8 = [list(range(KD))]
    X, H = (lambda k: m.x[:, k, :]), (lambda k: m.h[:, k, :])
    raw = lambda n: m.raw[:, n, :]
    mod = lambda part: lambda k: m.mod[:, 8 * part + k:8 * part + k + 1]
    gain = lambda a: lambda k: m.gains[:, 8 * a + k:8 * a + k + 1]

    def gated_add(part):
        return lambda e, bank, n: nc.vector.scalar_tensor_tensor(m.x[:, n, :], bank, m.mod[:, bass.ds(n + 8 * part, 1)], m.x[:, n, :],
                                                                 ALU.mult, ALU.add)

    norm_stage(m, X, KD, H, gain(0), D, shift=mod(0))
    linear_stage(m, C2["raw"], 1, [K8] * 8, H,
                 [("act", lambda e, bank, n: nc.scalar.activation(raw(n), bank, ACT.Copy, scale=float(DH) ** -0.5 if n < 4 else 1.0)),
                  ("dve", lambda e, bank, n: (nc.vector.tensor_scalar(raw(n), bank, float(DH) ** -0.5, None, ALU.mult) if n < 4
                                              else nc.vector.tensor_copy(raw(n), bank)))] * 4)
    misc2_stage(m)
    rotate_stage(m, [(raw, 10, P, T, None, None, DH, None, m.con("cos_n", T), m.con("sin_n", T), SWAP16)])
    index_stage(m)

    def split_heads(n):
        dst = m.qf if n < 4 else m.kf

        def emit(eng, bank, _):
            for half in range(2):
                r = nc.scalar.activation(dst[0:DH, 2 * (n % 4) + half, :], bank[64 * half:64 * half + 64, :], ACT.Copy,
                                         scale=float(DH) ** -0.5 if n < 4 else 1.0)
            return r
        return ("act", emit)

    linear_stage(m, C2["fox"], 1, [K8] * 8, H, [split_heads(n) for n in range(8)])
    forget_values_stage(m)
    linear_stage(m, C2["gate"], 4, [K8] * 4, H,
                 [("act", lambda e, bank, n: nc.scalar.activation(m.gates2[:, n, :], bank, ACT.Sigmoid))] * 4,
                 extra="top8 replaced marked", dve_side=lambda dve, *s: select_topk(m, dve, *s))
    attention_stage(m, 2, 1, lambda i, j: (m.raw[64 * (j % 2):64 * (j % 2) + 64, i * 2 + j // 2, :], m.qstage(j)[0:64, :]),
                    lambda i, j, b: raw(8), P,
                    lambda i, j, b: m.va.rearrange("p (t d) -> p t d", t=TT),
                    lambda b, qt: (m.select_bf[qt], 0), lambda i, j, b: None, lambda i, p: m.o_mla[:, i * 2 + p, :],
                    zero=[m.qstage(j)[64:128, :] for j in range(4)])
    attention_stage(m, 2, 1, lambda i, j: (m.qf[0:97, i * 4 + j, :], m.qstage(j)[0:97, :]),
                    lambda i, j, b: m.kf[0:97, i * 4 + j, :], 97,
                    lambda i, j, b: m.v_fox[:, :, bass.ds(i * (4 * DH) + j * DH, DH)],
                    lambda b, qt: (m.causal_bf, qt * P), lambda i, j, b: None, lambda i, p: m.o_nsa[:, i * 2 + p, :])
    merge_stage(m, C2["merge"], 2, [(n, b, n, 4 * b, b == 1) for n in range(KD) for b in range(2)], 8,
                lambda b, k: (m.o_mla, m.o_nsa)[b][:, k, :], lambda b, n: m.gates2[:, 8 * b + n, :], None)
    linear_stage(m, C2["wout"], 2, [K8] * 4, raw, [("dve", gated_add(2))] * 4)
    norm_stage(m, X, KD, H, gain(1), D, shift=mod(3))
    gated_up_stage(m)
    linear_stage(m, C2["ff_down"], 2, [[list(range(0, 8)), list(range(8, 16)), list(range(16, NF2))]] * 4,
                 lambda k: m.hidden[:, k, :], [("dve", gated_add(5))] * 4)


def second_stack(m, par, tri, vecs, pos, view, tiles):
    m.param = lambda name, w: view("par", PAR2[name], w)
    m.per_layer, m.stream_base = NC2, BASE2
    m.tri = m.con("cos_m", T)
    vs = view("vs", 0, 4 * 256).rearrange("p (u t d) -> p u t d", u=4, t=TT)
    m.vstage = lambda j, b: vs[:, j, :, :]
    m.va = view("vs", 4 * 256, 256)
    m.mod, m.gains = view("small", 64, 48), view("small", 112, 16)
    m.wi, m.logf = view("small", 128, 32), view("small", 160, 32)
    m.qf, m.kf = tiles("raw", 10 * T, 8), tiles("raw", 18 * T, 8)
    m.gates2 = tiles("raw", 26 * T, 16)
    m.v_fox = tiles("raw", 4 * T, TT)
    m.work = {1: view("o", 0, 256), 2: view("o", T, 384), 3: view("o", 2 * T, 512)}
    bits = view("extra", 0, 640).bitcast(BF16)
    m.select_bf = {0: bits[:, 0:128], 1: bits[:, 128:384], 2: bits[:, 384:768], 3: bits[:, 768:1280]}
    position_stage(m, tri, vecs, pos)
    with m.nc.Fori(0, DEPTH) as layer:
        m.layer = layer
        second_layer(m, par)
    norm_stage(m, lambda k: m.x[:, k, :], KD, lambda k: m.h[:, k, :], lambda k: m.con("final_g", 8)[:, k:k + 1], D)


def build(nc, wstream, par1, par2, con, causal, tri, vecs, pos, xT, outT, upto=None):
    with ExitStack() as ctx:
        arena = ctx.enter_context(nc.sbuf_tensor("arena", [P, NARENA], F32))
        ps = ctx.enter_context(nc.psum_tensor("ps", [P, 8, T], F32))
        landed = [ctx.enter_context(nc.semaphore(f"weights_landed{s}")) for s in range(RING)]
        loaded = ctx.enter_context(nc.semaphore("inputs_loaded"))
        cast = ctx.enter_context(nc.semaphore("masks_cast"))
        passed = ctx.enter_context(nc.semaphore("waits_passed"))
        stored = ctx.enter_context(nc.semaphore("output_stored"))

        def view(name, off, w):
            return arena[:, AR[name] + off:AR[name] + off + w]

        def tiles(name, off, n, w=T):
            return view(name, off, n * w).rearrange("p (k t) -> p k t", t=w)

        m = Program()
        m.nc, m.wstream, m.landed, m.passed = nc, wstream, landed, passed
        m.ps = ps[:, :, :]
        m.ring = tiles("ring", 0, RING, CHUNK)
        m.x, m.h, m.raw, m.g = tiles("x", 0, KD), tiles("h", 0, KD), tiles("raw", 0, 21), tiles("g", 0, 24)
        m.hidden = tiles("raw", 0, 45)
        m.p, m.pt = view("p", 0, 8 * T), view("pt", 0, 1280)
        m.par = view("par", 0, NPAR)
        m.con = lambda name, w: view("con", CON[name], w)
        m.ident, m.ones, m.bd64 = m.con("ident", P), m.con("ones", P), m.con("bd64", P)
        m.eps = m.con("eps", 1)
        m.ident_bf = view("idb", 0, 64).bitcast(BF16)
        m.causal_bf = view("caub", 0, 64).bitcast(BF16)
        m.small = view("small", 0, 256)
        qs = tiles("qs", 0, 4)
        vs = view("vs", 0, 8 * 256).rearrange("p (u t d) -> p u t d", u=8, t=TT)
        m.qstage = lambda j: qs[:, j, :]

        m.scratch = view("p", 0, 8 * T + 1280)
        m.spare = view("qs", 0, T)
        m.param = lambda name, w: view("par", PAR1[name], w)
        m.q_mla, m.k_mla = tiles("g", 0, 8), tiles("g", 8 * T, 8)
        m.v_mla, m.v_nsa = tiles("g", 16 * T, TT), tiles("g", 20 * T, TT, 256)
        m.kc2 = tiles("g", 22 * T, 2)
        m.o_mla, m.o_nsa = tiles("o", 0, 4), tiles("o", 4 * T, 4)
        m.gn, m.gcmp = view("small", 64, 96), view("small", 160, 32)
        m.hid, m.hsig = tiles("extra", 0, 2, 62), tiles("extra", 124, 2, 62)
        m.kcmp, m.vcmp = view("extra", 248, 62), tiles("extra", 310, 2, 64)
        m.krope = view("o", 0, T)

        with nc.Block() as block:
            @block.sync
            def _(sp):
                for c in range(RING):
                    sp.dma_start(m.ring[:, c, :], wstream[c]).then_inc(landed[c], 16)
                sp.dma_start(m.x, xT.rearrange("(k p) t -> p k t", p=P)).then_inc(loaded, 16)
                sp.dma_start(view("con", 0, NCON), con).then_inc(loaded, 16)
                sp.dma_start(m.pt[:, 0:P], causal).then_inc(loaded, 16)

            @block.vector
            def _(dve):
                dve.wait_ge(loaded, 48)
                nc.vector.tensor_copy(m.ident_bf, m.ident).then_inc(cast, 1)
                nc.vector.tensor_copy(m.causal_bf, m.pt[:, 0:P]).then_inc(cast, 1)
                dve.wait_ge(cast, 2)

        m.per_layer, m.stream_base = NC1, 0
        m.vstage = lambda j, b: vs[:, 2 * j + b, :, :]
        with nc.Fori(0, DEPTH) as layer:
            m.layer = layer
            first_layer(m, par1)
        if upto != "first":
            second_stack(m, par2, tri, vecs, pos, view, tiles)
        with nc.Block() as block:
            @block.sync
            def _(sp):
                res = m.x if upto == "first" else m.h
                sp.dma_start(outT.rearrange("(k p) t -> p k t", p=P), res).then_inc(stored, 16)
                sp.wait_ge(stored, 16)
                for s in range(RING):
                    if upto != "first":
                        sp.wait_ge(landed[s], 16 * (NCHUNKS // RING + 1))


def constants():
    f = np.float32
    c = np.zeros((P, NCON), f)

    def put(name, a):
        a = np.asarray(a, f)
        c[:a.shape[0], CON[name]:CON[name] + a.shape[1]] = a

    put("ident", np.eye(P))
    put("ones", np.ones((P, P)))
    put("bd64", np.kron(np.eye(2), np.ones((64, 64))))
    s = np.arange(P)[:, None]
    put("chunkmask", np.where(np.arange(P)[None, :] // 64 <= s // 64, 0.0, NEG))

    def table(rot, pos):
        half = rot // 2
        inv = np.power(f(500000.0), -np.arange(half, dtype=f) * f(2.0 / rot)).astype(f)
        ang = (pos.astype(f)[:, None] * inv).astype(f)
        return np.cos(ang).T, np.sin(ang).T

    def rows(head, at, rot, pos):
        co, si = np.ones((head, len(pos)), f), np.zeros((head, len(pos)), f)
        a, b = table(rot, pos)
        h = rot // 2
        co[at:at + h], co[at + h:at + rot] = a, a
        si[at:at + h], si[at + h:at + rot] = -b, b
        return co, si

    co, si = rows(MQK, MNOPE, MROPE, np.arange(T))
    put("cos_m", co)
    put("sin_m", si)
    co, si = rows(DH, 0, 16, np.arange(T))
    put("cos_n", np.tile(co, (2, 1)))
    put("sin_n", np.tile(si, (2, 1)))
    cpos = np.arange(NCMP) * CSTRIDE + CBLOCK - 1
    co, si = rows(DH, 0, 16, cpos)
    put("cos_c", np.tile(co, (1, 2)))
    put("sin_c", np.tile(si, (1, 2)))
    q = np.arange(TT)[None, :, None] * P + np.arange(P)[:, None, None]
    put("mask_c", np.where(cpos[None, None, :] <= q, 0.0, NEG).reshape(P, -1))
    put("rowok", (q[:, :, 0] >= CBLOCK - 1))
    r = np.arange(P) % 64
    inv = np.power(f(500000.0), -np.arange(0, 16, 2, dtype=f) / f(16)).astype(f)
    put("invf", np.where(r < 16, inv[r % 8], 0.0)[:, None])
    put("sgn", np.where(r < 8, -1.0, np.where(r < 16, 1.0, 0.0))[:, None])
    put("rotm", (r < 16)[:, None])
    put("unrot", (r >= 16)[:, None])
    put("eps", np.full((P, 1), EPS))
    put("eps_mla", np.full((P, 1), MQK * EPS))
    put("eps_nsa", np.full((P, 1), DH * EPS))
    return c


def causal_bias():
    return np.where(np.arange(P)[None, :] <= np.arange(P)[:, None], 0.0, NEG).astype(np.float32)


def col_tiles(w, n0, count, kt=KD):
    k = w.shape[0]
    a = w[:, n0:n0 + count * P].reshape(k // P, P, count, P).transpose(2, 1, 0, 3)
    return a.reshape(count, P, (k // P) * P)


def put_chunks(stream, at, a):
    stream[at:at + a.shape[0], :, 0:a.shape[2]] = a


def by_rows(w, c0, width):
    k = w.shape[0]
    return w[:, c0:c0 + width].reshape(k // P, P, width).transpose(1, 0, 2)


def pack_first(stream, at, i, l):
    w = i["w_in"][l]
    o = np.cumsum([0, QRANK, KVRANK, MROPE, 2 * CONV_CH, 512, 768, 24])
    cq, ckv, kr, u2, qn, kvn, gn, gm = o
    b = at + C1["raw"]
    put_chunks(stream, b, col_tiles(w, cq, 3))
    put_chunks(stream, b + 3, col_tiles(w, ckv, 2))
    for c in range(CCH):
        put_chunks(stream, b + 5 + 2 * c, col_tiles(w, u2 + c * P, 1))
        put_chunks(stream, b + 6 + 2 * c, col_tiles(w, u2 + CONV_CH + c * P, 1))
    put_chunks(stream, b + 13, col_tiles(w, qn, 4))
    put_chunks(stream, b + 17, col_tiles(w, kvn + 256, 1))
    put_chunks(stream, b + 18, col_tiles(w, kvn + 512, 1))
    put_chunks(stream, b + 19, col_tiles(w, kvn, 1))
    b = at + C1["misc"]
    put_chunks(stream, b, col_tiles(w, kvn + 128, 1))
    s = stream[b + 1].reshape(P, 8, P)
    s[:, :, 0:32] = by_rows(w, kr, 32)
    s[:, :, 32:56] = by_rows(w, gn, 24)
    vv = np.concatenate([by_rows(w, kvn + 384, 128), by_rows(w, kvn + 640, 128)], axis=2)
    stream[b + 2] = vv[:, 0:4].reshape(P, -1)
    stream[b + 3] = vv[:, 4:8].reshape(P, -1)
    b = at + C1["mla"]
    uq = i["w_uq"][l].reshape(QRANK, NH, MQK)
    uq = np.concatenate([uq[:, :, MROPE:], uq[:, :, :MROPE]], axis=2)
    for h in range(NH):
        s = stream[b + h // 2].reshape(P, 8, P)
        s[:, (h % 2) * 3:(h % 2) * 3 + 3, 0:MQK] = uq[:, h].reshape(3, P, MQK).transpose(1, 0, 2)
    ukv = i["w_ukv"][l].reshape(KVRANK, NH, 128)
    nope = np.ascontiguousarray(ukv[:, :, :64]).reshape(2, P, 4, P)
    stream[b + 4] = nope.transpose(1, 2, 0, 3).reshape(P, -1)
    v = np.ascontiguousarray(ukv[:, :, 64:]).reshape(2, P, T)
    stream[b + 5] = v.transpose(1, 0, 2).reshape(P, -1)
    b = at + C1["cmp"]
    for n_, name in enumerate(("w_cmp_k", "w_cmp_v")):
        a = i[name + "1"][l].reshape(2, 8, P, P).transpose(0, 2, 1, 3).reshape(2, P, -1)
        stream[b + 2 * n_:b + 2 * n_ + 2] = a
        stream[b + 4 + n_, :, 0:64] = i[name + "2"][l]
    put_chunks(stream, at + C1["gate"], col_tiles(w, gm, 24))
    b = at + C1["merge"]
    for n_, name in enumerate(("w_o_mla", "w_conv_out", "w_o_nsa")):
        a = i[name][l].reshape(4, P, 4, 2, P).transpose(2, 1, 3, 0, 4).reshape(4, P, -1)
        for p in range(4):
            stream[b + 3 * p + n_] = a[p]
    put_chunks(stream, at + C1["wout"], col_tiles(i["w_out"][l], 0, 8))
    put_chunks(stream, at + C1["ff_up"], col_tiles(i["w_ff1"][l], 0, 32))
    a = i["w_ff2"][l].reshape(4, 8, P, 8, P).transpose(3, 0, 2, 1, 4).reshape(32, P, -1)
    stream[at + C1["ff_down"]:at + C1["ff_down"] + 32] = a


def pack_par1(i, l):
    c = np.zeros((P, NPAR), np.float32)

    def put(name, a):
        a = a.reshape(a.shape[0], -1)
        c[:a.shape[0], PAR1[name]:PAR1[name] + a.shape[1]] = a

    vec = lambda a: a.reshape(-1, P).T
    turned = lambda a: np.concatenate([a[MROPE:], a[:MROPE]])[:, None]
    for name, key in (("g_mix", "g_mix"), ("g_ffn", "g_ffn"), ("g_cq", "g_cq"), ("g_ckv", "g_ckv"), ("b_glu", "b_glu"),
                      ("b_dw", "b_dw"), ("g_ln", "g_conv_ln"), ("b_ln", "b_conv_ln"), ("b_out", "b_conv_out")):
        put(name, vec(i[key][l]))
    put("gq_mla", turned(i["g_q_mla"][l]))
    put("gk_mla", turned(i["g_k_mla"][l]))
    put("gq_nsa", np.concatenate([i["g_q_nsa"][l]] * 2)[:, None])
    put("gk_nsa", np.concatenate([i["g_k_nsa"][l]] * 2)[:, None])
    put("w_dw", i["w_dw"][l].reshape(TAPS, CCH, P).transpose(2, 1, 0))
    for n_, name in (("pe_k", "pe_cmp_k"), ("pe_v", "pe_cmp_v")):
        put(n_, i[name][l].reshape(16, P).T)
    return c


def pack_second(stream, at, i, l):
    w = i["w_in_2"][l]
    qa, ka, va, qi, ki, wi, qf, kf, vf, ff, gates = np.cumsum([0, 512, 64, 64, 512, 64, 8, 512, 512, 512, 8])
    put_chunks(stream, at + C2["mod"], col_tiles(i["mod_w_2"][l], 0, 48))
    b = at + C2["raw"]
    put_chunks(stream, b, col_tiles(w, qa, 4))
    put_chunks(stream, b + 4, col_tiles(w, qi, 4))
    b = at + C2["misc"]
    s = stream[b].reshape(P, 8, P)
    s[:, :, 0:64], s[:, :, 64:128] = by_rows(w, ka, 64), by_rows(w, ki, 64)
    for n_, (c, width) in enumerate(((ff, 8), (va, 64), (wi, 8))):
        stream[b + 1 + n_].reshape(P, 8, P)[:, :, 0:width] = by_rows(w, c, width)
    b = at + C2["fox"]
    put_chunks(stream, b, col_tiles(w, qf, 4))
    put_chunks(stream, b + 4, col_tiles(w, kf, 4))
    v = by_rows(w, vf, 512)
    for c in range(4):
        stream[b + 8 + c] = v[:, 2 * c:2 * c + 2].reshape(P, -1)
    put_chunks(stream, at + C2["gate"], col_tiles(w, gates, 16))
    a = np.concatenate([col_tiles(i["w_branch_a_2"][l], 0, 8), col_tiles(i["w_branch_b_2"][l], 0, 8)], axis=2)
    put_chunks(stream, at + C2["merge"], a)
    put_chunks(stream, at + C2["wout"], col_tiles(i["w_out_2"][l], 0, 8))
    a = col_tiles(i["w_up_2"][l], 0, 44)
    put_chunks(stream, at + C2["ff_up"], a.reshape(2, NF2, P, -1).transpose(1, 0, 2, 3).reshape(44, P, -1))
    a = i["w_down_2"][l].reshape(NF2, P, 8, P).transpose(2, 1, 0, 3)
    for n_ in range(8):
        for c in range(3):
            part = a[n_, :, 8 * c:8 * c + 8]
            stream[at + C2["ff_down"] + 3 * n_ + c, :, 0:part.shape[1] * P] = part.reshape(P, -1)


def pack_par2(i, l):
    c = np.zeros((P, NPAR), np.float32)

    def put(name, a):
        a = a.reshape(a.shape[0], -1)
        c[:, PAR2[name]:PAR2[name] + a.shape[1]] = a

    vec = lambda a: a.reshape(-1, P).T
    put("mod_b", vec(i["mod_b_2"][l]))
    put("g1", vec(i["norm1_g_2"][l]))
    put("g2", vec(i["norm2_g_2"][l]))
    put("fbias", np.tile(i["forget_bias_2"][l][None, :], (P, TT)))
    put("conv_w", i["conv_w_2"][l].reshape(3, 44, P).transpose(2, 0, 1))
    put("conv_b", vec(i["conv_b_2"][l]))
    return c


def triangle():
    return (np.arange(T)[None, :] >= np.arange(P)[:, None]).astype(np.float32)


def host_arrays(i):
    stream = np.zeros((NCHUNKS + RING, P, CHUNK), np.float32)
    for l in range(DEPTH):
        pack_first(stream, l * NC1, i, l)
        pack_second(stream, BASE2 + l * NC2, i, l)
    vecs = np.concatenate([i["final_g_2"].reshape(KD, P).T, i["c_2"].reshape(KD, P).T], axis=1)
    return {"wstream": stream,
            "par1": np.stack([pack_par1(i, l) for l in range(DEPTH)]),
            "par2": np.stack([pack_par2(i, l) for l in range(DEPTH)]),
            "con": constants(), "causal": causal_bias(), "tri": triangle(), "vecs": np.ascontiguousarray(vecs),
            "pos": np.ascontiguousarray(i["positions_2"].reshape(1, T)), "xT": np.ascontiguousarray(i["x"][0].T)}


def kernel(**inputs):
    import concourse.bacc as bacc
    from concourse.bass_utils import run_bass_kernel_spmd

    i = {name: np.asarray(a) for name, a in inputs.items()}
    arrays = host_arrays(i)
    nc = bacc.Bacc("TRN2", target_bir_lowering=False, num_devices=1)
    args = [nc.dram_tensor(n_, a.shape, mybir.dt.from_np(a.dtype), kind="ExternalInput").ap() for n_, a in arrays.items()]
    out = nc.dram_tensor("outT", (D, T), F32, kind="ExternalOutput").ap()
    build(nc, *args, out)
    r = run_bass_kernel_spmd(nc, [arrays], core_ids=[0])
    return np.ascontiguousarray(np.asarray(r.results[0]["outT"]).T).reshape(1, T, D)
```

```python
from contextlib import ExitStack, contextmanager

import numpy as np
import concourse.bass as bass
from concourse import mybir

F32 = mybir.dt.float32
F32R = mybir.dt.float32r
BF16 = mybir.dt.bfloat16
I32 = mybir.dt.int32
ALU = mybir.AluOpType
ACT = mybir.ActivationFunctionType
AX = mybir.AxisListType.X

P = 128
T = 512
TT = T // P
D = 1024
KD = D // P
DEPTH = 2
EPS = 1e-6
NEG = -1e30

NH, DH = 8, 64
MQK, MNOPE, MROPE = 96, 64, 32
QRANK, KVRANK = 384, 256
CONV_CH, TAPS = 512, 31
CCH = CONV_CH // P
NCMP, CSTRIDE, CBLOCK = 31, 16, 32
FF1 = 4096
TOPK = 128
FF2 = 2816
NF2 = FF2 // P

RING = 4
CHUNK = 8 * P
C1 = {}
n = 0
for name, count in (("raw", 12), ("misc", 4), ("cmp", 6), ("mla", 6), ("glu", 8), ("gate", 24), ("merge", 12),
                    ("wout", 8), ("ff_up", 32), ("ff_down", 32)):
    C1[name] = n
    n += count
NC1 = n
C2 = {}
n = 0
for name, count in (("mod", 16), ("raw", 8), ("misc", 2), ("fox", 12), ("gate", 16), ("merge", 8),
                    ("wout", 8), ("ff_up", 44), ("ff_down", 22)):
    C2[name] = n
    n += count
NC2 = n
BASE2 = DEPTH * NC1
NCHUNKS = DEPTH * (NC1 + NC2)
assert NC1 % RING == 0 and NC2 % RING == 0

def columns(spec):
    at, off = {}, 0
    for name, w in spec:
        at[name] = off
        off += w
    return at, off


PAR1, NPAR1 = columns((("g_mix", 8), ("g_ffn", 8), ("g_cq", 3), ("g_ckv", 2), ("gq_mla", 1), ("gk_mla", 1),
                       ("gq_nsa", 1), ("gk_nsa", 1), ("b_glu", 8), ("w_dw", CCH * TAPS), ("b_dw", 4),
                       ("g_ln", 4), ("b_ln", 4), ("b_out", 8), ("pe_k", 16), ("pe_v", 16)))
PAR2, NPAR2 = columns((("mod_b", 48), ("g1", 8), ("g2", 8), ("fbias", 32), ("conv_w", 3 * 44), ("conv_b", 44)))
NPAR = max(NPAR1, NPAR2)

CON, NCON = columns((("ident", 128), ("ones", 128), ("bd64", 128), ("chunkmask", 128),
                     ("cos_m", 512), ("sin_m", 512), ("cos_n", 512), ("sin_n", 512),
                     ("cos_c", 62), ("sin_c", 62), ("mask_c", 124), ("rowok", 4), ("invf", 1), ("sgn", 1), ("rotm", 1),
                     ("unrot", 1), ("eps", 1), ("eps_mla", 1), ("eps_nsa", 1), ("final_g", 8), ("cvec", 8)))

AR = {}
n = 0
for name, w in (("ring", RING * CHUNK), ("x", KD * T), ("p", 8 * T), ("pt", 1280), ("qs", 4 * T), ("vs", 8 * 256),
                ("body", 28 * T), ("o", 8 * T), ("par", NPAR), ("con", NCON), ("idb", 64), ("caub", 64),
                ("extra", 640), ("small", 256)):
    AR[name] = n
    n += w
NARENA = n

SWAP32 = [(i + 16) % 32 for i in range(32)]
SWAP16 = [(i + 8) % 16 if i < 16 else i for i in range(32)]


class Program:
    pass


@contextmanager
def stage(m, names):
    nc = m.nc
    with ExitStack() as ctx:
        sems = [ctx.enter_context(nc.semaphore(s)) for s in names.split()]
        yield sems
        with nc.Block() as block:
            @block.gpsimd
            def _(pool):
                for s in sems:
                    pool.sem_clear(s)


@contextmanager
def loop(eng, count):
    if count == 1:
        yield 0
    else:
        with eng.Fori(0, count) as i:
            yield i


def chunk_flat(m, c):
    return m.layer * m.per_layer + (m.stream_base + c)


def hold(eng, m):
    eng.sem_inc(m.passed, 1)


def use_log_exp(m):
    m.nc.scalar.preload_act_table_set("natural_log_exp_and_others")


def wait_chunk(pe, m, c, i=0, body=0):
    rounds = (m.stream_base + c) // RING + 1
    pe.wait_ge(m.landed[c % RING], m.layer * (16 * m.per_layer // RING) + i * (16 * body // RING) + 16 * rounds)


def slab(m, c):
    return m.ring[:, c % RING, :]


def load_ahead(sp, m, c, done, j):
    sp.wait_ge(done, j)
    sp.dma_start(slab(m, c), m.wstream[chunk_flat(m, c) + RING]).then_inc(m.landed[c % RING], 16)


def load_ahead_loop(sp, m, base, done, iters, body, start=0, beside=None):
    with loop(sp, iters) as i:
        for j in range(body):
            if beside:
                beside(i, j)
            sp.wait_ge(done, i * body + j + 1 + start)
            sp.dma_start(slab(m, base + j), m.wstream[m.layer * m.per_layer + i * body + (m.stream_base + base + j + RING)])\
                .then_inc(m.landed[(base + j) % RING], 16)



def weights_hi(act, m, base, i, j, body, chunk_done, hi_ready):
    wait_chunk(act, m, base + j, i, body)
    if j:
        act.wait_ge(chunk_done, i * body + j)
    m.nc.scalar.activation(m.w_hi[:, j % 2, :], slab(m, base + j), ACT.Copy).then_inc(hi_ready, 1)


def weights_lo(pool, m, base, i, j, body, hi_ready, lo_ready):
    pool.wait_ge(hi_ready, i * body + j + 1)
    m.nc.gpsimd.tensor_tensor(m.w_lo[:, j % 2, :], slab(m, base + j), m.w_hi[:, j % 2, :].bitcast(F32), ALU.subtract)\
        .then_inc(lo_ready, 1)


def weights_lo_loop(pool, m, base, hi_ready, lo_ready, iters, body):
    with loop(pool, iters) as i:
        for j in range(body):
            weights_lo(pool, m, base, i, j, body, hi_ready, lo_ready)


def split_hi(m, k, tile):
    return m.nc.scalar.activation(m.a_hi[:, k, :], tile, ACT.Copy)


def split_lo(m, k, tile):
    return m.nc.vector.tensor_tensor(m.a_lo[:, k, :], tile, m.a_hi[:, k, :].bitcast(F32), ALU.subtract)


def split_source_hi(act, m, source, make, made, src_hi):
    for k in range(KD):
        if make:
            act.wait_ge(made, make[1] * (k + 1))
        split_hi(m, k, source(k)).then_inc(src_hi, 1)


def split_source_lo(dve, m, source, make, made, src_hi, src_lo):
    for k in range(KD + 1):
        if make and k < KD:
            make[0](dve, k, made).then_inc(made, 1)
        if k:
            dve.wait_ge(src_hi, k)
            split_lo(m, k - 1, source(k - 1)).then_inc(src_lo, 1)


def unit_tile(w, u):
    return w[:, u * P:(u + 1) * P]


def split_products(pe, m, base, i, j, body, bank, hi_ready, lo_ready, fresh=None):
    w_hi, w_lo = m.w_hi[:, j % 2, :], m.w_lo[:, j % 2, :]
    pe.wait_ge(hi_ready, i * body + j + 1)
    for k in range(KD):
        if fresh:
            pe.wait_ge(fresh[0], k + 1)
        m.nc.tensor.matmul(bank, unit_tile(w_hi, k), m.a_hi[:, k, :], start=(k == 0), stop=False)
    for k in range(KD):
        if fresh:
            pe.wait_ge(fresh[1], k + 1)
        m.nc.tensor.matmul(bank, unit_tile(w_hi, k), m.a_lo[:, k, :], start=False, stop=False)
    pe.wait_ge(lo_ready, i * body + j + 1)
    for k in range(KD):
        mm = m.nc.tensor.matmul(bank, unit_tile(w_lo, k), m.a_hi[:, k, :], start=False, stop=(k == KD - 1))
    return mm


def linear_stage(m, base, iters, body, evac, source=None, make=None, post=None, extra="", dve_side=None,
                 sync_side=None, pe_last=None, dve_last=None):
    assert body % RING == 0
    with stage(m, "chunk_done hi_ready lo_ready made src_hi src_lo act_evac dve_evac " + extra) as (
            chunk_done, hi_ready, lo_ready, made, src_hi, src_lo, act_evac, dve_evac, *side):
        counters = {"act": act_evac, "dve": dve_evac}
        mine = {e: [g for g in range(body) if evac[g][0] == e] for e in ("act", "dve")}
        with m.nc.Block() as block:
            @block.sync
            def _(sp):
                load_ahead_loop(sp, m, base, lo_ready, iters, body,
                                beside=sync_side and (lambda i, j: sync_side(sp, i, j, *side)))

            @block.gpsimd
            def _(pool):
                weights_lo_loop(pool, m, base, hi_ready, lo_ready, iters, body)

            @block.tensor
            def _(pe):
                pe.sem_inc(chunk_done, 1)
                with loop(pe, iters) as i:
                    for g in range(body):
                        who = evac[g][0]
                        pe.wait_ge(counters[who], i * len(mine[who]) + mine[who].index(g) + 1)
                        split_products(pe, m, base, i, g, body, m.ps[:, g, :], hi_ready, lo_ready,
                                       (src_hi, src_lo) if source and g == 0 else None).then_inc(chunk_done, 1)
                if pe_last:
                    pe_last(pe, *side)

            @block.scalar
            def _(act):
                weights_hi(act, m, base, 0, 0, body, chunk_done, hi_ready)
                if source:
                    split_source_hi(act, m, source, make, made, src_hi)
                if mine["act"]:
                    act.sem_inc(act_evac, len(mine["act"]))
                with loop(act, iters) as i:
                    for g in range(body):
                        weights_hi(act, m, base, i, g + 1, body, chunk_done, hi_ready)
                        if g in mine["act"]:
                            act.wait_ge(chunk_done, i * body + g + 2)
                            evac[g][1](act, m.ps[:, g, :], i * body + g, act_evac).then_inc(act_evac, 1)

            @block.vector
            def _(dve):
                if mine["dve"]:
                    dve.sem_inc(dve_evac, len(mine["dve"]))
                if source:
                    split_source_lo(dve, m, source, make, made, src_hi, src_lo)
                if dve_side:
                    dve_side(dve, *side)
                if post or mine["dve"]:
                    with loop(dve, iters) as i:
                        for g in range(body):
                            if g in mine["dve"]:
                                dve.wait_ge(chunk_done, i * body + g + 2)
                                evac[g][1](dve, m.ps[:, g, :], i * body + g, act_evac).then_inc(dve_evac, 1)
                            if post:
                                dve.wait_ge(act_evac, i * body + g + 1 + body)
                                post(dve, i * body + g)
                if dve_last:
                    dve_last(dve, *side)


def down_stage(m, base, blocks, update):
    nc = m.nc
    turns, rest = divmod(blocks, 2)
    hidden = lambda k: m.hidden[:, k, :]

    with stage(m, "chunk_done hi_ready lo_ready src_hi src_lo") as (chunk_done, hi_ready, lo_ready, src_hi, src_lo):
        with nc.Block() as block:
            @block.sync
            def _(sp):
                load_ahead_loop(sp, m, base, lo_ready, turns, 4)
                for j in range(2 * rest):
                    sp.wait_ge(lo_ready, turns * 4 + j + 1)
                    sp.dma_start(slab(m, base + j), m.wstream[chunk_flat(m, base + turns * 4 + j) + RING])\
                        .then_inc(m.landed[(base + j) % RING], 16)

            @block.gpsimd
            def _(pool):
                weights_lo_loop(pool, m, base, hi_ready, lo_ready, turns, 4)
                for j in range(2 * rest):
                    weights_lo(pool, m, base, turns, j, 4, hi_ready, lo_ready)

            def products(pe, i, h, first, last):
                for half in range(2):
                    j = 2 * h + half
                    pe.wait_ge(hi_ready, i * 4 + j + 1)
                    passes = ((m.w_hi, m.a_hi, src_hi), (m.w_hi, m.a_lo, src_lo), (m.w_lo, m.a_hi, None))
                    for p, (w, a, ready) in enumerate(passes):
                        if half == 0 and ready:
                            pe.wait_ge(ready, i * 4 + 2 * h + 2)
                        if p == 2:
                            pe.wait_ge(lo_ready, i * 4 + j + 1)
                        for n in range(4):
                            for k in range(2):
                                mm = nc.tensor.matmul(m.ps[:, 4 * half + n, :], unit_tile(w[:, j % 2, :], 2 * n + k),
                                                      a[:, 2 * h + k, :], start=(first and p == 0 and k == 0),
                                                      stop=(last and p == 2 and k == 1))
                    mm.then_inc(chunk_done, 1)

            @block.tensor
            def _(pe):
                pe.sem_inc(chunk_done, 1)
                products(pe, 0, 0, True, False)
                products(pe, 0, 1, False, False)
                with pe.Fori(1, turns - (1 - rest)) as i:
                    for h in range(2):
                        products(pe, i, h, False, False)
                if rest:
                    products(pe, turns, 0, False, True)
                else:
                    products(pe, turns - 1, 0, False, False)
                    products(pe, turns - 1, 1, False, True)

            @block.scalar
            def _(act):
                def cut(i, h):
                    for k in range(2):
                        split_hi(m, 2 * h + k, hidden(i * 4 + 2 * h + k)).then_inc(src_hi, 1)

                def block_(i, h, more):
                    weights_hi(act, m, base, i, 2 * h + 1, 4, chunk_done, hi_ready)
                    if more:
                        act.wait_ge(chunk_done, i * 4 + 2 * h + 1)
                        cut(*((i, 1) if h == 0 else (i + 1, 0)))
                        weights_hi(act, m, base, i, 2 * h + 2, 4, chunk_done, hi_ready)

                weights_hi(act, m, base, 0, 0, 4, chunk_done, hi_ready)
                cut(0, 0)
                with act.Fori(0, turns - (1 - rest)) as i:
                    block_(i, 0, True)
                    block_(i, 1, True)
                if rest:
                    block_(turns, 0, False)
                else:
                    block_(turns - 1, 0, True)
                    block_(turns - 1, 1, False)

            @block.vector
            def _(dve):
                def cut(i, h):
                    for k in range(2):
                        dve.wait_ge(src_hi, i * 4 + 2 * h + k + 1)
                        split_lo(m, 2 * h + k, hidden(i * 4 + 2 * h + k)).then_inc(src_lo, 1)

                with dve.Fori(0, turns) as i:
                    cut(i, 0)
                    cut(i, 1)
                if rest:
                    cut(turns, 0)
                for n in range(KD):
                    dve.wait_ge(chunk_done, 2 * blocks + n // 4)
                    update(n, m.ps[:, n, :])


def refined_rsqrt(m, dve, step, done, v, root, out, tmp):
    nc = m.nc
    nc.vector.reciprocal(out, root).then_inc(step, 1)
    dve.wait_ge(step, done + 1)
    nc.vector.tensor_tensor(tmp, v, out, ALU.mult).then_inc(step, 1)
    dve.wait_ge(step, done + 2)
    nc.vector.tensor_tensor(tmp, tmp, out, ALU.mult).then_inc(step, 1)
    dve.wait_ge(step, done + 3)
    nc.vector.tensor_scalar(tmp, tmp, -0.5, 1.5, ALU.mult, ALU.add).then_inc(step, 1)
    dve.wait_ge(step, done + 4)
    return nc.vector.tensor_tensor(out, out, tmp, ALU.mult)


def norm_stage(m, src, n_src, width, dst=None, gain=None, modulate=False):
    nc = m.nc
    sq = m.p[:, 0:8 * T].rearrange("p (k t) -> p k t", t=T)
    var, rstd = m.pt[:, 0:T], m.rstd
    with stage(m, "squared summed rooted step rstd_done mod_added mod_summed mod_biased") as (
            squared, summed, rooted, step, rstd_done, mod_added, mod_summed, mod_biased):
        with nc.Block() as block:
            @block.sync
            def _(sp):
                if modulate:
                    load_ahead_loop(sp, m, C2["mod"], mod_added, 4, 4, start=2)

            @block.scalar
            def _(act):
                for k in range(n_src):
                    nc.scalar.activation(sq[:, k, :], src(k), ACT.Square).then_inc(squared, 1)
                act.wait_ge(summed, 1)
                nc.scalar.activation(var, m.ps[:, 0, :], ACT.Identity, bias=m.eps, scale=1.0 / width).then_inc(rooted, 1)
                nc.scalar.activation(rstd, m.ps[:, 0, :], ACT.Sqrt, bias=m.eps, scale=1.0 / width).then_inc(rooted, 1)

            @block.tensor
            def _(pe):
                for k in range(n_src):
                    pe.wait_ge(squared, k + 1)
                    mm = nc.tensor.matmul(m.ps[:, 0, :], m.ones, sq[:, k, :], start=(k == 0), stop=(k == n_src - 1))
                mm.then_inc(summed, 1)
                if modulate:
                    pe.wait_ge(mod_added, 2 + 2 * KD)
                    over_partitions(m, (m.mod_accs[:, 0, :], m.mod_accs[:, 1, :]), 1).then_inc(mod_summed, 1)

            @block.vector
            def _(dve):
                if modulate:
                    for q in range(2):
                        nc.vector.memset(m.mod_accs[:, q, :], 0.0).then_inc(mod_added, 1)
                    with dve.Fori(0, 4) as i:
                        for c in range(4):
                            wait_chunk(dve, m, C2["mod"] + c, i, 4)
                            add_modulation(m, dve, m.mod_accs[:, c % 2, :], slab(m, C2["mod"] + c), i * 2 + c // 2, i * 4 + c, mod_added)
                dve.wait_ge(rooted, 2)
                refined_rsqrt(m, dve, step, 0, var, rstd, rstd, sq[:, 0, :]).then_inc(rstd_done, 1)
                if modulate:
                    bias_modulation(m, dve, 0, 2, 1, "g1", 1, mod_summed, mod_biased)
                if dst:
                    dve.wait_ge(rstd_done, 1)
                    for k in range(n_src):
                        nc.vector.scalar_tensor_tensor(dst(k), src(k), gain(k), rstd, ALU.mult, ALU.mult)


def normed_tiles(m, dst, gain, shift=None):
    def make(dve, k, made):
        r = m.nc.vector.scalar_tensor_tensor(dst(k), m.x[:, k, :], gain(k), m.rstd, ALU.mult, ALU.mult)
        if shift is None:
            return r
        r.then_inc(made, 1)
        dve.wait_ge(made, 2 * k + 1)
        return m.nc.vector.tensor_scalar(dst(k), dst(k), shift(k), None, ALU.add)
    return make, 1 if shift is None else 2


def rotate_stage(m, jobs):
    nc = m.nc
    buf = m.scratch[:, 0:10 * T].rearrange("p (b s t) -> p b s t", b=5, t=T)
    with stage(m, "squared summed rooted step rstd_done normed swapped swap_sin turned") as (
            squared, summed, rooted, step_, rstd_done, normed, swapped, swap_sin, turned):
        with nc.Block() as block:
            @block.scalar
            def _(act):
                t0 = 0
                for tile, count, rows, cols, ones, gain, width, eps, cos, sin, mask in jobs:
                    step = min(2, count)
                    if gain is None:
                        continue
                    with loop(act, count // step) as i:
                        for s in range(step):
                            nc.scalar.activation(buf[0:rows, 0, s, 0:cols], tile(i * 2 + s), ACT.Square).then_inc(squared, 1)
                        for s in range(step):
                            act.wait_ge(summed, t0 + i * 2 + s + 1)
                            act.wait_ge(normed, t0 + i * 2 + s + 1)
                            nc.scalar.activation(buf[0:rows, 1, s, 0:cols], m.ps[0:rows, s, 0:cols], ACT.Sqrt, bias=eps[0:rows],
                                                 scale=1.0 / width).then_inc(rooted, 1)
                            nc.scalar.activation(buf[0:rows, 4, s, 0:cols], m.ps[0:rows, s, 0:cols], ACT.Identity,
                                                 bias=eps[0:rows], scale=1.0 / width).then_inc(rooted, 1)
                    t0 += count

            @block.tensor
            def _(pe):
                pe.sem_inc(rooted, 4)
                t0 = 0
                for tile, count, rows, cols, ones, gain, width, eps, cos, sin, mask in jobs:
                    step = min(2, count)
                    if gain is None:
                        continue
                    with loop(pe, count // step) as i:
                        for s in range(step):
                            pe.wait_ge(squared, t0 + i * 2 + s + 1)
                            pe.wait_ge(rooted, 2 * t0 + i * 4 + 2 * s + 2)
                            nc.tensor.matmul(m.ps[0:rows, s, 0:cols], ones, buf[0:rows, 0, s, 0:cols], start=True, stop=True)\
                                .then_inc(summed, 1)
                    t0 += count

            @block.vector
            def _(dve):
                dve.sem_inc(normed, 2)
                t0 = 0
                for tile, count, rows, cols, ones, gain, width, eps, cos, sin, mask in jobs:
                    step = min(2, count)
                    with loop(dve, count // step) as i:
                        for s in range(step):
                            n_, sw = buf[0:rows, 2, s, 0:cols], buf[0:rows, 3, s, 0:cols]
                            if gain is None:
                                nc.vector.tensor_copy(n_, tile(i * 2 + s)).then_inc(normed, 1)
                            else:
                                dve.wait_ge(rooted, 2 * t0 + i * 4 + 2 * s + 6)
                                rstd, var, tmp = buf[0:rows, 1, s, 0:cols], buf[0:rows, 4, s, 0:cols], buf[0:rows, 3, s, 0:cols]
                                refined_rsqrt(m, dve, step_, i * 8 + (4 * t0 + 4 * s), var, rstd, rstd, tmp).then_inc(rstd_done, 1)
                                dve.wait_ge(rstd_done, t0 + i * 2 + s + 1)
                                nc.vector.scalar_tensor_tensor(n_, tile(i * 2 + s), gain, buf[0:rows, 1, s, 0:cols],
                                                               ALU.mult, ALU.mult).then_inc(normed, 1)
                        for s in range(step):
                            n_, sw = buf[0:rows, 2, s, 0:cols], buf[0:rows, 3, s, 0:cols]
                            dve.wait_ge(normed, t0 + i * 2 + s + 3)
                            nc.vector.tensor_tensor(tile(i * 2 + s), n_, cos, ALU.mult).then_inc(turned, 1)
                        for s in range(step):
                            n_, sw = buf[0:rows, 2, s, 0:cols], buf[0:rows, 3, s, 0:cols]
                            nc.vector.stream_shuffle(sw, n_, mask).then_inc(swapped, 1)
                        for s in range(step):
                            n_, sw = buf[0:rows, 2, s, 0:cols], buf[0:rows, 3, s, 0:cols]
                            dve.wait_ge(swap_sin, t0 + i * 2 + s + 1)
                            dve.wait_ge(turned, 2 * (t0 + i * 2) + s + 1)
                            nc.vector.tensor_tensor(tile(i * 2 + s), tile(i * 2 + s), sw, ALU.add).then_inc(turned, 1)
                    t0 += count

            @block.gpsimd
            def _(pool):
                t0 = 0
                for tile, count, rows, cols, ones, gain, width, eps, cos, sin, mask in jobs:
                    step = min(2, count)
                    with loop(pool, count // step) as i:
                        for s in range(step):
                            sw = buf[0:rows, 3, s, 0:cols]
                            pool.wait_ge(swapped, t0 + i * 2 + s + 1)
                            nc.gpsimd.tensor_tensor(sw, sw, sin, ALU.mult).then_inc(swap_sin, 1)
                    t0 += count


SCORE_BANKS = ((0, ((3, 0),)), (1, ((0, 0), (2, 128))), (2, ((1, 0),)))
PT_BANKS = ((3, ((0, 0),), "dve"), (4, ((1, 0), (3, 384)), "act"), (5, ((2, 0),), "dve"))
PT_AT = {0: 0, 1: 512, 3: 896, 2: 1024}
PT_SPAN = {3: (0, 512), 4: (512, 512), 5: (1024, 256)}
SCORE_AT = {qt: (bank, c) for bank, parts in SCORE_BANKS for qt, c in parts}


def attention_stage(m, iters, heads, stage_in, keys, krows, values, biases, weights, out, zero=(), add=False):
    nc = m.nc
    nb = heads
    NU = 4 * nb
    prob = m.p.rearrange("p (s q t) -> p s q t", s=2, t=T)
    pt = m.pt
    mx, sums, rinv = m.small[:, 0:8], m.small[:, 8:16], m.small[:, 16:24]
    with stage(m, "q_staged v_staged scores maxed exped summed inverted scaled transposed pt_dve pt_act pv_done o_out zeroed") as (
            q_staged, v_staged, scores, maxed, exped, summed, inverted, scaled, transposed, pt_dve, pt_act, pv_done, o_out, zeroed):
        with nc.Block() as block:
            @block.gpsimd
            def _(pool):
                for part in zero:
                    nc.gpsimd.memset(part, 0.0).then_inc(zeroed, 1)
                if zero:
                    pool.wait_ge(zeroed, len(zero))
                with loop(pool, iters) as i:
                    for j in range(4):
                        pool.wait_ge(pv_done, i * NU + (j + 1) * nb)
                        hold(pool, m)
                        src, dst = stage_in(i, j)
                        nc.gpsimd.tensor_copy(dst, src).then_inc(q_staged, 1)
                        pool.wait_ge(q_staged, i * 4 + j + 1)
                        hold(pool, m)
                        for b in range(nb):
                            nc.gpsimd.tensor_copy(m.vstage(j, b), values(i, j, b)).then_inc(v_staged, 1)
                        pool.wait_ge(v_staged, i * 4 * nb + (j + 1) * nb)

            @block.tensor
            def _(pe):
                pe.sem_inc(pv_done, NU)
                if zero:
                    pe.wait_ge(zeroed, len(zero))
                with loop(pe, iters) as i:
                    def score(u):
                        j, b = divmod(u, nb)
                        if b == 0:
                            pe.wait_ge(q_staged, i * 4 + j + 1)
                        for g, (bank, parts) in enumerate(SCORE_BANKS):
                            pe.wait_ge(exped, i * 3 * NU + 3 * u + g + 1)
                            for qt, c in parts:
                                w = P * (qt + 1)
                                o = m.ps[:, bank, c:c + w]
                                bias, c0 = biases(b, qt)
                                nc.tensor.matmul(o, m.qstage(j)[0:krows, qt * P:(qt + 1) * P], keys(i, j, b)[:, 0:w],
                                                 start=True, stop=False)
                                mm = nc.tensor.matmul(o[:, c0:w], m.ident_bf, bias, start=False, stop=True)
                            mm.then_inc(scores, 1)

                    def turn(u):
                        pe.wait_ge(scaled, i * NU + u + 1)
                        for g, (bank, parts, who) in enumerate(PT_BANKS):
                            pe.wait_ge(*((pt_dve, i * 2 * NU + 2 * u + g // 2 + 1) if who == "dve" else (pt_act, i * NU + u + 1)))
                            for kt, c in parts:
                                for qt in range(kt, TT):
                                    mm = nc.tensor.transpose(m.ps[:, bank, c + (qt - kt) * P:c + (qt - kt + 1) * P],
                                                             prob[:, u % 2, qt, kt * P:(kt + 1) * P], m.ident)
                            mm.then_inc(transposed, 1)

                    def product(u):
                        j, b = divmod(u, nb)
                        half = j % 2
                        if b == 0:
                            pe.wait_ge(v_staged, i * 4 * nb + (j + 1) * nb)
                            pe.wait_ge(o_out, i * 2 + j // 2 + 1)
                        pe.wait_ge(pt_dve, i * 2 * NU + 2 * u + 2 + 2)
                        pe.wait_ge(pt_act, i * NU + u + 1 + 1)
                        for kt in range(TT):
                            mm = nc.tensor.matmul(m.ps[64 * half:64 * half + 64, 6 + j // 2, kt * P:T], m.vstage(j, b)[:, kt, :],
                                                  pt[:, PT_AT[kt]:PT_AT[kt] + T - kt * P],
                                                  start=(b == 0 and kt == 0), stop=(b == nb - 1 and kt == TT - 1))
                        mm.then_inc(pv_done, 1)

                    score(0)
                    for u in range(NU):
                        if u + 1 < NU:
                            score(u + 1)
                        turn(u)
                        if u:
                            product(u - 1)
                    product(NU - 1)

            @block.vector
            def _(dve):
                dve.sem_inc(pt_dve, 2)
                with loop(dve, iters) as i:
                    def rowmax(u):
                        for g, (bank, parts) in enumerate(SCORE_BANKS):
                            dve.wait_ge(scores, i * 3 * NU + 3 * u + g + 1)
                            for qt, c in parts:
                                r = nc.vector.tensor_reduce(mx[:, 4 * (u % 2) + qt:4 * (u % 2) + qt + 1],
                                                            m.ps[:, bank, c:c + P * (qt + 1)], AX, ALU.max, negate=True)
                            r.then_inc(maxed, 1)

                    def scale(u):
                        j, b = divmod(u, nb)
                        s = 4 * (u % 2)
                        dve.wait_ge(exped, i * 3 * NU + 3 * u + 6)
                        nc.vector.reciprocal(rinv[:, s:s + 4], sums[:, s:s + 4]).then_inc(inverted, 1)
                        w = weights(i, j, b)
                        if w is not None:
                            dve.wait_ge(inverted, i * 2 * NU + 2 * u + 1)
                            nc.vector.tensor_tensor(rinv[:, s:s + 4], rinv[:, s:s + 4], w.rearrange("p t o -> p (t o)"), ALU.mult).then_inc(inverted, 1)
                            dve.wait_ge(inverted, i * 2 * NU + 2 * u + 2)
                        else:
                            dve.wait_ge(inverted, i * NU + u + 1)
                        for qt in range(TT):
                            v = prob[:, u % 2, qt, 0:P * (qt + 1)]
                            r = nc.vector.tensor_scalar(v, v, rinv[:, s + qt:s + qt + 1], None, ALU.mult)
                        r.then_inc(scaled, 1)

                    def copy_pt(u):
                        for g, (bank, parts, who) in enumerate(PT_BANKS):
                            if who == "dve":
                                at, w = PT_SPAN[bank]
                                dve.wait_ge(transposed, i * 3 * NU + 3 * u + g + 1)
                                dve.wait_ge(pv_done, i * NU + u + NU)
                                nc.vector.tensor_copy(pt[:, at:at + w], m.ps[:, bank, 0:w]).then_inc(pt_dve, 1)

                    rowmax(0)
                    scale(0)
                    rowmax(1)
                    for u in range(NU):
                        if u + 1 < NU:
                            scale(u + 1)
                        copy_pt(u)
                        if u + 2 < NU:
                            rowmax(u + 2)
                        for v in range(max(u - 1, 0), u if u < NU - 1 else NU):
                            j, b = divmod(v, nb)
                            if j % 2 and b == nb - 1 and add:
                                dve.wait_ge(pv_done, i * NU + v + 1 + NU)
                                nc.vector.tensor_tensor(out(i, j // 2), out(i, j // 2), m.ps[:, 6 + j // 2, :], ALU.add)\
                                    .then_inc(o_out, 1)

            @block.scalar
            def _(act):
                act.sem_inc(exped, 3)
                act.sem_inc(pt_act, 1)
                act.sem_inc(o_out, 2)
                with loop(act, iters) as i:
                    def exps(u):
                        for g, (bank, parts) in enumerate(SCORE_BANKS):
                            act.wait_ge(maxed, i * 3 * NU + 3 * u + g + 1)
                            if g == 0 and u >= 2:
                                act.wait_ge(transposed, i * 3 * NU + 3 * (u - 1))
                            elif g == 0:
                                act.wait_ge(pv_done, i * NU + NU)
                            for qt, c in parts:
                                s = 4 * (u % 2) + qt
                                a = nc.scalar.activation(prob[:, u % 2, qt, 0:P * (qt + 1)], m.ps[:, bank, c:c + P * (qt + 1)],
                                                         ACT.Exp, bias=mx[:, s:s + 1], accum_out=sums[:, s:s + 1])
                            a.then_inc(exped, 1)

                    exps(0)
                    for u in range(NU):
                        if u + 1 < NU:
                            exps(u + 1)
                        for g, (bank, parts, who) in enumerate(PT_BANKS):
                            if who == "act":
                                at, w = PT_SPAN[bank]
                                act.wait_ge(transposed, i * 3 * NU + 3 * u + g + 1)
                                act.wait_ge(pv_done, i * NU + u + NU)
                                nc.scalar.activation(pt[:, at:at + w], m.ps[:, bank, 0:w], ACT.Copy).then_inc(pt_act, 1)
                        for v in range(max(u - 1, 0), u if u < NU - 1 else NU):
                            j, b = divmod(v, nb)
                            if j % 2 and b == nb - 1 and not add:
                                act.wait_ge(pv_done, i * NU + v + 1 + NU)
                                nc.scalar.activation(out(i, j // 2), m.ps[:, 6 + j // 2, :], ACT.Copy).then_inc(o_out, 1)


def params_stage(m, src):
    with stage(m, "loaded") as (loaded,):
        with m.nc.Block() as block:
            @block.sync
            def _(sp):
                sp.dma_start(m.par[:, 0:NPAR], src[m.layer]).then_inc(loaded, 16)
                sp.wait_ge(loaded, 16)


def merge_stage(m, base, branches, source, gates, bias):
    nc = m.nc
    count = 4 * branches
    with stage(m, "chunk_done hi_ready lo_ready src_hi src_lo gated added") as (
            chunk_done, hi_ready, lo_ready, src_hi, src_lo, gated, added):
        with nc.Block() as block:
            @block.sync
            def _(sp):
                load_ahead_loop(sp, m, base, lo_ready, branches, 4)

            @block.gpsimd
            def _(pool):
                weights_lo_loop(pool, m, base, hi_ready, lo_ready, branches, 4)

            @block.tensor
            def _(pe):
                pe.sem_inc(chunk_done, 1)
                for b in range(branches):
                    for j in range(4):
                        if b:
                            pe.wait_ge(gated, 8 * (b - 1) + 2 * j + 2)
                        pe.wait_ge(hi_ready, 4 * b + j + 1)
                        passes = ((m.w_hi, m.a_hi, src_hi), (m.w_hi, m.a_lo, src_lo), (m.w_lo, m.a_hi, None))
                        for p, (w, a, ready) in enumerate(passes):
                            if p == 2:
                                pe.wait_ge(lo_ready, 4 * b + j + 1)
                            for k in range(4):
                                if j == 0 and ready:
                                    pe.wait_ge(ready, 4 * b + k + 1)
                                for n in range(2):
                                    mm = nc.tensor.matmul(m.ps[:, 2 * j + n, :], unit_tile(w[:, j % 2, :], 4 * n + k),
                                                          a[:, 4 * (b % 2) + k, :], start=(p == 0 and k == 0),
                                                          stop=(p == 2 and k == 3))
                        mm.then_inc(chunk_done, 1)

            @block.scalar
            def _(act):
                def cut(b):
                    for k in range(4):
                        split_hi(m, 4 * (b % 2) + k, source(b, k)).then_inc(src_hi, 1)

                cut(0)
                weights_hi(act, m, base, 0, 0, 4, chunk_done, hi_ready)
                for b in range(branches):
                    weights_hi(act, m, base, b, 1, 4, chunk_done, hi_ready)
                    if b + 1 < branches:
                        act.wait_ge(chunk_done, 4 * b + 1)
                        cut(b + 1)
                    for j in range(2, 5 if b + 1 < branches else 4):
                        weights_hi(act, m, base, b, j, 4, chunk_done, hi_ready)

            @block.vector
            def _(dve):
                def cut(b, k):
                    dve.wait_ge(src_hi, 4 * b + k + 1)
                    split_lo(m, 4 * (b % 2) + k, source(b, k)).then_inc(src_lo, 1)

                for k in range(4):
                    cut(0, k)
                adds = 0
                for b in range(branches):
                    for j in range(4):
                        if b + 1 < branches:
                            cut(b + 1, j)
                        dve.wait_ge(chunk_done, 4 * b + j + 2)
                        for n in (2 * j, 2 * j + 1):
                            mix, part = m.p[:, n * T:(n + 1) * T], m.pt[:, (n % 2) * T:(n % 2 + 1) * T]
                            if b and adds >= 2:
                                dve.wait_ge(added, adds - 1 + n % 2)
                            if bias is not None and b == 1:
                                r = nc.vector.scalar_tensor_tensor(part, m.ps[:, n, :], bias(n), gates(b, n), ALU.add, ALU.mult)
                            else:
                                r = nc.vector.tensor_tensor(part if b else mix, m.ps[:, n, :], gates(b, n), ALU.mult)
                            r.then_inc(gated, 1)
                        if b:
                            for n in (2 * j, 2 * j + 1):
                                mix, part = m.p[:, n * T:(n + 1) * T], m.pt[:, (n % 2) * T:(n % 2 + 1) * T]
                                dve.wait_ge(gated, 8 * b + n + 1)
                                if b > 1:
                                    dve.wait_ge(added, 8 * (b - 2) + n + 1)
                                nc.vector.tensor_tensor(mix, mix, part, ALU.add).then_inc(added, 1)
                                adds += 1


def mla_project_stage(m):
    nc = m.nc
    base = C1["mla"]
    qm, km, vm = m.q_mla, m.k_mla, m.v_mla
    with stage(m, "chunk_done head_done q_out k_out v_done v_out") as (chunk_done, head_done, q_out, k_out, v_done, v_out):
        with nc.Block() as block:
            @block.sync
            def _(sp):
                load_ahead_loop(sp, m, base, chunk_done, 1, 6)

            @block.tensor
            def _(pe):
                for h in range(NH):
                    if h % 2 == 0:
                        wait_chunk(pe, m, base + h // 2)
                    if h >= 4:
                        pe.wait_ge(q_out, h - 3)
                    for k in range(3):
                        u = (h % 2) * 3 + k
                        mm = nc.tensor.matmul(m.ps[0:MQK, h % 4, :], slab(m, base + h // 2)[:, u * P:u * P + MQK], m.raw[:, k, :],
                                              start=(k == 0), stop=(k == 2))
                    mm.then_inc(chunk_done if h % 2 else head_done, 1)
                wait_chunk(pe, m, base + 4)
                for p in range(4):
                    for k in range(2):
                        mm = nc.tensor.matmul(m.ps[:, 4 + p, :], slab(m, base + 4)[:, (2 * p + k) * P:(2 * p + k + 1) * P],
                                              m.raw[:, 3 + k, :], start=(k == 0), stop=(k == 1))
                    mm.then_inc(chunk_done if p == 3 else head_done, 1)
                wait_chunk(pe, m, base + 5)
                pe.wait_ge(q_out, NH)
                for t in range(TT):
                    for k in range(2):
                        mm = nc.tensor.matmul(m.ps[:, t, :], m.raw[:, 3 + k, t * P:(t + 1) * P],
                                              slab(m, base + 5)[:, k * T:(k + 1) * T], start=(k == 0), stop=(k == 1))
                    mm.then_inc(chunk_done if t == TT - 1 else v_done, 1)

            @block.scalar
            def _(act):
                for h in range(NH):
                    act.wait_ge(*((chunk_done, h // 2 + 1) if h % 2 else (head_done, h // 2 + 1)))
                    nc.scalar.activation(qm[0:MQK, h, :], m.ps[0:MQK, h % 4, :], ACT.Copy).then_inc(q_out, 1)
                for t in range(TT):
                    act.wait_ge(*((chunk_done, 6) if t == TT - 1 else (v_done, t + 1)))
                    nc.scalar.activation(vm[:, t, :], m.ps[:, t, :], ACT.Copy)

            @block.vector
            def _(dve):
                for p in range(4):
                    dve.wait_ge(*((chunk_done, 5) if p == 3 else (head_done, 4 + p + 1)))
                    for half in range(2):
                        nc.vector.tensor_copy(km[0:MNOPE, 2 * p + half, :], m.ps[64 * half:64 * half + 64, 4 + p, :])

            @block.gpsimd
            def _(pool):
                for h in range(NH):
                    nc.gpsimd.tensor_copy(km[MNOPE:MQK, h, :], m.krope[MNOPE:MQK, :])


def split_terms(m, slot):
    w_hi, w_lo = m.w_hi[:, slot, :], m.w_lo[:, slot, :]
    return ((w_hi, m.a_hi), (w_hi, m.a_lo), (w_lo, m.a_hi))


def token_major(m, out, t, slot, kt, width, weight, first=True, last=True):
    terms = split_terms(m, slot)
    for p, (w, a) in enumerate(terms):
        for n_, k in enumerate(kt):
            mm = m.nc.tensor.matmul(out, a[:, k, t * P:(t + 1) * P], weight(w, k), start=(first and p == 0 and n_ == 0),
                                    stop=(last and p == 2 and n_ == len(kt) - 1))
    return mm


def misc1_stage(m):
    nc = m.nc
    base = C1["misc"]
    rows = m.p[0:24, 0:T]
    with stage(m, "chunk_done hi_ready lo_ready rows_out gates_turned v_done gates_sig") as (
            chunk_done, hi_ready, lo_ready, rows_out, gates_turned, v_done, gates_sig):
        with nc.Block() as block:
            @block.sync
            def _(sp):
                load_ahead_loop(sp, m, base, lo_ready, 1, 4)

            @block.gpsimd
            def _(pool):
                weights_lo_loop(pool, m, base, hi_ready, lo_ready, 1, 4)

            @block.tensor
            def _(pe):
                pe.sem_inc(chunk_done, 1)
                split_products(pe, m, base, 0, 0, 4, m.ps[:, 0, :], hi_ready, lo_ready).then_inc(chunk_done, 1)
                split_products(pe, m, base, 0, 1, 4, m.ps[:, 1, :], hi_ready, lo_ready).then_inc(chunk_done, 1)
                pe.wait_ge(lo_ready, 4)
                for t in range(TT):
                    for half in range(2):
                        mm = token_major(m, m.ps[:, 3 + t, 0:256], t, half, range(4 * half, 4 * half + 4), 256,
                                         lambda w, k: w[:, (k % 4) * 256:(k % 4 + 1) * 256], half == 0, half == 1)
                    mm.then_inc(v_done, 1)
                    if t == 0:
                        pe.wait_ge(rows_out, 1)
                        for t_ in range(TT):
                            tr = nc.tensor.transpose(m.ps[:, 2, t_ * 24:(t_ + 1) * 24], rows[:, t_ * P:(t_ + 1) * P], m.ident[0:24, 0:24])
                        tr.then_inc(gates_turned, 1)

            @block.scalar
            def _(act):
                for j in range(3):
                    weights_hi(act, m, base, 0, j, 4, chunk_done, hi_ready)
                act.wait_ge(chunk_done, 2)
                nc.scalar.activation(m.raw[:, 12, :], m.ps[:, 0, :], ACT.Copy)
                weights_hi(act, m, base, 0, 3, 4, chunk_done, hi_ready)
                act.wait_ge(chunk_done, 3)
                nc.scalar.activation(rows, m.ps[0:24, 1, :], ACT.Copy).then_inc(rows_out, 1)
                nc.scalar.activation(m.krope[64:96, :], m.ps[64:96, 1, :], ACT.Copy)
                act.wait_ge(gates_turned, 1)
                nc.scalar.activation(m.gn, m.ps[:, 2, 0:96], ACT.Sigmoid).then_inc(gates_sig, 1)

            @block.vector
            def _(dve):
                dve.wait_ge(gates_sig, 1)
                gn = m.gn.rearrange("p (t h n) -> p t h n", t=TT, n=3)
                gm = m.gcmp.rearrange("p (t h) -> p t h", t=TT)
                for t in range(TT):
                    nc.vector.tensor_scalar(gm[:, t, :], gn[:, t, :, 0], m.con("rowok", 4)[:, t:t + 1], None, ALU.mult)
                for t in range(TT):
                    dve.wait_ge(v_done, t + 1)
                    nc.vector.tensor_copy(m.v_nsa[:, t, :], m.ps[:, 3 + t, 0:256])


def compress_stage(m):
    nc = m.nc
    base = C1["cmp"]
    kc2 = m.kc2
    with stage(m, "chunk_done shifted hidden sig silu kcmp_done copied") as (
            chunk_done, shifted, hidden, sig, silu, kcmp_done, copied):
        with nc.Block() as block:
            @block.sync
            def _(sp):
                load_ahead_loop(sp, m, base, chunk_done, 1, 6)

            @block.vector
            def _(dve):
                for which in range(2):
                    src = m.raw[:, 11 + which, :]
                    if which == 1:
                        dve.wait_ge(chunk_done, 2)
                    for g in range(2):
                        nc.vector.tensor_copy(kc2[0:64, g, :], src[64 * g:64 * g + 64, :])
                        r = nc.vector.tensor_copy(kc2[64:128, g, 0:T - 1], src[64 * g:64 * g + 64, 1:T])
                    r.then_inc(shifted, 1)
                for which in range(2):
                    dve.wait_ge(sig, which + 1)
                    nc.vector.tensor_tensor(m.hid[:, which, :], m.ps[:, which, 0:62], m.hsig[:, which, :], ALU.mult).then_inc(silu, 1)
                dve.wait_ge(chunk_done, 6)
                for g in range(2):
                    nc.vector.tensor_copy(m.vcmp[0:NCMP, g, :], m.ps[0:NCMP, 3 + g, 0:64])

            @block.tensor
            def _(pe):
                for which, pe_col in enumerate(("pe_k", "pe_v")):
                    pe.wait_ge(shifted, which + 1)
                    for p in range(16):
                        if p % 8 == 0:
                            wait_chunk(pe, m, base + 2 * which + p // 8)
                        w = slab(m, base + 2 * which + p // 8)[:, (p % 8) * P:(p % 8 + 1) * P]
                        v = kc2.rearrange("p g (j s) -> p g j s", s=CSTRIDE)
                        o = 2 * p // CSTRIDE
                        tok = v[:, :, o:o + NCMP, 2 * p % CSTRIDE]
                        nc.tensor.matmul(m.ps[:, which, 0:62].rearrange("p (g j) -> p g j", g=2), w, tok, start=(p == 0), stop=False)
                        mm = nc.tensor.matmul(m.ps[:, which, 0:62], w, m.param(pe_col, 16)[:, p:p + 1].to_broadcast([P, 62]),
                                              start=False, stop=(p == 15))
                        if p % 8 == 7:
                            mm.then_inc(chunk_done, 1)
                for which in range(2):
                    pe.wait_ge(silu, which + 1)
                    wait_chunk(pe, m, base + 4 + which)
                    if which == 0:
                        nc.tensor.matmul(m.ps[0:64, 2, 0:62], slab(m, base + 4)[:, 0:64], m.hid[:, 0, :], start=True, stop=True)\
                            .then_inc(chunk_done, 1)
                    else:
                        for g in range(2):
                            mm = nc.tensor.matmul(m.ps[0:NCMP, 3 + g, 0:64], m.hid[:, 1, g * NCMP:(g + 1) * NCMP],
                                                  slab(m, base + 5)[:, 0:64], start=True, stop=True)
                        mm.then_inc(chunk_done, 1)

            @block.scalar
            def _(act):
                for which in range(2):
                    act.wait_ge(chunk_done, 2 * which + 2)
                    nc.scalar.activation(m.hsig[:, which, :], m.ps[:, which, 0:62], ACT.Sigmoid).then_inc(sig, 1)
                act.wait_ge(chunk_done, 5)
                nc.scalar.activation(m.kcmp[0:64, :], m.ps[0:64, 2, 0:62], ACT.Copy)


def compressed_attention_stage(m):
    nc = m.nc
    W = TT * NCMP
    with stage(m, "dup scores masked maxed centred exped summed inverted weighted scaled transposed copied pv_done") as (
            dup, scores, masked, maxed, centred, exped, summed, inverted, weighted, scaled, transposed, copied, pv_done):
        sc = m.p[:, 0:2 * 128].rearrange("p (s w) -> p s w", s=2)
        st = m.small[:, 32:64]
        ptc = m.p[:, 512:512 + 2 * T].rearrange("p (s t) -> p s t", s=2)
        mask = m.con("mask_c", W)

        def three(ap):
            return ap[:, 0:W].rearrange("p (t j) -> p t j", t=TT)

        with nc.Block() as block:
            @block.scalar
            def _(act):
                nc.scalar.activation(m.kcmp[64:128, :], m.kcmp[0:64, :], ACT.Copy).then_inc(dup, 1)
                for h in range(NH):
                    act.wait_ge(centred, h + 1)
                    nc.scalar.activation(sc[:, h % 2, 0:W], sc[:, h % 2, 0:W], ACT.Exp).then_inc(exped, 1)
                    act.wait_ge(transposed, h + 1)
                    nc.scalar.activation(ptc[0:NCMP, h % 2, :], m.ps[0:NCMP, 2 + h % 2, :], ACT.Copy).then_inc(copied, 1)
                    if h % 2:
                        act.wait_ge(pv_done, h + 1)
                        nc.scalar.activation(m.o_nsa[:, h // 2, :], m.ps[:, 4 + (h // 2) % 2, :], ACT.Copy).then_inc(dup, 1)

            @block.tensor
            def _(pe):
                pe.wait_ge(dup, 1)

                def score(h):
                    r0 = 64 * (h % 2)
                    if h >= 2:
                        pe.wait_ge(masked, h - 1)
                    for t in range(TT):
                        mm = nc.tensor.matmul(m.ps[:, h % 2, t * NCMP:(t + 1) * NCMP],
                                              m.raw[r0:r0 + 64, 5 + h // 2, t * P:(t + 1) * P],
                                              m.kcmp[r0:r0 + 64, (h // 4) * NCMP:(h // 4 + 1) * NCMP], start=True, stop=True)
                    mm.then_inc(scores, 1)

                score(0)
                for h in range(NH):
                    if h + 1 < NH:
                        score(h + 1)
                    pe.wait_ge(scaled, h + 1)
                    if h >= 2:
                        pe.wait_ge(copied, h - 1)
                    for t in range(TT):
                        mm = nc.tensor.transpose(m.ps[0:NCMP, 2 + h % 2, t * P:(t + 1) * P],
                                                 sc[:, h % 2, t * NCMP:(t + 1) * NCMP], m.ident)
                    mm.then_inc(transposed, 1)
                    pe.wait_ge(copied, h + 1)
                    if h >= 4:
                        pe.wait_ge(dup, 1 + h // 2 - 1)
                    r0 = 64 * (h % 2)
                    nc.tensor.matmul(m.ps[r0:r0 + 64, 4 + (h // 2) % 2, :], m.vcmp[0:NCMP, h // 4, :], ptc[0:NCMP, h % 2, :],
                                     start=True, stop=True).then_inc(pv_done, 1)

            @block.vector
            def _(dve):
                for h in range(NH):
                    s, a = sc[:, h % 2, :], st[:, 16 * (h % 2):16 * (h % 2) + 16]
                    dve.wait_ge(scores, h + 1)
                    if h >= 2:
                        dve.wait_ge(transposed, h - 1)
                    nc.vector.tensor_tensor(s[:, 0:W], m.ps[:, h % 2, 0:W], mask, ALU.add).then_inc(masked, 1)
                    dve.wait_ge(masked, h + 1)
                    nc.vector.tensor_reduce(a[:, 0:4], three(s), AX, ALU.max).then_inc(maxed, 1)
                    dve.wait_ge(maxed, h + 1)
                    nc.vector.tensor_tensor(three(s), three(s), a[:, 0:4].rearrange("p (t o) -> p t o", o=1).to_broadcast([P, TT, NCMP]),
                                            ALU.subtract).then_inc(centred, 1)
                    dve.wait_ge(exped, h + 1)
                    nc.vector.tensor_reduce(a[:, 4:8], three(s), AX, ALU.add).then_inc(summed, 1)
                    dve.wait_ge(summed, h + 1)
                    nc.vector.reciprocal(a[:, 8:12], a[:, 4:8]).then_inc(inverted, 1)
                    dve.wait_ge(inverted, h + 1)
                    g = m.gcmp.rearrange("p (t h) -> p t h", t=TT)[:, :, h]
                    nc.vector.tensor_tensor(a[:, 12:16], a[:, 8:12], g, ALU.mult).then_inc(weighted, 1)
                    dve.wait_ge(weighted, h + 1)
                    nc.vector.tensor_tensor(three(s), three(s), a[:, 12:16].rearrange("p (t o) -> p t o", o=1).to_broadcast([P, TT, NCMP]),
                                            ALU.mult).then_inc(scaled, 1)


def conv_padded(m):
    return m.p[:, 0:CCH * 544].rearrange("p (c t) -> p c t", c=CCH)


def glu_stage(m):
    up = conv_padded(m)
    bias = m.param("b_glu", 8)

    def gate(c):
        return "act", lambda e, bank, n, act_evac: m.nc.scalar.activation(m.glu[:, c, :], bank, ACT.Sigmoid,
                                                                          bias=bias[:, 4 + c:5 + c])

    def half(c):
        def emit(e, bank, n, act_evac):
            e.wait_ge(act_evac, CCH + c + 1)
            return m.nc.vector.scalar_tensor_tensor(up[:, c, TAPS - 1:TAPS - 1 + T], bank, bias[:, c:c + 1], m.glu[:, c, :],
                                                    ALU.add, ALU.mult)
        return "dve", emit

    def pad(dve):
        for c in range(CCH):
            m.nc.vector.memset(up[:, c, 0:TAPS - 1], 0.0)

    linear_stage(m, C1["glu"], 1, 8, [f(c) for c in range(CCH) for f in (gate, half)], dve_side=pad)


def conv_taps(m, dve, tapped):
    nc = m.nc
    up = conv_padded(m)
    w = m.param("w_dw", CCH * TAPS).rearrange("p (c w) -> p c w", c=CCH)
    for c in range(CCH):
        nc.vector.tensor_scalar(m.conv[:, c, :], up[:, c, 0:T], w[:, c, 0:1], m.param("b_dw", 4)[:, c:c + 1],
                                ALU.mult, ALU.add).then_inc(tapped, 1)
    with dve.Fori(1, TAPS) as i:
        for c in range(CCH):
            dve.wait_ge(tapped, i * CCH + (c + 1 - CCH))
            nc.vector.scalar_tensor_tensor(m.conv[:, c, :], up[:, c, bass.ds(i, T)], w[:, c, bass.ds(i, 1)], m.conv[:, c, :],
                                           ALU.mult, ALU.add).then_inc(tapped, 1)
    dve.wait_ge(tapped, CCH * TAPS)


def conv_norm_stage(m):
    nc = m.nc
    x = lambda c: m.conv[:, c, :]
    sq = m.p[:, 0:4 * T].rearrange("p (k t) -> p k t", t=T)
    mu, rstd, sig = m.pt[:, 0:T], m.pt[:, T:2 * T], m.p[:, 4 * T:8 * T].rearrange("p (k t) -> p k t", t=T)
    var = m.spare
    with stage(m, "summed mean centred squared varsum rooted step rstd_done scaled sig_done") as (
            summed, mean, centred, squared, varsum, rooted, step, rstd_done, scaled, sig_done):
        with nc.Block() as block:
            @block.tensor
            def _(pe):
                for c in range(CCH):
                    mm = nc.tensor.matmul(m.ps[:, 0, :], m.ones, x(c), start=(c == 0), stop=(c == CCH - 1))
                mm.then_inc(summed, 1)
                for c in range(CCH):
                    pe.wait_ge(squared, c + 1)
                    mm = nc.tensor.matmul(m.ps[:, 1, :], m.ones, sq[:, c, :], start=(c == 0), stop=(c == CCH - 1))
                mm.then_inc(varsum, 1)

            @block.scalar
            def _(act):
                act.wait_ge(summed, 1)
                nc.scalar.activation(mu, m.ps[:, 0, :], ACT.Copy, scale=1.0 / CONV_CH).then_inc(mean, 1)
                for c in range(CCH):
                    act.wait_ge(centred, c + 1)
                    nc.scalar.activation(sq[:, c, :], x(c), ACT.Square).then_inc(squared, 1)
                act.wait_ge(varsum, 1)
                nc.scalar.activation(rstd, m.ps[:, 1, :], ACT.Sqrt, bias=m.eps, scale=1.0 / CONV_CH).then_inc(rooted, 1)
                nc.scalar.activation(var, m.ps[:, 1, :], ACT.Identity, bias=m.eps, scale=1.0 / CONV_CH).then_inc(rooted, 1)
                for c in range(CCH):
                    act.wait_ge(scaled, c + 1)
                    nc.scalar.activation(sig[:, c, :], x(c), ACT.Sigmoid, bias=m.param("b_ln", 4)[:, c:c + 1]).then_inc(sig_done, 1)

            @block.vector
            def _(dve):
                dve.wait_ge(mean, 1)
                for c in range(CCH):
                    nc.vector.tensor_tensor(x(c), x(c), mu, ALU.subtract).then_inc(centred, 1)
                dve.wait_ge(rooted, 2)
                refined_rsqrt(m, dve, step, 0, var, rstd, rstd, sq[:, 0, :]).then_inc(rstd_done, 1)
                dve.wait_ge(rstd_done, 1)
                for c in range(CCH):
                    nc.vector.scalar_tensor_tensor(x(c), x(c), m.param("g_ln", 4)[:, c:c + 1], rstd, ALU.mult, ALU.mult).then_inc(scaled, 1)
                for c in range(CCH):
                    dve.wait_ge(sig_done, c + 1)
                    nc.vector.scalar_tensor_tensor(x(c), x(c), m.param("b_ln", 4)[:, c:c + 1], sig[:, c, :], ALU.add, ALU.mult)


def first_layer(m, par):
    nc = m.nc
    params_stage(m, par)

    def copy_act(dst):
        return "act", lambda eng, bank, n, _: m.nc.scalar.activation(dst(n), bank, ACT.Copy)

    def copy_dve(dst):
        return "dve", lambda eng, bank, n, _: m.nc.vector.tensor_copy(dst(n), bank)

    X = lambda k: m.x[:, k, :]
    raw = lambda n: m.raw[:, n, :]
    scratch = lambda k: m.p[:, k * T:(k + 1) * T]
    g_mix, g_ffn, g_cq, g_ckv = (lambda k, g=g: m.param(g, 1 + k)[:, k:k + 1] for g in ("g_mix", "g_ffn", "g_cq", "g_ckv"))
    norm_stage(m, X, KD, D)
    linear_stage(m, C1["raw"], 3, 4, [copy_act(raw), copy_dve(raw)] * 2, source=scratch, make=normed_tiles(m, scratch, g_mix))
    misc1_stage(m)
    compress_stage(m)
    norm_stage(m, raw, 3, QRANK, raw, g_cq)
    norm_stage(m, lambda k: raw(3 + k), 2, KVRANK, lambda k: raw(3 + k), g_ckv)
    mla_project_stage(m)
    rows96, rows128, rows64 = m.ones[0:MQK, 0:MQK], m.bd64, m.bd64[0:64, 0:64]
    rotate_stage(m, [
        (lambda i: m.q_mla[0:MQK, i, :], NH, MQK, T, rows96, m.param("gq_mla", 1)[0:MQK], 1, m.con("eps_mla", 1),
         m.con("cos_m", T)[0:MQK], m.con("sin_m", T)[0:MQK], SWAP32),
        (lambda i: m.k_mla[0:MQK, i, :], NH, MQK, T, rows96, m.param("gk_mla", 1)[0:MQK], MQK, m.eps,
         m.con("cos_m", T)[0:MQK], m.con("sin_m", T)[0:MQK], SWAP32),
        (lambda i: raw(i + 5), 4, P, T, rows128, m.param("gq_nsa", 1), 1, m.con("eps_nsa", 1),
         m.con("cos_n", T), m.con("sin_n", T), SWAP16),
        (lambda i: raw(i + 9), 2, P, T, rows128, m.param("gk_nsa", 1), DH, m.eps,
         m.con("cos_n", T), m.con("sin_n", T), SWAP16),
        (lambda i: m.kcmp[0:64, :], 1, 64, 62, rows64, m.param("gk_nsa", 1)[0:64], DH, m.eps,
         m.con("cos_c", 62)[0:64], m.con("sin_c", 62)[0:64], SWAP16),
    ])
    causal = lambda b, qt: (m.causal_bf, qt * P)
    attention_stage(m, 2, 1, lambda i, j: (m.q_mla[0:MQK, i * 4 + j, :], m.qstage(j)[0:MQK, :]),
                    lambda i, j, b: m.k_mla[0:MQK, i * 4 + j, :], MQK,
                    lambda i, j, b: m.v_mla[:, :, bass.ds(i * (4 * DH) + j * DH, DH)], causal,
                    lambda i, j, b: None, lambda i, p: m.o_mla[:, i * 2 + p, :])
    compressed_attention_stage(m)
    attention_stage(m, 2, 2, lambda i, j: (m.raw[64 * (j % 2):64 * (j % 2) + 64, i + (5 + 2 * (j // 2)), :],
                                           m.qstage(j)[64 * (j // 2):64 * (j // 2) + 64, :]),
                    lambda i, j, b: raw(9 + b), P,
                    lambda i, j, b: m.v_nsa[:, :, b * 128 + (j // 2) * 64:b * 128 + (j // 2) * 64 + 64], causal,
                    lambda i, j, b: m.gn.rearrange("p (t c) -> p t c", t=TT)[:, :, bass.ds(i * 6 + (12 * (j // 2) + 3 * (j % 2) + 1 + b), 1)],
                    lambda i, p: m.o_nsa[:, i + 2 * p, :],
                    zero=[m.qstage(j)[64 - 64 * (j // 2):128 - 64 * (j // 2), :] for j in range(4)], add=True)
    glu_stage(m)
    linear_stage(m, C1["gate"], 6, 4, [("act", lambda e, bank, n, _: nc.scalar.activation(m.g[:, n, :], bank, ACT.Sigmoid))] * 4,
                 extra="tapped", dve_side=lambda dve, *s: conv_taps(m, dve, *s))
    conv_norm_stage(m)
    merge_stage(m, C1["merge"], 3, lambda b, k: (m.o_mla, m.conv, m.o_nsa)[b][:, k, :],
                lambda b, n: m.g[:, 8 * b + n, :], lambda n: m.param("b_out", 8)[:, n:n + 1])
    add_x = lambda eng, bank, n, _=None: nc.vector.tensor_tensor(m.x[:, n, :], m.x[:, n, :], bank, ALU.add)
    linear_stage(m, C1["wout"], 2, 4, [("dve", add_x)] * 4, source=scratch)
    norm_stage(m, X, KD, D)
    linear_stage(m, C1["ff_up"], 8, 4, [("act", lambda e, bank, n, _: nc.scalar.activation(m.hidden[:, n, :], bank, ACT.Relu))] * 4,
                 source=scratch, make=normed_tiles(m, scratch, g_ffn),
                 post=lambda dve, n: nc.vector.tensor_tensor(m.hidden[:, n, :], m.hidden[:, n, :], m.hidden[:, n, :], ALU.mult))
    down_stage(m, C1["ff_down"], FF1 // P // 2, lambda n, bank: add_x(None, bank, n))


def position_stage(m, tri, vecs, pos):
    nc = m.nc
    turn = 2 * np.pi
    c1 = 6.28125
    c2 = float(np.round((turn - c1) * 2.0 ** 21) / 2.0 ** 21)
    c3 = float(turn - c1 - c2)
    magic = 1.5 * 2.0 ** 23
    lim = 3.1415925
    ang, n_, r, rc = (m.p[:, k * T:(k + 1) * T] for k in range(4))
    posi = m.p[:, 4 * T:5 * T].bitcast(I32)
    cos, sin = m.con("cos_n", T), m.con("sin_n", T)
    with stage(m, "pos_loaded step args lut") as (pos_loaded, step, args, lut):
        with nc.Block() as block:
            @block.sync
            def _(sp):
                sp.dma_start(posi, pos.to_broadcast([P, T])).then_inc(pos_loaded, 16)
                sp.dma_start(m.con("cos_m", T), tri).then_inc(pos_loaded, 16)
                sp.dma_start(m.con("final_g", 16), vecs).then_inc(pos_loaded, 16)
                sp.wait_ge(pos_loaded, 48)

            @block.vector
            def _(dve):
                done = 0

                def then(ins):
                    nonlocal done
                    ins.then_inc(step, 1)
                    done += 1
                    dve.wait_ge(step, done)

                dve.wait_ge(pos_loaded, 48)
                then(nc.vector.tensor_copy(ang, posi))
                then(nc.vector.tensor_scalar(ang, ang, m.con("invf", 1), None, ALU.mult))
                then(nc.vector.tensor_scalar(n_, ang, 1.0 / turn, magic, ALU.mult, ALU.add))
                then(nc.vector.tensor_scalar(n_, n_, magic, None, ALU.subtract))
                then(nc.vector.scalar_tensor_tensor(r, n_, -c1, ang, ALU.mult, ALU.add))
                then(nc.vector.scalar_tensor_tensor(r, n_, -c2, r, ALU.mult, ALU.add))
                then(nc.vector.scalar_tensor_tensor(r, n_, -c3, r, ALU.mult, ALU.add))
                then(nc.vector.tensor_scalar(rc, r, np.pi / 2, None, ALU.add))
                then(nc.vector.tensor_scalar(ang, rc, np.pi, -turn, ALU.is_gt, ALU.mult))
                then(nc.vector.tensor_tensor(rc, rc, ang, ALU.add))
                then(nc.vector.tensor_scalar(rc, rc, lim, -lim, ALU.min, ALU.max))
                then(nc.vector.tensor_scalar(r, r, lim, -lim, ALU.min, ALU.max))
                nc.vector.tensor_scalar(r, r, 1.0, None, ALU.mult).then_inc(args, 1)
                dve.wait_ge(lut, 2)
                then(nc.vector.tensor_scalar(sin, sin, m.con("sgn", 1), None, ALU.mult))
                then(nc.vector.tensor_scalar(cos, cos, m.con("rotm", 1), m.con("unrot", 1), ALU.mult, ALU.add))

            @block.scalar
            def _(act):
                act.wait_ge(args, 1)
                nc.scalar.activation(sin, r, ACT.Sin).then_inc(lut, 1)
                nc.scalar.activation(cos, rc, ACT.Sin).then_inc(lut, 1)



def add_modulation(m, dve, acc, weights, k, c, mod_added):
    dve.wait_ge(mod_added, c + 1)
    m.nc.vector.scalar_tensor_tensor(acc, weights, m.con("cvec", KD)[:, bass.ds(k, 1)], acc, ALU.mult, ALU.add).then_inc(mod_added, 1)


def over_partitions(m, accs, bank):
    for q, acc in enumerate(accs):
        for n in range(KD):
            mm = m.nc.tensor.matmul(m.ps[:, bank, KD * q + n:KD * q + n + 1], unit_tile(acc, n), m.ones[:, 0:1], start=True, stop=True)
    return mm


def bias_modulation(m, dve, first, count, bank, gain, scale, mod_summed, mod_biased):
    nc = m.nc
    dve.wait_ge(mod_summed, 1)
    mod = m.mod[:, KD * first:KD * (first + count)]
    nc.vector.tensor_tensor(mod, m.ps[:, bank, 0:KD * count], m.param("mod_b", 48)[:, KD * first:KD * (first + count)], ALU.add)\
        .then_inc(mod_biased, 1)
    dve.wait_ge(mod_biased, 1)
    a = 0 if gain == "g1" else 1
    nc.vector.scalar_tensor_tensor(m.gains[:, KD * a:KD * (a + 1)], m.mod[:, KD * scale:KD * (scale + 1)], 1.0, m.param(gain, KD),
                                   ALU.add, ALU.mult).then_inc(mod_biased, 1)


def rest_sync(m, sp, i, j, mod_added):
    for s in range(2):
        slot = (2 * j + s) % 4
        sp.wait_ge(mod_added, i * 8 + 2 * j + s + 1)
        sp.dma_start(m.mod_slots[:, slot, :], m.modw[m.layer * (4 * KD) + i * 8 + (2 * j + s)]).then_inc(m.mod_landed[slot], 16)


def rest_vector(m, dve, mod_added, *_):
    for q in range(4):
        m.nc.vector.memset(m.mod_accs[:, q, :], 0.0).then_inc(mod_added, 1)
    with dve.Fori(0, 4) as i:
        for c in range(8):
            dve.wait_ge(m.mod_landed[c % 4], m.layer * (16 * 8) + i * 32 + (c // 4) * 16 + 16)
            add_modulation(m, dve, m.mod_accs[:, c % 4, :], m.mod_slots[:, c % 4, :], i * 2 + c // 4, i * 8 + c, mod_added)


def misc2_stage(m):
    nc = m.nc
    base = C2["misc"]
    W = DH + 2 * NH
    rows = m.p[0:W, 0:T]
    with stage(m, "chunk_done hi_ready lo_ready rows_out turned") as (chunk_done, hi_ready, lo_ready, rows_out, turned):
        with nc.Block() as block:
            @block.sync
            def _(sp):
                load_ahead_loop(sp, m, base, lo_ready, 1, 2)

            @block.gpsimd
            def _(pool):
                weights_lo_loop(pool, m, base, hi_ready, lo_ready, 1, 2)

            @block.tensor
            def _(pe):
                pe.sem_inc(chunk_done, 1)
                split_products(pe, m, base, 0, 1, 2, m.ps[:, 1, :], hi_ready, lo_ready).then_inc(chunk_done, 1)
                split_products(pe, m, base, 0, 0, 2, m.ps[:, 0, :], hi_ready, lo_ready).then_inc(chunk_done, 1)
                pe.wait_ge(rows_out, 1)
                for t in range(TT):
                    tr = nc.tensor.transpose(m.ps[:, 2, t * W:(t + 1) * W], rows[:, t * P:(t + 1) * P], m.ident[0:W, 0:W])
                tr.then_inc(turned, 1)

            @block.scalar
            def _(act):
                for j in range(2):
                    weights_hi(act, m, base, 0, j, 2, chunk_done, hi_ready)
                act.wait_ge(chunk_done, 2)
                nc.scalar.activation(rows, m.ps[0:W, 1, :], ACT.Copy).then_inc(rows_out, 1)
                act.wait_ge(chunk_done, 3)
                nc.scalar.activation(m.raw[:, 8, :], m.ps[:, 0, :], ACT.Copy)
                nc.scalar.activation(m.raw[64:128, 9, :], m.ps[64:128, 0, :], ACT.Copy)
                nc.scalar.activation(m.raw[0:64, 9, :], m.ps[64:128, 0, :], ACT.Copy)

            @block.vector
            def _(dve):
                dve.wait_ge(turned, 1)
                out = m.ps[:, 2, 0:TT * W].rearrange("p (t w) -> p t w", t=TT)
                tokens = lambda a: a.rearrange("p (t w) -> p t w", t=TT)
                nc.vector.tensor_copy(tokens(m.va), out[:, :, 0:DH])
                nc.vector.tensor_tensor(tokens(m.logf), out[:, :, DH:DH + NH], tokens(m.param("fbias", 32)), ALU.add)
                nc.vector.tensor_scalar(tokens(m.wi), out[:, :, DH + NH:W], float(NH) ** -0.5, None, ALU.mult)


def index_stage(m):
    nc = m.nc
    relu = m.p[:, 0:4 * T].rearrange("p (s t) -> p s t", s=4)
    cum = m.p[:, 4 * T:6 * T].rearrange("p (s t) -> p s t", s=2)
    neg, absx, low, ex = (m.small[:, 192 + 16 * 0:224], m.small[:, 224:256], m.small[:, 0:32], m.small[:, 32:64])
    work = m.work
    order = [(h, qt) for h in range(NH) for qt in range(1, TT)]
    with stage(m, "step log_exp logf_done summed cum_done filled rows_set started scored rectified") as (
            step, log_exp, logf_done, summed, cum_done, filled, rows_set, started, scored, rectified):
        with nc.Block() as block:
            @block.gpsimd
            def _(pool):
                nc.gpsimd.memset(m.qf[64:96, :, :], 0.0).then_inc(filled, 1)
                nc.gpsimd.memset(m.qf[96:97, :, :], 1.0).then_inc(filled, 1)
                nc.gpsimd.memset(m.kf[64:96, :, :], 0.0).then_inc(filled, 1)
                pool.wait_ge(filled, 3)
                nc.gpsimd.memset(m.kf[64:65, :, :], 1.0).then_inc(filled, 1)

            @block.sync
            def _(sp):
                sp.wait_ge(cum_done, 2)
                sp.wait_ge(filled, 4)
                for h in range(NH):
                    sp.dma_start(m.qf[64:65, h, :], cum[h:h + 1, 0, :]).then_inc(rows_set, 16)
                    sp.dma_start(m.kf[96:97, h, :], cum[h:h + 1, 1, :]).then_inc(rows_set, 16)
                sp.wait_ge(rows_set, 16 * 2 * NH)

            @block.scalar
            def _(act):
                use_log_exp(m)
                act.wait_ge(step, 2)
                nc.scalar.activation(ex, absx, ACT.Exp, scale=-1.0).then_inc(log_exp, 1)
                act.wait_ge(log_exp, 1)
                nc.scalar.activation(ex, ex, ACT.Ln, bias=1.0).then_inc(log_exp, 1)
                for n_, (h, qt) in enumerate(order):
                    w = P * (qt + 1)
                    act.wait_ge(scored, n_ + 1)
                    if n_ >= 4:
                        act.wait_ge(started, 3 + n_ - 3)
                    nc.scalar.activation(relu[:, n_ % 4, 0:w], m.ps[:, n_ % 4, 0:w], ACT.Relu, scale=float(DH) ** -0.5)\
                        .then_inc(rectified, 1)
                act.wait_ge(summed, 1)
                nc.scalar.activation(cum[0:NH, 0, :], m.ps[0:NH, 4, :], ACT.Copy).then_inc(cum_done, 1)
                nc.scalar.activation(cum[0:NH, 1, :], m.ps[0:NH, 4, :], ACT.Copy, scale=-1.0).then_inc(cum_done, 1)

            @block.vector
            def _(dve):
                nc.vector.tensor_scalar(neg, m.logf, -1.0, None, ALU.mult).then_inc(step, 1)
                dve.wait_ge(step, 1)
                nc.vector.tensor_tensor(absx, neg, m.logf, ALU.max).then_inc(step, 1)
                nc.vector.tensor_scalar(low, neg, 0.0, None, ALU.max).then_inc(step, 1)
                dve.wait_ge(log_exp, 2)
                dve.wait_ge(step, 3)
                nc.vector.tensor_tensor(low, low, ex, ALU.add).then_inc(step, 1)
                dve.wait_ge(step, 4)
                nc.vector.tensor_scalar(m.logf, low, -1.0, None, ALU.mult).then_inc(logf_done, 1)
                for qt in range(1, TT):
                    nc.vector.memset(work[qt][:, 0:qt * P], 0.0)
                    nc.vector.tensor_copy(work[qt][:, qt * P:(qt + 1) * P], m.con("chunkmask", P)).then_inc(started, 1)
                for n_, (h, qt) in enumerate(order):
                    w = P * (qt + 1)
                    dve.wait_ge(rectified, n_ + 1)
                    dve.wait_ge(started, n_ + 1)
                    nc.vector.scalar_tensor_tensor(work[qt], relu[:, n_ % 4, 0:w], m.wi[:, qt * NH + h:qt * NH + h + 1], work[qt],
                                                   ALU.mult, ALU.add).then_inc(started, 1)

            @block.tensor
            def _(pe):
                for n_, (h, qt) in enumerate(order):
                    w, r0 = P * (qt + 1), 64 * (h % 2)
                    if n_ >= 4:
                        pe.wait_ge(rectified, n_ - 3)
                    nc.tensor.matmul(m.ps[:, n_ % 4, 0:w], m.raw[r0:r0 + 64, 4 + h // 2, qt * P:(qt + 1) * P],
                                     m.raw[r0:r0 + 64, 9, 0:w], start=True, stop=True).then_inc(scored, 1)
                pe.wait_ge(logf_done, 1)
                for t in range(TT):
                    mm = nc.tensor.matmul(m.ps[0:NH, 4, t * P:T], m.logf[:, t * NH:(t + 1) * NH], m.tri[:, 0:T - t * P],
                                          start=(t == 0), stop=(t == TT - 1))
                mm.then_inc(summed, 1)


TAKEN = -3e38


def select_topk(m, dve, top8, replaced, marked):
    nc = m.nc
    best = m.small[:, 0:24]
    dve.sem_inc(replaced, 3)
    with dve.Fori(0, TOPK // 8) as r:
        dve.wait_ge(replaced, r * 3 + 3)
        hold(dve, m)
        for qt in range(1, TT):
            nc.vector.max(best[:, 8 * (qt - 1):8 * qt], m.work[qt]).then_inc(top8, 1)
        dve.wait_ge(top8, r * 3 + 3)
        hold(dve, m)
        for qt in range(1, TT):
            nc.vector.match_replace(m.work[qt], best[:, 8 * (qt - 1):8 * qt], m.work[qt], TAKEN).then_inc(replaced, 1)
    dve.wait_ge(replaced, 3 * (TOPK // 8) + 3)
    nc.vector.tensor_copy(m.select_bf[0], m.con("chunkmask", P)).then_inc(marked, 1)
    for qt in range(1, TT):
        nc.vector.tensor_scalar(m.select_bf[qt], m.work[qt], TAKEN / 2, NEG, ALU.is_ge, ALU.mult).then_inc(marked, 1)


def forget_values_stage(m):
    nc = m.nc
    base = C2["fox"] + 8
    with stage(m, "chunk_done hi_ready lo_ready") as (chunk_done, hi_ready, lo_ready):
        with nc.Block() as block:
            @block.sync
            def _(sp):
                load_ahead_loop(sp, m, base, lo_ready, 1, 4)

            @block.gpsimd
            def _(pool):
                weights_lo_loop(pool, m, base, hi_ready, lo_ready, 1, 4)

            @block.tensor
            def _(pe):
                pe.sem_inc(chunk_done, 1)
                for c in range(4):
                    pe.wait_ge(lo_ready, c + 1)
                    for t in range(TT):
                        mm = token_major(m, m.ps[:, t, :], t, c % 2, (2 * c, 2 * c + 1), T,
                                         lambda w, k: w[:, (k % 2) * T:(k % 2 + 1) * T], c == 0, c == 3)
                    mm.then_inc(chunk_done, 1)

            @block.scalar
            def _(act):
                for j in range(4):
                    weights_hi(act, m, base, 0, j, 4, chunk_done, hi_ready)
                act.wait_ge(chunk_done, 5)
                for t in range(TT):
                    nc.scalar.activation(m.v_fox[:, t, :], m.ps[:, t, :], ACT.Copy)


def gated_up_stage(m, source, make):
    nc = m.nc
    base = C2["ff_up"]
    W = T + 2
    u = m.scratch[:, 0:4 * W].rearrange("p (s t) -> p s t", s=4)
    acc = m.scratch[:, 4 * W:4 * W + 4 * T].rearrange("p (s t) -> p s t", s=4)
    sig = m.scratch[:, 4 * W + 4 * T:4 * W + 6 * T].rearrange("p (s t) -> p s t", s=2)
    cw = m.param("conv_w", 132)
    cb = m.param("conv_b", 44)
    with stage(m, "chunk_done hi_ready lo_ready made src_hi src_lo zeroed copied tap1 tap2 tap3 sig_done half_done pair_done") as (
            chunk_done, hi_ready, lo_ready, made, src_hi, src_lo, zeroed, copied, tap1, tap2, tap3, sig_done, half_done, pair_done):
        with nc.Block() as block:
            @block.sync
            def _(sp):
                load_ahead_loop(sp, m, base, lo_ready, 11, 4)

            @block.gpsimd
            def _(pool):
                weights_lo_loop(pool, m, base, hi_ready, lo_ready, 11, 4)

            @block.tensor
            def _(pe):
                pe.sem_inc(chunk_done, 1)
                with pe.Fori(0, 11) as i:
                    for s in range(4):
                        pe.wait_ge(copied, i * 4 + s + 1)
                        split_products(pe, m, base, i, s, 4, m.ps[:, s, :], hi_ready, lo_ready,
                                       (src_hi, src_lo) if s == 0 else None).then_inc(chunk_done, 1)

            @block.scalar
            def _(act):
                weights_hi(act, m, base, 0, 0, 4, chunk_done, hi_ready)
                split_source_hi(act, m, source, make, made, src_hi)
                act.sem_inc(copied, 4)
                act.wait_ge(zeroed, 1)

                def sigmoid(i, p):
                    act.wait_ge(tap3, i * 4 + 2 * p + 5)
                    nc.scalar.activation(sig[:, p, :], acc[:, 2 * p, :], ACT.Sigmoid).then_inc(sig_done, 1)

                def turn(i, first):
                    for s in range(4):
                        weights_hi(act, m, base, i, s + 1, 4, chunk_done, hi_ready)
                        act.wait_ge(chunk_done, i * 4 + s + 2)
                        act.wait_ge(tap3, i * 4 + s + 1)
                        nc.scalar.activation(u[:, s, 2:W], m.ps[:, s, :], ACT.Copy).then_inc(copied, 1)
                        if s == 1 and not first:
                            sigmoid(i - 1, 1)
                        if s == 3:
                            sigmoid(i, 0)

                turn(0, True)
                with act.Fori(1, 11) as i:
                    turn(i, False)
                sigmoid(10, 1)

            @block.vector
            def _(dve):
                dve.sem_inc(tap3, 4)
                nc.vector.memset(u[:, :, 0:2], 0.0).then_inc(zeroed, 1)
                split_source_lo(dve, m, source, make, made, src_hi, src_lo)

                def out(i, p):
                    if isinstance(i, int):
                        return m.hidden[:, 2 * i + p, :]
                    return m.hidden[:, bass.ds(i * 2 + p, 1), :].rearrange("p o t -> p (o t)")

                def column(w, f):
                    return w[:, f:f + 1] if isinstance(f, int) else w[:, bass.ds(f, 1)]

                def finish(i, p):
                    dve.wait_ge(sig_done, i * 2 + p + 1)
                    dve.wait_ge(half_done, i * 2 + p + 1)
                    nc.vector.tensor_tensor(out(i, p), out(i, p), sig[:, p, :], ALU.mult).then_inc(pair_done, 1)

                def turn(i, first):
                    for p in range(2):
                        for s in (2 * p, 2 * p + 1):
                            f = i * 2 + (p + NF2 * (s % 2))
                            if s % 2 == 0 and not first:
                                dve.wait_ge(sig_done, i * 2 + p - 1)
                            dve.wait_ge(copied, i * 4 + s + 5)
                            nc.vector.tensor_scalar(acc[:, s, :], u[:, s, 2:W], column(cw, f + 88), column(cb, f),
                                                    ALU.mult, ALU.add).then_inc(tap1, 1)
                        for s in (2 * p, 2 * p + 1):
                            f = i * 2 + (p + NF2 * (s % 2))
                            dve.wait_ge(tap1, i * 4 + s + 1)
                            nc.vector.scalar_tensor_tensor(acc[:, s, :], u[:, s, 1:W - 1], column(cw, f + 44), acc[:, s, :],
                                                           ALU.mult, ALU.add).then_inc(tap2, 1)
                        for s in (2 * p, 2 * p + 1):
                            f = i * 2 + (p + NF2 * (s % 2))
                            dve.wait_ge(tap2, i * 4 + s + 1)
                            nc.vector.scalar_tensor_tensor(acc[:, s, :], u[:, s, 0:T], column(cw, f), acc[:, s, :],
                                                           ALU.mult, ALU.add).then_inc(tap3, 1)
                        dve.wait_ge(tap3, i * 4 + 2 * p + 6)
                        nc.vector.tensor_tensor(out(i, p), acc[:, 2 * p, :], acc[:, 2 * p + 1, :], ALU.mult).then_inc(half_done, 1)
                        if p:
                            finish(i, 0)
                        elif not first:
                            finish(i - 1, 1)

                turn(0, True)
                with dve.Fori(1, 11) as i:
                    turn(i, False)
                finish(10, 1)


def second_layer(m, par):
    nc = m.nc
    params_stage(m, par)
    X = lambda k: m.x[:, k, :]
    scratch = lambda k: m.p[:, k * T:(k + 1) * T]
    spare = lambda k: m.o[:, k, :]
    raw = lambda n: m.raw[:, n, :]
    mod = lambda part: lambda k: m.mod[:, 8 * part + k:8 * part + k + 1]
    gain = lambda a: lambda k: m.gains[:, 8 * a + k:8 * a + k + 1]

    def gated_add(part):
        return lambda e, bank, n, _=None: nc.vector.scalar_tensor_tensor(m.x[:, n, :], bank, (m.mod[:, n + 8 * part:n + 8 * part + 1] if isinstance(n, int) else m.mod[:, bass.ds(n + 8 * part, 1)]), m.x[:, n, :],
                                                                 ALU.mult, ALU.add)

    norm_stage(m, X, KD, D, modulate=True)
    linear_stage(m, C2["raw"], 1, 8,
                 [("act", lambda e, bank, n, _: nc.scalar.activation(raw(n), bank, ACT.Copy, scale=float(DH) ** -0.5 if n < 4 else 1.0)),
                  ("dve", lambda e, bank, n, _: (nc.vector.tensor_scalar(raw(n), bank, float(DH) ** -0.5, None, ALU.mult) if n < 4
                                                 else nc.vector.tensor_copy(raw(n), bank)))] * 4,
                 source=scratch, make=normed_tiles(m, scratch, gain(0), mod(0)))
    misc2_stage(m)
    rotate_stage(m, [(raw, 10, P, T, None, None, DH, None, m.con("cos_n", T), m.con("sin_n", T), SWAP16)])
    index_stage(m)

    def split_heads(n):
        dst = m.qf if n < 4 else m.kf

        def emit(eng, bank, n_, act_evac):
            for half in range(2):
                r = nc.scalar.activation(dst[0:DH, 2 * (n % 4) + half, :], bank[64 * half:64 * half + 64, :], ACT.Copy,
                                         scale=float(DH) ** -0.5 if n < 4 else 1.0)
            return r
        return ("act", emit)

    linear_stage(m, C2["fox"], 1, 8, [split_heads(n) for n in range(8)],
                 extra="top8 replaced marked", dve_side=lambda dve, *s: select_topk(m, dve, *s))
    forget_values_stage(m)
    attention_stage(m, 2, 1, lambda i, j: (m.raw[64 * (j % 2):64 * (j % 2) + 64, i * 2 + j // 2, :], m.qstage(j)[0:64, :]),
                    lambda i, j, b: raw(8), P,
                    lambda i, j, b: m.va.rearrange("p (t d) -> p t d", t=TT),
                    lambda b, qt: (m.select_bf[qt], 0), lambda i, j, b: None, lambda i, p: m.o_mla[:, i * 2 + p, :],
                    zero=[m.qstage(j)[64:128, :] for j in range(4)])
    attention_stage(m, 2, 1, lambda i, j: (m.qf[0:97, i * 4 + j, :], m.qstage(j)[0:97, :]),
                    lambda i, j, b: m.kf[0:97, i * 4 + j, :], 97,
                    lambda i, j, b: m.v_fox[:, :, bass.ds(i * (4 * DH) + j * DH, DH)],
                    lambda b, qt: (m.causal_bf, qt * P), lambda i, j, b: None, lambda i, p: m.o_nsa[:, i * 2 + p, :])

    def rest_tensor(pe, mod_added, mod_summed, mod_biased):
        pe.wait_ge(mod_added, 4 + 4 * KD)
        over_partitions(m, [m.mod_accs[:, q, :] for q in range(4)], 4).then_inc(mod_summed, 1)

    linear_stage(m, C2["gate"], 4, 4, [("act", lambda e, bank, n, _: nc.scalar.activation(m.gates2[:, n, :], bank, ACT.Sigmoid))] * 4,
                 extra="mod_added mod_summed mod_biased", dve_side=lambda dve, *side: rest_vector(m, dve, *side),
                 sync_side=lambda sp, i, j, mod_added, *_: rest_sync(m, sp, i, j, mod_added), pe_last=rest_tensor,
                 dve_last=lambda dve, _, mod_summed, mod_biased: bias_modulation(m, dve, 2, 4, 4, "g2", 4, mod_summed, mod_biased))
    merge_stage(m, C2["merge"], 2, lambda b, k: (m.o_mla, m.o_nsa)[b][:, k, :], lambda b, n: m.gates2[:, 8 * b + n, :], None)
    linear_stage(m, C2["wout"], 2, 4, [("dve", gated_add(2))] * 4, source=scratch)
    norm_stage(m, X, KD, D)
    gated_up_stage(m, spare, normed_tiles(m, spare, gain(1), mod(3)))
    down_stage(m, C2["ff_down"], NF2 // 2, lambda n, bank: gated_add(5)(None, bank, n))


def second_stack(m, par, tri, vecs, pos, view, tiles):
    m.param = lambda name, w: view("par", PAR2[name], w)
    m.per_layer, m.stream_base = NC2, BASE2
    m.tri = m.con("cos_m", T)
    vs = view("vs", 0, 4 * 256).rearrange("p (u t d) -> p u t d", u=4, t=TT)
    m.vstage = lambda j, b: vs[:, j, :, :]
    m.va = view("vs", 4 * 256, 256)
    m.mod, m.gains = view("small", 64, 48), view("small", 112, 16)
    m.wi, m.logf = view("small", 128, 32), view("small", 160, 32)
    m.raw = tiles("body", 0, 10)
    m.qf, m.kf = tiles("body", 10 * T, 8), tiles("body", 18 * T, 8)
    m.v_fox = tiles("body", 4 * T, TT)
    m.gates2 = tiles("body", 0, 16)
    m.work = {1: view("o", 0, 256), 2: view("o", T, 384), 3: view("o", 2 * T, 512)}
    bits = view("extra", 0, 640).bitcast(BF16)
    m.select_bf = {0: bits[:, 0:128], 1: bits[:, 128:384], 2: bits[:, 384:768], 3: bits[:, 768:1280]}
    position_stage(m, tri, vecs, pos)
    with m.nc.Fori(0, DEPTH) as layer:
        m.layer = layer
        second_layer(m, par)
    norm_stage(m, lambda k: m.x[:, k, :], KD, D, lambda k: m.hidden[:, k, :], lambda k: m.con("final_g", 8)[:, k:k + 1])


def build(nc, wstream, modw, par1, par2, con, causal, tri, vecs, pos, xT, outT, upto=None):
    with ExitStack() as ctx:
        arena = ctx.enter_context(nc.sbuf_tensor("arena", [P, NARENA], F32))
        w_hi, w_lo = (ctx.enter_context(nc.sbuf_tensor(n_, [P, 2, CHUNK], F32R)) for n_ in ("weights_hi", "weights_lo"))
        a_hi, a_lo = (ctx.enter_context(nc.sbuf_tensor(n_, [P, KD, T], F32R)) for n_ in ("moving_hi", "moving_lo"))
        ps = ctx.enter_context(nc.psum_tensor("ps", [P, 8, T], F32))
        landed = [ctx.enter_context(nc.semaphore(f"weights_landed{s}")) for s in range(RING)]
        mod_landed = [ctx.enter_context(nc.semaphore(f"modulation_landed{s}")) for s in range(4)]
        loaded = ctx.enter_context(nc.semaphore("inputs_loaded"))
        cast = ctx.enter_context(nc.semaphore("masks_cast"))
        passed = ctx.enter_context(nc.semaphore("waits_passed"))
        stored = ctx.enter_context(nc.semaphore("output_stored"))

        def view(name, off, w):
            return arena[:, AR[name] + off:AR[name] + off + w]

        def tiles(name, off, n, w=T):
            return view(name, off, n * w).rearrange("p (k t) -> p k t", t=w)

        m = Program()
        m.nc, m.wstream, m.landed, m.passed = nc, wstream, landed, passed
        m.modw, m.mod_landed = modw, mod_landed
        m.mod_slots, m.mod_accs = tiles("p", 0, 4, CHUNK), tiles("qs", 0, 4, CHUNK)
        m.ps = ps[:, :, :]
        m.ring = tiles("ring", 0, RING, CHUNK)
        m.x = tiles("x", 0, KD)
        m.hidden = tiles("body", 0, 36)
        m.w_hi, m.w_lo, m.a_hi, m.a_lo = w_hi[:, :, :], w_lo[:, :, :], a_hi[:, :, :], a_lo[:, :, :]
        m.p, m.pt = view("p", 0, 8 * T), view("pt", 0, 1280)
        m.par = view("par", 0, NPAR)
        m.con = lambda name, w: view("con", CON[name], w)
        m.ident, m.ones, m.bd64 = m.con("ident", P), m.con("ones", P), m.con("bd64", P)
        m.eps = m.con("eps", 1)
        m.ident_bf = view("idb", 0, 64).bitcast(BF16)
        m.causal_bf = view("caub", 0, 64).bitcast(BF16)
        m.small = view("small", 0, 256)
        qs = tiles("qs", 0, 4)
        vs = view("vs", 0, 8 * 256).rearrange("p (u t d) -> p u t d", u=8, t=TT)
        m.qstage = lambda j: qs[:, j, :]

        m.scratch = view("p", 0, 8 * T + 1280)
        m.rstd = m.pt[:, T:2 * T]
        m.spare = view("qs", 0, T)
        m.param = lambda name, w: view("par", PAR1[name], w)
        at = AR["body"] - 5 * T
        m.raw = arena[:, at:at + 13 * T].rearrange("p (k t) -> p k t", t=T)
        m.q_mla, m.k_mla = tiles("body", 6 * T, 8), tiles("body", 14 * T, 8)
        m.v_mla, m.v_nsa = tiles("body", 22 * T, TT), tiles("body", 26 * T, TT, 256)
        m.g, m.conv = tiles("body", 0, 24), tiles("body", 24 * T, CCH)
        m.glu = tiles("qs", 0, CCH)
        m.kc2 = tiles("p", 0, 2)
        m.o = tiles("o", 0, 8)
        m.o_mla, m.o_nsa = tiles("o", 0, 4), tiles("o", 4 * T, 4)
        m.gn, m.gcmp = view("small", 64, 96), view("small", 160, 32)
        m.hid, m.hsig = tiles("extra", 0, 2, 62), tiles("extra", 124, 2, 62)
        m.kcmp, m.vcmp = view("extra", 248, 62), tiles("extra", 310, 2, 64)
        m.krope = view("o", 0, T)

        with nc.Block() as block:
            @block.sync
            def _(sp):
                sp.dma_start(m.x, xT.rearrange("(k p) t -> p k t", p=P)).then_inc(loaded, 16)
                sp.dma_start(view("con", 0, NCON), con).then_inc(loaded, 16)
                sp.dma_start(m.pt[:, 0:P], causal).then_inc(loaded, 16)
                for c in range(RING):
                    sp.dma_start(m.ring[:, c, :], wstream[c]).then_inc(landed[c], 16)

            @block.vector
            def _(dve):
                dve.wait_ge(loaded, 48)
                nc.vector.tensor_copy(m.ident_bf, m.ident).then_inc(cast, 1)
                nc.vector.tensor_copy(m.causal_bf, m.pt[:, 0:P]).then_inc(cast, 1)
                dve.wait_ge(cast, 2)

        m.per_layer, m.stream_base = NC1, 0
        m.vstage = lambda j, b: vs[:, 2 * j + b, :, :]
        with nc.Fori(0, DEPTH) as layer:
            m.layer = layer
            first_layer(m, par1)
        if upto != "first":
            second_stack(m, par2, tri, vecs, pos, view, tiles)
        with nc.Block() as block:
            @block.sync
            def _(sp):
                res = m.x if upto == "first" else m.hidden[:, 0:KD, :]
                sp.dma_start(outT.rearrange("(k p) t -> p k t", p=P), res).then_inc(stored, 16)
                sp.wait_ge(stored, 16)
                for s in range(RING):
                    if upto != "first":
                        sp.wait_ge(landed[s], 16 * (NCHUNKS // RING + 1))


def constants():
    f = np.float32
    c = np.zeros((P, NCON), f)

    def put(name, a):
        a = np.asarray(a, f)
        c[:a.shape[0], CON[name]:CON[name] + a.shape[1]] = a

    put("ident", np.eye(P))
    put("ones", np.ones((P, P)))
    put("bd64", np.kron(np.eye(2), np.ones((64, 64))))
    s = np.arange(P)[:, None]
    put("chunkmask", np.where(np.arange(P)[None, :] // 64 <= s // 64, 0.0, NEG))

    def table(rot, pos):
        half = rot // 2
        inv = np.power(f(500000.0), -np.arange(half, dtype=f) * f(2.0 / rot)).astype(f)
        ang = (pos.astype(f)[:, None] * inv).astype(f)
        return np.cos(ang).T, np.sin(ang).T

    def rows(head, at, rot, pos):
        co, si = np.ones((head, len(pos)), f), np.zeros((head, len(pos)), f)
        a, b = table(rot, pos)
        h = rot // 2
        co[at:at + h], co[at + h:at + rot] = a, a
        si[at:at + h], si[at + h:at + rot] = -b, b
        return co, si

    co, si = rows(MQK, MNOPE, MROPE, np.arange(T))
    put("cos_m", co)
    put("sin_m", si)
    co, si = rows(DH, 0, 16, np.arange(T))
    put("cos_n", np.tile(co, (2, 1)))
    put("sin_n", np.tile(si, (2, 1)))
    cpos = np.arange(NCMP) * CSTRIDE + CBLOCK - 1
    co, si = rows(DH, 0, 16, cpos)
    put("cos_c", np.tile(co, (1, 2)))
    put("sin_c", np.tile(si, (1, 2)))
    q = np.arange(TT)[None, :, None] * P + np.arange(P)[:, None, None]
    put("mask_c", np.where(cpos[None, None, :] <= q, 0.0, NEG).reshape(P, -1))
    put("rowok", (q[:, :, 0] >= CBLOCK - 1))
    r = np.arange(P) % 64
    inv = np.power(f(500000.0), -np.arange(0, 16, 2, dtype=f) / f(16)).astype(f)
    put("invf", np.where(r < 16, inv[r % 8], 0.0)[:, None])
    put("sgn", np.where(r < 8, -1.0, np.where(r < 16, 1.0, 0.0))[:, None])
    put("rotm", (r < 16)[:, None])
    put("unrot", (r >= 16)[:, None])
    put("eps", np.full((P, 1), EPS))
    put("eps_mla", np.full((P, 1), MQK * EPS))
    put("eps_nsa", np.full((P, 1), DH * EPS))
    return c


def causal_bias():
    return np.where(np.arange(P)[None, :] <= np.arange(P)[:, None], 0.0, NEG).astype(np.float32)


def col_tiles(w, n0, count, kt=KD):
    k = w.shape[0]
    a = w[:, n0:n0 + count * P].reshape(k // P, P, count, P).transpose(2, 1, 0, 3)
    return a.reshape(count, P, (k // P) * P)


def put_chunks(stream, at, a):
    stream[at:at + a.shape[0], :, 0:a.shape[2]] = a


def pair_tiles(w):
    return w.reshape(4, P, 4, 2, P).transpose(2, 1, 3, 0, 4).reshape(4, P, -1)


def down_tiles(w):
    k = w.shape[0]
    return w.reshape(k // (2 * P), 2, P, 2, 4, P).transpose(0, 3, 2, 4, 1, 5).reshape(k // P, P, -1)


def by_rows(w, c0, width):
    k = w.shape[0]
    return w[:, c0:c0 + width].reshape(k // P, P, width).transpose(1, 0, 2)


def pack_first(stream, at, i, l):
    w = i["w_in"][l]
    o = np.cumsum([0, QRANK, KVRANK, MROPE, 2 * CONV_CH, 512, 768, 24])
    cq, ckv, kr, u2, qn, kvn, gn, gm = o
    b = at + C1["raw"]
    put_chunks(stream, b, col_tiles(w, cq, 3))
    put_chunks(stream, b + 3, col_tiles(w, ckv, 2))
    put_chunks(stream, b + 5, col_tiles(w, qn, 4))
    put_chunks(stream, b + 9, col_tiles(w, kvn + 256, 1))
    put_chunks(stream, b + 10, col_tiles(w, kvn + 512, 1))
    put_chunks(stream, b + 11, col_tiles(w, kvn, 1))
    b = at + C1["glu"]
    for c in range(CCH):
        put_chunks(stream, b + 2 * c, col_tiles(w, u2 + CONV_CH + c * P, 1))
        put_chunks(stream, b + 2 * c + 1, col_tiles(w, u2 + c * P, 1))
    b = at + C1["misc"]
    put_chunks(stream, b, col_tiles(w, kvn + 128, 1))
    s = stream[b + 1].reshape(P, 8, P)
    s[:, :, 64:96] = by_rows(w, kr, 32)
    s[:, :, 0:24] = by_rows(w, gn, 24)
    vv = np.concatenate([by_rows(w, kvn + 384, 128), by_rows(w, kvn + 640, 128)], axis=2)
    stream[b + 2] = vv[:, 0:4].reshape(P, -1)
    stream[b + 3] = vv[:, 4:8].reshape(P, -1)
    b = at + C1["mla"]
    uq = i["w_uq"][l].reshape(QRANK, NH, MQK)
    uq = np.concatenate([uq[:, :, MROPE:], uq[:, :, :MROPE]], axis=2)
    for h in range(NH):
        s = stream[b + h // 2].reshape(P, 8, P)
        s[:, (h % 2) * 3:(h % 2) * 3 + 3, 0:MQK] = uq[:, h].reshape(3, P, MQK).transpose(1, 0, 2)
    ukv = i["w_ukv"][l].reshape(KVRANK, NH, 128)
    nope = np.ascontiguousarray(ukv[:, :, :64]).reshape(2, P, 4, P)
    stream[b + 4] = nope.transpose(1, 2, 0, 3).reshape(P, -1)
    v = np.ascontiguousarray(ukv[:, :, 64:]).reshape(2, P, T)
    stream[b + 5] = v.transpose(1, 0, 2).reshape(P, -1)
    b = at + C1["cmp"]
    for n_, name in enumerate(("w_cmp_k", "w_cmp_v")):
        a = i[name + "1"][l].reshape(2, 8, P, P).transpose(0, 2, 1, 3).reshape(2, P, -1)
        stream[b + 2 * n_:b + 2 * n_ + 2] = a
        stream[b + 4 + n_, :, 0:64] = i[name + "2"][l]
    put_chunks(stream, at + C1["gate"], col_tiles(w, gm, 24))
    b = at + C1["merge"]
    for n_, name in enumerate(("w_o_mla", "w_conv_out", "w_o_nsa")):
        stream[b + 4 * n_:b + 4 * n_ + 4] = pair_tiles(i[name][l])
    put_chunks(stream, at + C1["wout"], col_tiles(i["w_out"][l], 0, 8))
    put_chunks(stream, at + C1["ff_up"], col_tiles(i["w_ff1"][l], 0, 32))
    stream[at + C1["ff_down"]:at + C1["ff_down"] + 32] = down_tiles(i["w_ff2"][l])


def pack_par1(i, l):
    c = np.zeros((P, NPAR), np.float32)

    def put(name, a):
        a = a.reshape(a.shape[0], -1)
        c[:a.shape[0], PAR1[name]:PAR1[name] + a.shape[1]] = a

    vec = lambda a: a.reshape(-1, P).T
    turned = lambda a: np.concatenate([a[MROPE:], a[:MROPE]])[:, None]
    for name, key in (("g_mix", "g_mix"), ("g_ffn", "g_ffn"), ("g_cq", "g_cq"), ("g_ckv", "g_ckv"), ("b_glu", "b_glu"),
                      ("b_dw", "b_dw"), ("g_ln", "g_conv_ln"), ("b_ln", "b_conv_ln"), ("b_out", "b_conv_out")):
        put(name, vec(i[key][l]))
    put("gq_mla", turned(i["g_q_mla"][l]))
    put("gk_mla", turned(i["g_k_mla"][l]))
    put("gq_nsa", np.concatenate([i["g_q_nsa"][l]] * 2)[:, None])
    put("gk_nsa", np.concatenate([i["g_k_nsa"][l]] * 2)[:, None])
    put("w_dw", i["w_dw"][l].reshape(TAPS, CCH, P).transpose(2, 1, 0))
    for n_, name in (("pe_k", "pe_cmp_k"), ("pe_v", "pe_cmp_v")):
        put(n_, i[name][l].reshape(16, P).T)
    return c


def modulation_chunks(w, first, count):
    return w.reshape(KD, P, 6, D)[:, :, first:first + count].transpose(0, 2, 1, 3).reshape(KD * count, P, D)


def pack_second(stream, at, i, l):
    w = i["w_in_2"][l]
    qa, ka, va, qi, ki, wi, qf, kf, vf, ff, gates = np.cumsum([0, 512, 64, 64, 512, 64, 8, 512, 512, 512, 8])
    stream[at + C2["mod"]:at + C2["mod"] + 2 * KD] = modulation_chunks(i["mod_w_2"][l], 0, 2)
    b = at + C2["raw"]
    put_chunks(stream, b, col_tiles(w, qa, 4))
    put_chunks(stream, b + 4, col_tiles(w, qi, 4))
    b = at + C2["misc"]
    s = stream[b].reshape(P, 8, P)
    s[:, :, 0:64], s[:, :, 64:128] = by_rows(w, ka, 64), by_rows(w, ki, 64)
    s = stream[b + 1].reshape(P, 8, P)
    s[:, :, 0:64], s[:, :, 64:72], s[:, :, 72:80] = by_rows(w, va, 64), by_rows(w, ff, 8), by_rows(w, wi, 8)
    b = at + C2["fox"]
    put_chunks(stream, b, col_tiles(w, qf, 4))
    put_chunks(stream, b + 4, col_tiles(w, kf, 4))
    v = by_rows(w, vf, 512)
    for c in range(4):
        stream[b + 8 + c] = v[:, 2 * c:2 * c + 2].reshape(P, -1)
    put_chunks(stream, at + C2["gate"], col_tiles(w, gates, 16))
    for n_, name in enumerate(("w_branch_a_2", "w_branch_b_2")):
        b = at + C2["merge"] + 4 * n_
        stream[b:b + 4] = pair_tiles(i[name][l])
    put_chunks(stream, at + C2["wout"], col_tiles(i["w_out_2"][l], 0, 8))
    a = col_tiles(i["w_up_2"][l], 0, 44)
    put_chunks(stream, at + C2["ff_up"], a.reshape(2, NF2, P, -1).transpose(1, 0, 2, 3).reshape(44, P, -1))
    stream[at + C2["ff_down"]:at + C2["ff_down"] + NF2] = down_tiles(i["w_down_2"][l])


def pack_par2(i, l):
    c = np.zeros((P, NPAR), np.float32)

    def put(name, a):
        a = a.reshape(a.shape[0], -1)
        c[:, PAR2[name]:PAR2[name] + a.shape[1]] = a

    vec = lambda a: a.reshape(-1, P).T
    put("mod_b", vec(i["mod_b_2"][l]))
    put("g1", vec(i["norm1_g_2"][l]))
    put("g2", vec(i["norm2_g_2"][l]))
    put("fbias", np.tile(i["forget_bias_2"][l][None, :], (P, TT)))
    put("conv_w", i["conv_w_2"][l].reshape(3, 44, P).transpose(2, 0, 1))
    put("conv_b", vec(i["conv_b_2"][l]))
    return c


def triangle():
    return (np.arange(T)[None, :] >= np.arange(P)[:, None]).astype(np.float32)


def host_arrays(i):
    stream = np.zeros((NCHUNKS + RING, P, CHUNK), np.float32)
    for l in range(DEPTH):
        pack_first(stream, l * NC1, i, l)
        pack_second(stream, BASE2 + l * NC2, i, l)
    vecs = np.concatenate([i["final_g_2"].reshape(KD, P).T, i["c_2"].reshape(KD, P).T], axis=1)
    return {"wstream": stream, "modw": np.concatenate([modulation_chunks(i["mod_w_2"][l], 2, 4) for l in range(DEPTH)]),
            "par1": np.stack([pack_par1(i, l) for l in range(DEPTH)]),
            "par2": np.stack([pack_par2(i, l) for l in range(DEPTH)]),
            "con": constants(), "causal": causal_bias(), "tri": triangle(), "vecs": np.ascontiguousarray(vecs),
            "pos": np.ascontiguousarray(i["positions_2"].reshape(1, T)), "xT": np.ascontiguousarray(i["x"][0].T)}


def kernel(**inputs):
    import concourse.bacc as bacc
    from concourse.bass_utils import run_bass_kernel_spmd

    i = {name: np.asarray(a) for name, a in inputs.items()}
    arrays = host_arrays(i)
    nc = bacc.Bacc("TRN2", target_bir_lowering=False, num_devices=1)
    args = [nc.dram_tensor(n_, a.shape, mybir.dt.from_np(a.dtype), kind="ExternalInput").ap() for n_, a in arrays.items()]
    out = nc.dram_tensor("outT", (D, T), F32, kind="ExternalOutput").ap()
    build(nc, *args, out)
    r = run_bass_kernel_spmd(nc, [arrays], core_ids=[0])
    return np.ascontiguousarray(np.asarray(r.results[0]["outT"]).T).reshape(1, T, D)
```

```python
from contextlib import ExitStack, contextmanager

import numpy as np
import concourse.bass as bass
from concourse import mybir

F32 = mybir.dt.float32
F32R = mybir.dt.float32r
BF16 = mybir.dt.bfloat16
I32 = mybir.dt.int32
ALU = mybir.AluOpType
ACT = mybir.ActivationFunctionType
AX = mybir.AxisListType.X

P = 128
T = 512
TT = T // P
D = 1024
KD = D // P
DEPTH = 2
EPS = 1e-6
NEG = -1e30

NH, DH = 8, 64
MQK, MNOPE, MROPE = 96, 64, 32
QRANK, KVRANK = 384, 256
CONV_CH, TAPS = 512, 31
CCH = CONV_CH // P
NCMP, CSTRIDE, CBLOCK = 31, 16, 32
FF1 = 4096
TOPK = 128
FF2 = 2816
NF2 = FF2 // P

RING = 4
CHUNK = 8 * P
C1 = {}
n = 0
for name, count in (("raw", 12), ("misc", 4), ("cmp", 6), ("mla", 6), ("glu", 8), ("gate", 24), ("merge", 12),
                    ("wout", 8), ("ff_up", 32), ("ff_down", 32)):
    C1[name] = n
    n += count
NC1 = n
C2 = {}
n = 0
for name, count in (("raw", 8), ("misc", 2), ("fox", 12), ("gate", 16), ("merge", 8),
                    ("wout", 8), ("ff_up", 44), ("ff_down", 22)):
    C2[name] = n
    n += count
NC2 = n
BASE2 = DEPTH * NC1
NCHUNKS = DEPTH * (NC1 + NC2)
assert NC1 % RING == 0 and NC2 % RING == 0

def columns(spec):
    at, off = {}, 0
    for name, w in spec:
        at[name] = off
        off += w
    return at, off


PAR1, NPAR1 = columns((("g_mix", 8), ("g_ffn", 8), ("g_cq", 3), ("g_ckv", 2), ("gq_mla", 1), ("gk_mla", 1),
                       ("gq_nsa", 1), ("gk_nsa", 1), ("b_glu", 8), ("w_dw", CCH * TAPS), ("b_dw", 4),
                       ("g_ln", 4), ("b_ln", 4), ("b_out", 8), ("pe_k", 16), ("pe_v", 16)))
PAR2, NPAR2 = columns((("mod_b", 48), ("g1", 8), ("g2", 8), ("fbias", 32), ("conv_w", 3 * 44), ("conv_b", 44)))
NPAR = max(NPAR1, NPAR2)

CON, NCON = columns((("ident", 128), ("ones", 128), ("bd64", 128), ("chunkmask", 128),
                     ("cos_m", 512), ("sin_m", 512), ("cos_n", 512), ("sin_n", 512),
                     ("cos_c", 62), ("sin_c", 62), ("mask_c", 124), ("rowok", 4), ("invf", 1), ("sgn", 1), ("rotm", 1),
                     ("select1", 16), ("select2", 26), ("sum_scale", 1), ("sum_eps", 1),
                     ("unrot", 1), ("eps", 1), ("eps_mla", 1), ("eps_nsa", 1), ("final_g", 8), ("cvec", 8)))

AR = {}
n = 0
for name, w in (("ring", RING * CHUNK), ("x", KD * T), ("p", 8 * T), ("pt", 1280), ("qs", 4 * T), ("vs", 4 * T),
                ("body", 28 * T), ("o", 8 * T), ("par", NPAR), ("con", NCON), ("idb", 64), ("caub", 64),
                ("extra", 640), ("small", 256)):
    AR[name] = n
    n += w
NARENA = n

SWAP32 = [(i + 16) % 32 for i in range(32)]
SWAP16 = [(i + 8) % 16 if i < 16 else i for i in range(32)]


class Program:
    pass


@contextmanager
def stage(m, names):
    ctx = ExitStack()
    m.parity = 1 - m.parity
    sems = [ctx.enter_context(m.nc.semaphore(f"{s}_{m.parity}")) for s in names.split()]
    with m.nc.Block() as block:
        if m.used:
            @block.gpsimd
            def _(pool):
                for s in m.used[1]:
                    pool.sem_clear(s)
        yield block, sems
    if m.used:
        m.used[0].close()
    m.used = (ctx, sems)


def zero_used(m):
    if m.used:
        with m.nc.Block() as block:
            @block.gpsimd
            def _(pool):
                for s in m.used[1]:
                    pool.sem_clear(s)
        m.used[0].close()
    m.used = None


@contextmanager
def loop(eng, count):
    if count == 1:
        yield 0
    else:
        with eng.Fori(0, count) as i:
            yield i


def chunk_flat(m, c):
    return m.layer * m.per_layer + (m.stream_base + c)


def hold(eng, m):
    eng.sem_inc(m.passed, 1)


def use_log_exp(m):
    m.nc.scalar.preload_act_table_set("natural_log_exp_and_others")


def wait_chunk(pe, m, c, i=0, body=0):
    rounds = (m.stream_base + c) // RING + 1
    pe.wait_ge(m.landed[c % RING], m.layer * (16 * m.per_layer // RING) + i * (16 * body // RING) + 16 * rounds)


def slab(m, c):
    return m.ring[:, c % RING, :]


def load_ahead_loop(sp, m, base, done, iters, body, beside=None):
    with loop(sp, iters) as i:
        for j in range(body):
            if beside:
                beside(i, j)
            sp.wait_ge(done, i * body + j + 1)
            sp.dma_start(slab(m, base + j), m.wstream[m.layer * m.per_layer + i * body + (m.stream_base + base + j + RING)])\
                .then_inc(m.landed[(base + j) % RING], 16)



def weights_hi(act, m, base, i, j, body, chunk_done, hi_ready):
    wait_chunk(act, m, base + j, i, body)
    if j:
        act.wait_ge(chunk_done, i * body + j)
    m.nc.scalar.activation(m.w_hi[:, j % 2, :], slab(m, base + j), ACT.Copy).then_inc(hi_ready, 1)


def weights_lo(pool, m, base, i, j, body, hi_ready, lo_ready):
    pool.wait_ge(hi_ready, i * body + j + 1)
    m.nc.gpsimd.tensor_tensor(m.w_lo[:, j % 2, :], slab(m, base + j), m.w_hi[:, j % 2, :].bitcast(F32), ALU.subtract)\
        .then_inc(lo_ready, 1)


def weights_lo_loop(pool, m, base, hi_ready, lo_ready, iters, body):
    with loop(pool, iters) as i:
        for j in range(body):
            weights_lo(pool, m, base, i, j, body, hi_ready, lo_ready)


def split_hi(m, k, tile):
    return m.nc.scalar.activation(m.a_hi[:, k, :], tile, ACT.Copy)


def split_lo(m, k, tile):
    return m.nc.vector.tensor_tensor(m.a_lo[:, k, :], tile, m.a_hi[:, k, :].bitcast(F32), ALU.subtract)


def split_source_hi(act, m, source, make, made, src_hi):
    for k in range(KD):
        if make:
            act.wait_ge(made, k + 1)
        if make and make[1]:
            m.nc.scalar.activation(m.a_hi[:, k, :], source(k), ACT.Identity, bias=make[1](k)).then_inc(src_hi, 1)
        else:
            split_hi(m, k, source(k)).then_inc(src_hi, 1)


def split_source_lo(dve, m, source, make, made, src_hi, src_lo):
    if make:
        for k in range(KD):
            make[0](k).then_inc(made, 1)
    for k in range(KD):
        dve.wait_ge(src_hi, k + 1)
        if make and make[1]:
            m.nc.vector.scalar_tensor_tensor(m.a_lo[:, k, :], source(k), make[1](k), m.a_hi[:, k, :].bitcast(F32), ALU.add, ALU.subtract)\
                .then_inc(src_lo, 1)
        else:
            split_lo(m, k, source(k)).then_inc(src_lo, 1)


def unit_tile(w, u):
    return w[:, u * P:(u + 1) * P]


def split_products(pe, m, base, i, j, body, bank, hi_ready, lo_ready, fresh=None):
    w_hi, w_lo = m.w_hi[:, j % 2, :], m.w_lo[:, j % 2, :]
    hi_hi, hi_lo, lo_hi = (w_hi, m.a_hi, hi_ready), (w_hi, m.a_lo, None), (w_lo, m.a_hi, lo_ready)
    order = (hi_hi, lo_hi, hi_lo) if fresh else (hi_hi, hi_lo, lo_hi)
    for p, (w, a, ready) in enumerate(order):
        if ready:
            pe.wait_ge(ready, i * body + j + 1)
        for k in range(KD):
            if fresh and p != 1:
                pe.wait_ge(fresh[p // 2], k + 1)
            mm = m.nc.tensor.matmul(bank, unit_tile(w, k), a[:, k, :], start=(p == 0 and k == 0), stop=(p == 2 and k == KD - 1))
    return mm


def linear_stage(m, base, iters, body, evac, source=None, make=None, post=None, extra="", dve_side=None,
                 sync_side=None, pe_last=None, dve_last=None, squares=False):
    assert body % RING == 0
    with stage(m, "chunk_done hi_ready lo_ready made src_hi src_lo act_evac dve_evac " + extra) as (block, (
            chunk_done, hi_ready, lo_ready, made, src_hi, src_lo, act_evac, dve_evac, *side)):
        counters = {"act": act_evac, "dve": dve_evac}
        if squares:
            squared, added = side
        sq = m.p.rearrange("p (k t) -> p k t", t=T)
        mine = {e: [g for g in range(body) if evac[g][0] == e] for e in ("act", "dve")}
        @block.sync
        def _(sp):
            load_ahead_loop(sp, m, base, lo_ready, iters, body,
                            beside=sync_side and (lambda i, j: sync_side(sp, i, j, *side)))

        @block.gpsimd
        def _(pool):
            weights_lo_loop(pool, m, base, hi_ready, lo_ready, iters, body)

        @block.tensor
        def _(pe):
            pe.sem_inc(chunk_done, 1)
            with loop(pe, iters) as i:
                for g in range(body):
                    who = evac[g][0]
                    pe.wait_ge(counters[who], i * len(mine[who]) + mine[who].index(g) + 1)
                    split_products(pe, m, base, i, g, body, m.ps[:, g, :], hi_ready, lo_ready,
                                   (src_hi, src_lo) if source and g == 0 else None).then_inc(chunk_done, 1)
            if pe_last:
                pe_last(pe, *side)

        @block.scalar
        def _(act):
            weights_hi(act, m, base, 0, 0, body, chunk_done, hi_ready)
            if source:
                split_source_hi(act, m, source, make, made, src_hi)
            if mine["act"]:
                act.sem_inc(act_evac, len(mine["act"]))
            with loop(act, iters) as i:
                for g in range(body):
                    weights_hi(act, m, base, i, g + 1, body, chunk_done, hi_ready)
                    if g in mine["act"]:
                        act.wait_ge(chunk_done, i * body + g + 2)
                        evac[g][1](act, m.ps[:, g, :], i * body + g, act_evac).then_inc(act_evac, 1)
                    if squares:
                        if g == 0:
                            act.wait_ge(src_lo, KD)
                        act.wait_ge(dve_evac, i * body + g + 1 + body)
                        m.nc.scalar.activation(sq[:, i * body + g, :], m.x[:, i * body + g, :], ACT.Square).then_inc(squared, 1)

        def add_square(dve, k):
            dve.wait_ge(squared, k + 1)
            if k > 1:
                dve.wait_ge(added, k - 1)
            m.nc.vector.tensor_tensor(sq[:, 0, :], sq[:, 0, :], sq[:, k, :], ALU.add).then_inc(added, 1)

        @block.vector
        def _(dve):
            if mine["dve"]:
                dve.sem_inc(dve_evac, len(mine["dve"]))
            if source:
                split_source_lo(dve, m, source, make, made, src_hi, src_lo)
            if dve_side:
                dve_side(dve, *side)
            if post or mine["dve"]:
                with loop(dve, iters) as i:
                    for g in range(body):
                        if g in mine["dve"]:
                            dve.wait_ge(chunk_done, i * body + g + 2)
                            evac[g][1](dve, m.ps[:, g, :], i * body + g, act_evac).then_inc(dve_evac, 1)
                        if squares and g > 1:
                            add_square(dve, i * body + g - 1)
                        if post:
                            dve.wait_ge(act_evac, i * body + g + 1 + body)
                            post(dve, i * body + g)
            if dve_last:
                dve_last(dve, *side)
            if squares:
                add_square(dve, body - 1)


def down_stage(m, base, blocks, update, run, chunk_of_mod):
    nc = m.nc
    turns, rest = divmod(blocks, 2)
    per = 2 if turns >= KD else 4
    with_mod = 2 * KD // per
    assert with_mod <= turns
    hidden = lambda k: m.hidden[:, k, :]

    with stage(m, "chunk_done hi_ready lo_ready src_hi src_lo mod_added") as (block, (
            chunk_done, hi_ready, lo_ready, src_hi, src_lo, mod_added)):
        @block.sync
        def _(sp):
            def load(i, j, mod):
                for q in range(j * per // 4, (j + 1) * per // 4) if mod else ():
                    sp.wait_ge(mod_added, i * per + q + 1)
                    sp.dma_start(m.mod_slots[:, q % 2, :], m.modw_first[chunk_of_mod + i * per + q]).then_inc(m.mod_first_landed[q % 2], 16)
                sp.wait_ge(lo_ready, i * 4 + j + 1)
                sp.dma_start(slab(m, base + j), m.wstream[m.layer * m.per_layer + i * 4 + (m.stream_base + base + j + RING)])\
                    .then_inc(m.landed[(base + j) % RING], 16)

            with sp.Fori(0, with_mod) as i:
                for j in range(4):
                    load(i, j, True)
            for i in range(with_mod, turns):
                for j in range(4):
                    load(i, j, False)
            for j in range(2 * rest):
                sp.wait_ge(lo_ready, turns * 4 + j + 1)
                sp.dma_start(slab(m, base + j), m.wstream[chunk_flat(m, base + turns * 4 + j) + RING])\
                    .then_inc(m.landed[(base + j) % RING], 16)

        @block.gpsimd
        def _(pool):
            weights_lo_loop(pool, m, base, hi_ready, lo_ready, turns, 4)
            for j in range(2 * rest):
                weights_lo(pool, m, base, turns, j, 4, hi_ready, lo_ready)

        def products(pe, i, h, first, last):
            for half in range(2):
                j = 2 * h + half
                pe.wait_ge(hi_ready, i * 4 + j + 1)
                passes = ((m.w_hi, m.a_hi, src_hi), (m.w_hi, m.a_lo, src_lo), (m.w_lo, m.a_hi, None))
                for p, (w, a, ready) in enumerate(passes):
                    if half == 0 and ready:
                        pe.wait_ge(ready, i * 4 + 2 * h + 2)
                    if p == 2:
                        pe.wait_ge(lo_ready, i * 4 + j + 1)
                    for n in range(4):
                        for k in range(2):
                            mm = nc.tensor.matmul(m.ps[:, 4 * half + n, :], unit_tile(w[:, j % 2, :], 2 * n + k),
                                                  a[:, 2 * h + k, :], start=(first and p == 0 and k == 0),
                                                  stop=(last and p == 2 and k == 1))
                mm.then_inc(chunk_done, 1)

        @block.tensor
        def _(pe):
            pe.sem_inc(chunk_done, 1)
            products(pe, 0, 0, True, False)
            products(pe, 0, 1, False, False)
            with pe.Fori(1, turns - (1 - rest)) as i:
                for h in range(2):
                    products(pe, i, h, False, False)
            if rest:
                products(pe, turns, 0, False, True)
            else:
                products(pe, turns - 1, 0, False, False)
                products(pe, turns - 1, 1, False, True)

        @block.scalar
        def _(act):
            def cut(i, h):
                for k in range(2):
                    split_hi(m, 2 * h + k, hidden(i * 4 + 2 * h + k)).then_inc(src_hi, 1)

            def block_(i, h, more):
                weights_hi(act, m, base, i, 2 * h + 1, 4, chunk_done, hi_ready)
                if more:
                    act.wait_ge(chunk_done, i * 4 + 2 * h + 1)
                    cut(*((i, 1) if h == 0 else (i + 1, 0)))
                    weights_hi(act, m, base, i, 2 * h + 2, 4, chunk_done, hi_ready)

            weights_hi(act, m, base, 0, 0, 4, chunk_done, hi_ready)
            cut(0, 0)
            with act.Fori(0, turns - (1 - rest)) as i:
                block_(i, 0, True)
                block_(i, 1, True)
            if rest:
                block_(turns, 0, False)
            else:
                block_(turns - 1, 0, True)
                block_(turns - 1, 1, False)

        @block.vector
        def _(dve):
            def cut(i, h):
                for k in range(2):
                    dve.wait_ge(src_hi, i * 4 + 2 * h + k + 1)
                    split_lo(m, 2 * h + k, hidden(i * 4 + 2 * h + k)).then_inc(src_lo, 1)

            for q in range(2):
                nc.vector.memset(m.mod_accs[:, q, :], 0.0).then_inc(mod_added, 1)
            with dve.Fori(0, with_mod) as i:
                for h in range(2):
                    cut(i, h)
                    for q in range(h * per // 2, (h + 1) * per // 2):
                        dve.wait_ge(m.mod_first_landed[q % 2], run * (16 * KD) + i * (8 * per) + (16 * (q // 2) + 16))
                        add_modulation(m, dve, m.mod_accs[:, q % 2, :], m.mod_slots[:, q % 2, :], i * (per // 2) + q // 2, i * per + q, mod_added)
            for i in range(with_mod, turns):
                cut(i, 0)
                cut(i, 1)
            if rest:
                cut(turns, 0)
            for n in range(KD):
                dve.wait_ge(chunk_done, 2 * blocks + n // 4)
                update(n, m.ps[:, n, :])


def refined_rsqrt(m, dve, step, done, v, root, out, tmp):
    nc = m.nc
    nc.vector.reciprocal(out, root).then_inc(step, 1)
    dve.wait_ge(step, done + 1)
    nc.vector.tensor_tensor(tmp, v, out, ALU.mult).then_inc(step, 1)
    dve.wait_ge(step, done + 2)
    nc.vector.tensor_tensor(tmp, tmp, out, ALU.mult).then_inc(step, 1)
    dve.wait_ge(step, done + 3)
    nc.vector.tensor_scalar(tmp, tmp, -0.5, 1.5, ALU.mult, ALU.add).then_inc(step, 1)
    dve.wait_ge(step, done + 4)
    return nc.vector.tensor_tensor(out, out, tmp, ALU.mult)


def norm_stage(m, src, n_src, width, dst=None, gain=None, modulate=False, params=None, squared_before=False):
    nc = m.nc
    sq = m.p[:, 0:8 * T].rearrange("p (k t) -> p k t", t=T)
    diag = m.pt[:, 0:T]
    var, root, tmp = m.small[:, 0:TT], m.small[:, 4:4 + TT], m.small[:, 8:8 + TT]
    with stage(m, "squared added summed rooted step inverted diag_done spread_done mod_summed mod_biased "
                  "params_loaded") as (block, (
            squared, added, summed, rooted, step, inverted, diag_done, spread_done, mod_summed, mod_biased,
            params_loaded)):
        @block.sync
        def _(sp):
            if params is not None:
                sp.dma_start(m.par[:, 0:NPAR], params[m.layer]).then_inc(params_loaded, 16)
            if params is not None:
                sp.wait_ge(params_loaded, 16)

        @block.scalar
        def _(act):
            for k in range(0 if squared_before else n_src):
                nc.scalar.activation(sq[:, k, :], src(k), ACT.Square).then_inc(squared, 1)
            act.wait_ge(summed, 1)
            nc.scalar.activation(root, m.ps[:, 0, 0:TT], ACT.Sqrt, bias=m.eps, scale=1.0 / width).then_inc(rooted, 1)
            nc.scalar.activation(var, m.ps[:, 0, 0:TT], ACT.Identity, bias=m.eps, scale=1.0 / width).then_inc(rooted, 1)

        @block.tensor
        def _(pe):
            if modulate:
                over_partitions(m, (m.mod_accs[:, 0, :], m.mod_accs[:, 1, :]), 1).then_inc(mod_summed, 1)
            if not squared_before:
                pe.wait_ge(added, n_src - 1)
            for t in range(TT):
                mm = nc.tensor.matmul(m.ps[:, 0, t:t + 1], sq[:, 0, t * P:(t + 1) * P], m.ones[:, 0:1], start=True, stop=True)
            mm.then_inc(summed, 1)
            for t in range(TT):
                pe.wait_ge(diag_done, t + 1)
                mm = nc.tensor.matmul(m.ps[:, 7, t * P:(t + 1) * P], m.ones, diag[:, t * P:(t + 1) * P], start=True, stop=True)
            mm.then_inc(spread_done, 1)

        @block.vector
        def _(dve):
            for k in range(1, 1 if squared_before else n_src):
                dve.wait_ge(squared, k + 1)
                if k > 1:
                    dve.wait_ge(added, k - 1)
                nc.vector.tensor_tensor(sq[:, 0, :], sq[:, 0, :], sq[:, k, :], ALU.add).then_inc(added, 1)
            dve.wait_ge(rooted, 2)
            refined_rsqrt(m, dve, step, 0, var, root, root, tmp).then_inc(inverted, 1)
            dve.wait_ge(inverted, 1)
            for t in range(TT):
                nc.vector.tensor_scalar(diag[:, t * P:(t + 1) * P], m.ident, root[:, t:t + 1], None, ALU.mult).then_inc(diag_done, 1)
            if modulate:
                dve.wait_ge(params_loaded, 16)
                bias_modulation(m, dve, 0, 2, 1, "g1", 1, mod_summed, mod_biased)
            if dst:
                dve.wait_ge(spread_done, 1)
                for k in range(n_src):
                    nc.vector.scalar_tensor_tensor(dst(k), src(k), gain(k), m.rstd, ALU.mult, ALU.mult)


def normed_tiles(m, dst, gain, shift=None):
    return lambda k: m.nc.vector.scalar_tensor_tensor(dst(k), m.x[:, k, :], gain(k), m.rstd, ALU.mult, ALU.mult), shift


def rotate_stage(m, groups):
    nc = m.nc
    buf = m.p.rearrange("p (b s t) -> p b s t", b=2, t=T)
    sq = m.spare4[:, 0:4 * T].rearrange("p (s t) -> p s t", t=T)
    roots = m.spare4[:, 4 * T:7 * T].rearrange("p (g t) -> p g t", t=T)
    var, tmp = m.pt[:, 0:T], m.pt[:, T:2 * T]
    tiles = [(g, *tile) for g, group in enumerate(groups) for tile in group[0]]
    norm = groups[0][1] is not None
    cut_groups = (0, 1) if norm else ()
    picks = m.w_hi[0:NH, 1, 0:NH]
    parts = lambda g, p: (m.w_hi, m.w_lo)[p][0:groups[g][1], 0, g * T:(g + 1) * T]
    first = [sum(len(group[0]) for group in groups[:g]) for g in range(len(groups) + 1)]

    def size(view):
        return view.shape[0], view.shape[1]

    with stage(m, "squared taken rooted step rstd_done spread_done normed swapped cos_done cos_by_dve sin_done turned "
                  "cut_hi cut_lo picks_done") as (block, (
            squared, taken, rooted, step, rstd_done, spread_done, normed, swapped, cos_done, cos_by_dve,
            sin_done, turned, cut_hi, cut_lo, picks_done)):
        @block.scalar
        def _(act):
            if not norm:
                return
            nc.scalar.activation(picks, m.ident[0:NH, 0:NH], ACT.Copy).then_inc(picks_done, 1)
            for t, (g, view, *_) in enumerate(tiles):
                r, c = size(view)
                if t >= 4:
                    act.wait_ge(taken, t - 3)
                nc.scalar.activation(sq[0:r, t % 4, 0:c], view, ACT.Square).then_inc(squared, 1)
                if t + 1 == first[g + 1]:
                    _, k, width, eps = groups[g]
                    act.wait_ge(taken, t + 1)
                    if g:
                        act.wait_ge(rstd_done, g)
                    nc.scalar.activation(roots[0:k, g, :], m.ps[0:k, g, :], ACT.Sqrt, bias=eps, scale=width).then_inc(rooted, 1)
                    nc.scalar.activation(var[0:k, :], m.ps[0:k, g, :], ACT.Identity, bias=eps, scale=width).then_inc(rooted, 1)

        @block.tensor
        def _(pe):
            if not norm:
                return

            def add_squares(t):
                g, view, select, *_ = tiles[t]
                r, c = size(view)
                pe.wait_ge(squared, t + 1)
                nc.tensor.matmul(m.ps[0:groups[g][1], g, 0:c], select, sq[0:r, t % 4, 0:c], start=(t == first[g]),
                                 stop=(t + 1 == first[g + 1])).then_inc(taken, 1)

            def spread(t):
                g, view, _, back, *_ = tiles[t]
                r, c = size(view)
                if g in cut_groups:
                    pe.wait_ge(picks_done, 1)
                    pe.wait_ge(cut_lo, g + 1)
                else:
                    pe.wait_ge(rstd_done, g + 1)
                if t >= 4:
                    pe.wait_ge(normed, t - 3)
                if g in cut_groups:
                    k = groups[g][1]
                    pick = picks[0:k, t - first[g]:t - first[g] + 1].to_broadcast([k, r])
                    nc.tensor.matmul(m.ps[0:r, 4 + t % 4, 0:c], pick, parts(g, 0), start=True, stop=False)
                    mm = nc.tensor.matmul(m.ps[0:r, 4 + t % 4, 0:c], pick, parts(g, 1), start=False, stop=True)
                for head, w in enumerate(() if g in cut_groups else back):
                    n = w.shape[1]
                    mm = nc.tensor.matmul(m.ps[head * n:(head + 1) * n, 4 + t % 4, 0:c], w, roots[0:groups[g][1], g, 0:c],
                                          start=True, stop=True)
                mm.then_inc(spread_done, 1)

            for t in range(first[min(2, len(groups))]):
                add_squares(t)
            for t in range(len(tiles)):
                spread(t)
                if t + first[2] < len(tiles):
                    add_squares(t + first[2])

        @block.vector
        def _(dve):
            def turn(t):
                view = tiles[t][1]
                r, c = size(view)
                if not norm:
                    dve.wait_ge(cos_by_dve, t + 1)
                elif t % 4 == 3:
                    dve.wait_ge(cos_by_dve, t // 4 + 1)
                else:
                    dve.wait_ge(cos_done, t + 1 - t // 4)
                dve.wait_ge(sin_done, t + 1)
                nc.vector.tensor_tensor(view, view, buf[0:r, 1, t % 4, 0:c], ALU.add).then_inc(turned, 1)

            for t, (g, view, _, _, gain, cos, sin, mask) in enumerate(tiles):
                r, c = size(view)
                swap = buf[0:r, 1, t % 4, 0:c]
                if norm:
                    for h in {0: (0, 1), first[1]: (2,)}.get(t, ()):
                        k = groups[h][1]
                        dve.wait_ge(rooted, 2 * h + 2)
                        if h:
                            dve.wait_ge(rstd_done, h)
                        refined_rsqrt(m, dve, step, 4 * h, var[0:k, :], roots[0:k, h, :], roots[0:k, h, :], tmp[0:k, :])\
                            .then_inc(rstd_done, 1)
                        if h in cut_groups:
                            dve.wait_ge(rstd_done, h + 1)
                            nc.vector.tensor_copy(parts(h, 0), roots[0:k, h, :]).then_inc(cut_hi, 1)
                            dve.wait_ge(cut_hi, h + 1)
                            nc.vector.tensor_tensor(parts(h, 1), roots[0:k, h, :], parts(h, 0).bitcast(F32), ALU.subtract)\
                                .then_inc(cut_lo, 1)
                    dve.wait_ge(spread_done, t + 1)
                    nc.vector.scalar_tensor_tensor(buf[0:r, 0, t % 4, 0:c], view, gain, m.ps[0:r, 4 + t % 4, 0:c], ALU.mult, ALU.mult)\
                        .then_inc(normed, 1)
                    if t >= 2:
                        turn(t - 2)
                    dve.wait_ge(normed, t + 1)
                    nc.vector.stream_shuffle(swap, buf[0:r, 0, t % 4, 0:c], mask).then_inc(swapped, 1)
                    if t % 4 == 3:
                        nc.vector.tensor_tensor(view, buf[0:r, 0, 3, 0:c], cos, ALU.mult).then_inc(cos_by_dve, 1)
                else:
                    if t >= 4:
                        dve.wait_ge(turned, t - 3)
                    nc.vector.stream_shuffle(swap, view, mask).then_inc(swapped, 1)
                    nc.vector.tensor_tensor(view, view, cos, ALU.mult).then_inc(cos_by_dve, 1)
                    if t >= 2:
                        turn(t - 2)
            for t in (len(tiles) - 2, len(tiles) - 1):
                turn(t)

        @block.gpsimd
        def _(pool):
            for t, (g, view, _, _, gain, cos, sin, mask) in enumerate(tiles):
                r, c = size(view)
                swap = buf[0:r, 1, t % 4, 0:c]
                if norm and t % 4 != 3:
                    pool.wait_ge(normed, t + 1)
                    nc.gpsimd.tensor_tensor(view, buf[0:r, 0, t % 4, 0:c], cos, ALU.mult).then_inc(cos_done, 1)
                pool.wait_ge(swapped, t + 1)
                nc.gpsimd.tensor_tensor(swap, swap, sin, ALU.mult).then_inc(sin_done, 1)


SCORE_BANKS = ((0, ((3, 0),)), (1, ((0, 0), (2, 128))), (2, ((1, 0),)))
PT_BANKS = ((3, ((0, 0),), "dve"), (4, ((1, 0), (3, 384)), "act"), (5, ((2, 0),), "dve"))
PT_AT = {0: 0, 1: 512, 3: 896, 2: 1024}
PT_SPAN = {3: (0, 512), 4: (512, 512), 5: (1024, 256)}
SCORE_AT = {qt: (bank, c) for bank, parts in SCORE_BANKS for qt, c in parts}


def attention_stage(m, nb, queries, keys, values, biases, weights, out, add=False):
    nc = m.nc
    NU = NH * nb
    prob = m.p.rearrange("p (s q t) -> p s q t", s=2, t=T)
    pt = m.pt
    mx, sums, rinv = m.small[:, 0:8], m.small[:, 8:16], m.small[:, 16:24]
    with stage(m, "scores maxed exped summed inverted scaled transposed pt_dve pt_act pv_done o_out") as (block, (
            scores, maxed, exped, summed, inverted, scaled, transposed, pt_dve, pt_act, pv_done, o_out)):
        @block.tensor
        def _(pe):
            def score(u):
                j, b = divmod(u, nb)
                for g, (bank, parts) in enumerate(SCORE_BANKS):
                    if u:
                        pe.wait_ge(exped, 3 * (u - 1) + g + 1)
                    for qt, c in parts:
                        w = P * (qt + 1)
                        o = m.ps[:, bank, c:c + w]
                        bias, c0 = biases(b, qt)
                        nc.tensor.matmul(o, queries(j)[:, qt * P:(qt + 1) * P], keys(j, b)[:, 0:w], start=True, stop=False)
                        mm = nc.tensor.matmul(o[:, c0:w], m.ident_bf, bias, start=False, stop=True)
                    mm.then_inc(scores, 1)

            def turn(u):
                pe.wait_ge(scaled, u + 1)
                for g, (bank, parts, who) in enumerate(PT_BANKS):
                    if u:
                        pe.wait_ge(*((pt_dve, 2 * u - 1 + g // 2) if who == "dve" else (pt_act, u)))
                    for kt, c in parts:
                        for qt in range(kt, TT):
                            mm = nc.tensor.transpose(m.ps[:, bank, c + (qt - kt) * P:c + (qt - kt + 1) * P],
                                                     prob[:, u % 2, qt, kt * P:(kt + 1) * P], m.ident)
                    mm.then_inc(transposed, 1)

            def product(u):
                j, b = divmod(u, nb)
                half = j % 2
                if b == 0 and j >= 4:
                    pe.wait_ge(o_out, j // 2 - 1)
                pe.wait_ge(pt_dve, 2 * u + 2)
                pe.wait_ge(pt_act, u + 1)
                for kt in range(TT):
                    mm = nc.tensor.matmul(m.ps[64 * half:64 * half + 64, 6 + j // 2 % 2, kt * P:T], values(j, b)[:, kt, :],
                                          pt[:, PT_AT[kt]:PT_AT[kt] + T - kt * P],
                                          start=(b == 0 and kt == 0), stop=(b == nb - 1 and kt == TT - 1))
                mm.then_inc(pv_done, 1)

            score(0)
            for u in range(NU):
                if u + 1 < NU:
                    score(u + 1)
                turn(u)
                if u:
                    product(u - 1)
            product(NU - 1)

        def pairs_out(u):
            for v in range(max(u - 1, 0), u if u < NU - 1 else NU):
                j, b = divmod(v, nb)
                if j % 2 and b == nb - 1:
                    yield j // 2, v

        @block.vector
        def _(dve):
            def rowmax(u):
                for g, (bank, parts) in enumerate(SCORE_BANKS):
                    dve.wait_ge(scores, 3 * u + g + 1)
                    for qt, c in parts:
                        r = nc.vector.tensor_reduce(mx[:, 4 * (u % 2) + qt:4 * (u % 2) + qt + 1],
                                                    m.ps[:, bank, c:c + P * (qt + 1)], AX, ALU.max, negate=True)
                    r.then_inc(maxed, 1)

            def scale(u):
                j, b = divmod(u, nb)
                s = 4 * (u % 2)
                dve.wait_ge(exped, 3 * u + 3)
                nc.vector.reciprocal(rinv[:, s:s + 4], sums[:, s:s + 4]).then_inc(inverted, 1)
                w = weights(j, b)
                if w is not None:
                    dve.wait_ge(inverted, 2 * u + 1)
                    nc.vector.tensor_tensor(rinv[:, s:s + 4], rinv[:, s:s + 4], w, ALU.mult).then_inc(inverted, 1)
                    dve.wait_ge(inverted, 2 * u + 2)
                else:
                    dve.wait_ge(inverted, u + 1)
                for qt in range(TT):
                    v = prob[:, u % 2, qt, 0:P * (qt + 1)]
                    r = nc.vector.tensor_scalar(v, v, rinv[:, s + qt:s + qt + 1], None, ALU.mult)
                r.then_inc(scaled, 1)

            def copy_pt(u):
                for g, (bank, parts, who) in enumerate(PT_BANKS):
                    if who == "dve":
                        at, w = PT_SPAN[bank]
                        dve.wait_ge(transposed, 3 * u + g + 1)
                        if u:
                            dve.wait_ge(pv_done, u)
                        nc.vector.tensor_copy(pt[:, at:at + w], m.ps[:, bank, 0:w]).then_inc(pt_dve, 1)

            rowmax(0)
            scale(0)
            rowmax(1)
            for u in range(NU):
                if u + 1 < NU:
                    scale(u + 1)
                copy_pt(u)
                if u + 2 < NU:
                    rowmax(u + 2)
                if add:
                    for pair, v in pairs_out(u):
                        dve.wait_ge(pv_done, v + 1)
                        nc.vector.tensor_tensor(out(pair), out(pair), m.ps[:, 6 + pair % 2, :], ALU.add).then_inc(o_out, 1)

        @block.scalar
        def _(act):
            def exps(u):
                for g, (bank, parts) in enumerate(SCORE_BANKS):
                    act.wait_ge(maxed, 3 * u + g + 1)
                    if g == 0 and u >= 2:
                        act.wait_ge(transposed, 3 * (u - 1))
                    for qt, c in parts:
                        s = 4 * (u % 2) + qt
                        a = nc.scalar.activation(prob[:, u % 2, qt, 0:P * (qt + 1)], m.ps[:, bank, c:c + P * (qt + 1)],
                                                 ACT.Exp, bias=mx[:, s:s + 1], accum_out=sums[:, s:s + 1])
                    a.then_inc(exped, 1)

            exps(0)
            for u in range(NU):
                if u + 1 < NU:
                    exps(u + 1)
                for g, (bank, parts, who) in enumerate(PT_BANKS):
                    if who == "act":
                        at, w = PT_SPAN[bank]
                        act.wait_ge(transposed, 3 * u + g + 1)
                        if u:
                            act.wait_ge(pv_done, u)
                        nc.scalar.activation(pt[:, at:at + w], m.ps[:, bank, 0:w], ACT.Copy).then_inc(pt_act, 1)
                if not add:
                    for pair, v in pairs_out(u):
                        act.wait_ge(pv_done, v + 1)
                        nc.scalar.activation(out(pair), m.ps[:, 6 + pair % 2, :], ACT.Copy).then_inc(o_out, 1)


def merge_stage(m, base, branches, conv=False):
    nc = m.nc
    x = lambda c: m.conv[:, c, :]
    sq = m.spare4[:, 0:4 * T].rearrange("p (k t) -> p k t", t=T)
    mu, var, rstd, tmp = (m.spare4[:, k * T:(k + 1) * T] for k in range(4, 8))
    with stage(m, "chunk_done hi_ready lo_ready src_hi src_lo gated added conv_summed mean centred squared varsum rooted step "
                  "rstd_done scaled sig_done conv_done") as (block, (
            chunk_done, hi_ready, lo_ready, src_hi, src_lo, gated, added, conv_summed, mean, centred, squared, varsum, rooted, step,
            rstd_done, scaled, sig_done, conv_done)):
        @block.sync
        def _(sp):
            load_ahead_loop(sp, m, base, lo_ready, len(branches), 4)

        @block.gpsimd
        def _(pool):
            weights_lo_loop(pool, m, base, hi_ready, lo_ready, len(branches), 4)

        @block.tensor
        def _(pe):
            pe.sem_inc(chunk_done, 1)
            if conv:
                for c in range(CCH):
                    mm = nc.tensor.matmul(m.ps[:, 6, :], m.ones, x(c), start=(c == 0), stop=(c == CCH - 1))
                mm.then_inc(conv_summed, 1)
            for b in range(len(branches)):
                for j in range(4):
                    if conv and (b, j) == (0, 2):
                        for c in range(CCH):
                            pe.wait_ge(squared, c + 1)
                            mm = nc.tensor.matmul(m.ps[:, 7, :], m.ones, sq[:, c, :], start=(c == 0), stop=(c == CCH - 1))
                        mm.then_inc(varsum, 1)
                    if conv and (b, j) == (0, 3):
                        pe.wait_ge(mean, 1)
                        pe.wait_ge(rooted, 2)
                    if b:
                        pe.wait_ge(gated, 8 * (b - 1) + 2 * j + 2)
                    pe.wait_ge(hi_ready, 4 * b + j + 1)
                    passes = ((m.w_hi, m.a_hi, src_hi), (m.w_hi, m.a_lo, src_lo), (m.w_lo, m.a_hi, None))
                    for p, (w, a, ready) in enumerate(passes):
                        if p == 2:
                            pe.wait_ge(lo_ready, 4 * b + j + 1)
                        for k in range(4):
                            if j == 0 and ready:
                                pe.wait_ge(ready, 4 * b + k + 1)
                            for n in range(2):
                                mm = nc.tensor.matmul(m.ps[:, 2 * j + n, :], unit_tile(w[:, j % 2, :], 4 * n + k),
                                                      a[:, 4 * (b % 2) + k, :], start=(p == 0 and k == 0),
                                                      stop=(p == 2 and k == 3))
                    mm.then_inc(chunk_done, 1)

        @block.scalar
        def _(act):
            def cut(b):
                if b:
                    act.wait_ge(chunk_done, 4 * b - 3)
                if conv and b == 2:
                    act.wait_ge(conv_done, CCH)
                for k in range(4):
                    split_hi(m, 4 * (b % 2) + k, branches[b][0](k)).then_inc(src_hi, 1)

            cut(0)
            weights_hi(act, m, base, 0, 0, 4, chunk_done, hi_ready)
            if conv:
                act.wait_ge(conv_summed, 1)
                nc.scalar.activation(mu, m.ps[:, 6, :], ACT.Copy, scale=1.0 / CONV_CH).then_inc(mean, 1)
            for b in range(len(branches)):
                more = b + 1 < len(branches)
                weights_hi(act, m, base, b, 1, 4, chunk_done, hi_ready)
                for c in range(CCH):
                    if conv and b == 0:
                        act.wait_ge(centred, c + 1)
                        nc.scalar.activation(sq[:, c, :], x(c), ACT.Square).then_inc(squared, 1)
                    if conv and b == 1:
                        act.wait_ge(scaled, c + 1)
                        nc.scalar.activation(sq[:, c, :], x(c), ACT.Sigmoid, bias=m.param("b_ln", 4)[:, c:c + 1]).then_inc(sig_done, 1)
                weights_hi(act, m, base, b, 2, 4, chunk_done, hi_ready)
                if conv and b == 0:
                    act.wait_ge(varsum, 1)
                    nc.scalar.activation(rstd, m.ps[:, 7, :], ACT.Sqrt, bias=m.eps, scale=1.0 / CONV_CH).then_inc(rooted, 1)
                    nc.scalar.activation(var, m.ps[:, 7, :], ACT.Identity, bias=m.eps, scale=1.0 / CONV_CH).then_inc(rooted, 1)
                weights_hi(act, m, base, b, 3, 4, chunk_done, hi_ready)
                if more:
                    cut(b + 1)
                    weights_hi(act, m, base, b, 4, 4, chunk_done, hi_ready)

        @block.vector
        def _(dve):
            adds = 0

            def cut(b):
                for k in range(4):
                    dve.wait_ge(src_hi, 4 * b + k + 1)
                    split_lo(m, 4 * (b % 2) + k, branches[b][0](k)).then_inc(src_lo, 1)

            def gate(b, j):
                nonlocal adds
                _, gates, bias = branches[b]
                dve.wait_ge(chunk_done, 4 * b + j + 2)
                for n in (2 * j, 2 * j + 1):
                    mix, part = m.p[:, n * T:(n + 1) * T], m.pt[:, (n % 2) * T:(n % 2 + 1) * T]
                    if b and adds >= 2:
                        dve.wait_ge(added, adds - 1 + n % 2)
                    if bias:
                        r = nc.vector.scalar_tensor_tensor(part, m.ps[:, n, :], bias(n), gates(n), ALU.add, ALU.mult)
                    else:
                        r = nc.vector.tensor_tensor(part if b else mix, m.ps[:, n, :], gates(n), ALU.mult)
                    r.then_inc(gated, 1)
                if b:
                    for n in (2 * j, 2 * j + 1):
                        mix, part = m.p[:, n * T:(n + 1) * T], m.pt[:, (n % 2) * T:(n % 2 + 1) * T]
                        dve.wait_ge(gated, 8 * b + n + 1)
                        if b > 1:
                            dve.wait_ge(added, 8 * (b - 2) + n + 1)
                        nc.vector.tensor_tensor(mix, mix, part, ALU.add).then_inc(added, 1)
                        adds += 1

            cut(0)
            if conv:
                dve.wait_ge(mean, 1)
                for c in range(CCH):
                    nc.vector.tensor_tensor(x(c), x(c), mu, ALU.subtract).then_inc(centred, 1)
            for b in range(len(branches)):
                gate(b, 0)
                gate(b, 1)
                if conv and b == 0:
                    dve.wait_ge(rooted, 2)
                    refined_rsqrt(m, dve, step, 0, var, rstd, rstd, tmp).then_inc(rstd_done, 1)
                    dve.wait_ge(rstd_done, 1)
                    for c in range(CCH):
                        nc.vector.scalar_tensor_tensor(x(c), x(c), m.param("g_ln", 4)[:, c:c + 1], rstd, ALU.mult, ALU.mult)\
                            .then_inc(scaled, 1)
                if conv and b == 1:
                    for c in range(CCH):
                        dve.wait_ge(sig_done, c + 1)
                        nc.vector.scalar_tensor_tensor(x(c), x(c), m.param("b_ln", 4)[:, c:c + 1], sq[:, c, :], ALU.add, ALU.mult)\
                            .then_inc(conv_done, 1)
                gate(b, 2)
                if b + 1 < len(branches):
                    cut(b + 1)
                gate(b, 3)


def mla_project_stage(m):
    nc = m.nc
    base = C1["mla"]
    qm, km, vm = m.q_mla, m.k_mla, m.v_mla
    with stage(m, "chunk_done head_done q_out k_out v_done v_out") as (block, (chunk_done, head_done, q_out, k_out, v_done, v_out)):
        @block.sync
        def _(sp):
            load_ahead_loop(sp, m, base, chunk_done, 1, 6)

        @block.tensor
        def _(pe):
            for h in range(NH):
                if h % 2 == 0:
                    wait_chunk(pe, m, base + h // 2)
                if h >= 4:
                    pe.wait_ge(q_out, h - 3)
                for k in range(3):
                    u = (h % 2) * 3 + k
                    mm = nc.tensor.matmul(m.ps[0:MQK, h % 4, :], slab(m, base + h // 2)[:, u * P:u * P + MQK], m.raw[:, k, :],
                                          start=(k == 0), stop=(k == 2))
                mm.then_inc(chunk_done if h % 2 else head_done, 1)
            wait_chunk(pe, m, base + 4)
            for p in range(4):
                for k in range(2):
                    mm = nc.tensor.matmul(m.ps[:, 4 + p, :], slab(m, base + 4)[:, (2 * p + k) * P:(2 * p + k + 1) * P],
                                          m.raw[:, 3 + k, :], start=(k == 0), stop=(k == 1))
                mm.then_inc(chunk_done if p == 3 else head_done, 1)
            wait_chunk(pe, m, base + 5)
            pe.wait_ge(q_out, NH)
            for t in range(TT):
                for k in range(2):
                    mm = nc.tensor.matmul(m.ps[:, t, :], m.raw[:, 3 + k, t * P:(t + 1) * P],
                                          slab(m, base + 5)[:, k * T:(k + 1) * T], start=(k == 0), stop=(k == 1))
                mm.then_inc(chunk_done if t == TT - 1 else v_done, 1)

        @block.scalar
        def _(act):
            for h in range(NH):
                act.wait_ge(*((chunk_done, h // 2 + 1) if h % 2 else (head_done, h // 2 + 1)))
                nc.scalar.activation(qm[0:MQK, h, :], m.ps[0:MQK, h % 4, :], ACT.Copy).then_inc(q_out, 1)
            for t in range(TT):
                act.wait_ge(*((chunk_done, 6) if t == TT - 1 else (v_done, t + 1)))
                nc.scalar.activation(vm[:, t, :], m.ps[:, t, :], ACT.Copy)

        @block.vector
        def _(dve):
            for p in range(4):
                dve.wait_ge(*((chunk_done, 5) if p == 3 else (head_done, 4 + p + 1)))
                for half in range(2):
                    nc.vector.tensor_copy(km[0:MNOPE, 2 * p + half, :], m.ps[64 * half:64 * half + 64, 4 + p, :])

        @block.gpsimd
        def _(pool):
            for h in range(NH):
                nc.gpsimd.tensor_copy(km[MNOPE:MQK, h, :], m.krope[MNOPE:MQK, :])


def split_terms(m, slot):
    w_hi, w_lo = m.w_hi[:, slot, :], m.w_lo[:, slot, :]
    return ((w_hi, m.a_hi), (w_hi, m.a_lo), (w_lo, m.a_hi))


def token_major(m, out, t, slot, kt, width, weight, first=True, last=True):
    terms = split_terms(m, slot)
    for p, (w, a) in enumerate(terms):
        for n_, k in enumerate(kt):
            mm = m.nc.tensor.matmul(out, a[:, k, t * P:(t + 1) * P], weight(w, k), start=(first and p == 0 and n_ == 0),
                                    stop=(last and p == 2 and n_ == len(kt) - 1))
    return mm


def misc1_stage(m):
    nc = m.nc
    base = C1["misc"]
    rows = m.p[0:24, 0:T]
    with stage(m, "chunk_done hi_ready lo_ready rows_out gates_turned v_done gates_sig") as (block, (
            chunk_done, hi_ready, lo_ready, rows_out, gates_turned, v_done, gates_sig)):
        @block.sync
        def _(sp):
            load_ahead_loop(sp, m, base, lo_ready, 1, 4)

        @block.gpsimd
        def _(pool):
            weights_lo_loop(pool, m, base, hi_ready, lo_ready, 1, 4)

        @block.tensor
        def _(pe):
            pe.sem_inc(chunk_done, 1)
            split_products(pe, m, base, 0, 0, 4, m.ps[:, 0, :], hi_ready, lo_ready).then_inc(chunk_done, 1)
            split_products(pe, m, base, 0, 1, 4, m.ps[:, 1, :], hi_ready, lo_ready).then_inc(chunk_done, 1)
            pe.wait_ge(lo_ready, 4)
            for t in range(TT):
                for half in range(2):
                    mm = token_major(m, m.ps[:, 3 + t, 0:256], t, half, range(4 * half, 4 * half + 4), 256,
                                     lambda w, k: w[:, (k % 4) * 256:(k % 4 + 1) * 256], half == 0, half == 1)
                mm.then_inc(v_done, 1)
                if t == 0:
                    pe.wait_ge(rows_out, 1)
                    for t_ in range(TT):
                        tr = nc.tensor.transpose(m.ps[:, 2, t_ * 24:(t_ + 1) * 24], rows[:, t_ * P:(t_ + 1) * P], m.ident[0:24, 0:24])
                    tr.then_inc(gates_turned, 1)

        @block.scalar
        def _(act):
            for j in range(3):
                weights_hi(act, m, base, 0, j, 4, chunk_done, hi_ready)
            act.wait_ge(chunk_done, 2)
            nc.scalar.activation(m.raw[:, 12, :], m.ps[:, 0, :], ACT.Copy)
            weights_hi(act, m, base, 0, 3, 4, chunk_done, hi_ready)
            act.wait_ge(chunk_done, 3)
            nc.scalar.activation(rows, m.ps[0:24, 1, :], ACT.Copy).then_inc(rows_out, 1)
            nc.scalar.activation(m.krope[64:96, :], m.ps[64:96, 1, :], ACT.Copy)
            act.wait_ge(gates_turned, 1)
            nc.scalar.activation(m.gn, m.ps[:, 2, 0:96], ACT.Sigmoid).then_inc(gates_sig, 1)

        @block.vector
        def _(dve):
            dve.wait_ge(gates_sig, 1)
            gn = m.gn.rearrange("p (t h n) -> p t h n", t=TT, n=3)
            gm = m.gcmp.rearrange("p (t h) -> p t h", t=TT)
            for t in range(TT):
                nc.vector.tensor_scalar(gm[:, t, :], gn[:, t, :, 0], m.con("rowok", 4)[:, t:t + 1], None, ALU.mult)
            for t in range(TT):
                dve.wait_ge(v_done, t + 1)
                nc.vector.tensor_copy(m.v_nsa[:, t, :], m.ps[:, 3 + t, 0:256])


def compress_stage(m, latents):
    nc = m.nc
    base = C1["cmp"]
    kc2 = [m.p[:, 2 * T * w:2 * T * (w + 1)].rearrange("p (g t) -> p g t", g=2) for w in range(2)]
    sq = m.scratch[:, 4 * T:9 * T].rearrange("p (k t) -> p k t", t=T)
    diag = m.spare4[:, 0:2 * T]
    var, root, tmp = m.small[:, 0:2 * TT], m.small[:, 8:8 + 2 * TT], m.small[:, 16:16 + 2 * TT]
    spread = [m.ps[:, 6 + n, :] for n in range(len(latents))]
    first = [sum(len(tiles) for tiles, _, _ in latents[:n]) for n in range(len(latents) + 1)]
    tiles = [tile for part in latents for tile in part[0]]
    with stage(m, "chunk_done keys_shifted values_shifted sig silu squared added summed rooted step inverted diag_done "
                  "spread_done") as (block, (
            chunk_done, keys_shifted, values_shifted, sig, silu, squared, added, summed, rooted, step, inverted, diag_done,
            spread_done)):
        @block.sync
        def _(sp):
            load_ahead_loop(sp, m, base, chunk_done, 1, 6)

        def shift(copy, which, done):
            src = m.raw[:, 11 + which, :]
            for g in range(2):
                copy(kc2[which][0:64, g, :], src[64 * g:64 * g + 64, :]).then_inc(done, 1)
                copy(kc2[which][64:128, g, 0:T - 1], src[64 * g:64 * g + 64, 1:T]).then_inc(done, 1)

        @block.vector
        def _(dve):
            shift(nc.vector.tensor_copy, 0, keys_shifted)
            adds = 0
            for n in range(len(latents)):
                for k in range(first[n] + 1, first[n + 1]):
                    dve.wait_ge(squared, k + 1)
                    if adds:
                        dve.wait_ge(added, adds)
                    nc.vector.tensor_tensor(sq[:, first[n], :], sq[:, first[n], :], sq[:, k, :], ALU.add).then_inc(added, 1)
                    adds += 1
            dve.wait_ge(rooted, 2 * len(latents))
            refined_rsqrt(m, dve, step, 0, var, root, root, tmp).then_inc(inverted, 1)
            dve.wait_ge(inverted, 1)
            for t in range(2 * TT):
                nc.vector.tensor_scalar(diag[:, t * P:(t + 1) * P], m.ident, root[:, t:t + 1], None, ALU.mult).then_inc(diag_done, 1)
            for which in range(2):
                dve.wait_ge(sig, which + 1)
                nc.vector.tensor_tensor(m.hid[:, which, :], m.ps[:, which, 0:62], m.hsig[:, which, :], ALU.mult).then_inc(silu, 1)
            for n, (part, gain, _) in enumerate(latents):
                dve.wait_ge(spread_done, n + 1)
                for k, tile in enumerate(part):
                    nc.vector.scalar_tensor_tensor(tile, tile, gain(k), spread[n], ALU.mult, ALU.mult)
            dve.wait_ge(chunk_done, 6)
            for g in range(2):
                nc.vector.tensor_copy(m.vcmp[0:NCMP, g, :], m.ps[0:NCMP, 3 + g, 0:64])

        @block.tensor
        def _(pe):
            for which, pe_col in enumerate(("pe_k", "pe_v")):
                pe.wait_ge((keys_shifted, values_shifted)[which], 4)
                for p in range(16):
                    if p % 8 == 0:
                        wait_chunk(pe, m, base + 2 * which + p // 8)
                    w = slab(m, base + 2 * which + p // 8)[:, (p % 8) * P:(p % 8 + 1) * P]
                    v = kc2[which].rearrange("p g (j s) -> p g j s", s=CSTRIDE)
                    o = 2 * p // CSTRIDE
                    tok = v[:, :, o:o + NCMP, 2 * p % CSTRIDE]
                    nc.tensor.matmul(m.ps[:, which, 0:62].rearrange("p (g j) -> p g j", g=2), w, tok, start=(p == 0), stop=False)
                    mm = nc.tensor.matmul(m.ps[:, which, 0:62], w, m.param(pe_col, 16)[:, p:p + 1].to_broadcast([P, 62]),
                                          start=False, stop=(p == 15))
                    if p % 8 == 7:
                        mm.then_inc(chunk_done, 1)
                if which == 0:
                    pe.wait_ge(added, first[-1] - len(latents))
                    for n in range(len(latents)):
                        for t in range(TT):
                            mm = nc.tensor.matmul(m.ps[:, 5, n * TT + t:n * TT + t + 1], sq[:, first[n], t * P:(t + 1) * P],
                                                  m.ones[:, 0:1], start=True, stop=True)
                    mm.then_inc(summed, 1)
            for n in range(len(latents)):
                for t in range(TT):
                    pe.wait_ge(diag_done, n * TT + t + 1)
                    mm = nc.tensor.matmul(spread[n][:, t * P:(t + 1) * P], m.ones, diag[:, (n * TT + t) * P:(n * TT + t + 1) * P],
                                          start=True, stop=True)
                mm.then_inc(spread_done, 1)
            for which in range(2):
                pe.wait_ge(silu, which + 1)
                wait_chunk(pe, m, base + 4 + which)
                if which == 0:
                    nc.tensor.matmul(m.ps[0:64, 2, 0:62], slab(m, base + 4)[:, 0:64], m.hid[:, 0, :], start=True, stop=True)\
                        .then_inc(chunk_done, 1)
                else:
                    for g in range(2):
                        mm = nc.tensor.matmul(m.ps[0:NCMP, 3 + g, 0:64], m.hid[:, 1, g * NCMP:(g + 1) * NCMP],
                                              slab(m, base + 5)[:, 0:64], start=True, stop=True)
                    mm.then_inc(chunk_done, 1)

        @block.scalar
        def _(act):
            shift(lambda out, src: nc.scalar.activation(out, src, ACT.Copy), 1, values_shifted)
            for k, tile in enumerate(tiles):
                nc.scalar.activation(sq[:, k, :], tile, ACT.Square).then_inc(squared, 1)
            act.wait_ge(summed, 1)
            for out, func in ((root, ACT.Sqrt), (var, ACT.Identity)):
                for n, (_, _, width) in enumerate(latents):
                    nc.scalar.activation(out[:, n * TT:(n + 1) * TT], m.ps[:, 5, n * TT:(n + 1) * TT], func, bias=m.eps,
                                         scale=1.0 / width).then_inc(rooted, 1)
            for which in range(2):
                act.wait_ge(chunk_done, 2 * which + 2)
                nc.scalar.activation(m.hsig[:, which, :], m.ps[:, which, 0:62], ACT.Sigmoid).then_inc(sig, 1)
            act.wait_ge(chunk_done, 5)
            nc.scalar.activation(m.kcmp[0:64, :], m.ps[0:64, 2, 0:62], ACT.Copy)


def compressed_attention_stage(m):
    nc = m.nc
    W = TT * NCMP
    heads = [0, 2, 4, 6, 1, 3, 5, 7]
    with stage(m, "dup scores masked maxed centred exped summed inverted weighted scaled transposed copied pv_done o_out "
                  "swap_done") as (block, (
            dup, scores, masked, maxed, centred, exped, summed, inverted, weighted, scaled, transposed, copied, pv_done, o_out,
            swap_done)):
        sc = m.p[:, 0:2 * 4 * W].rearrange("p (s w) -> p s w", s=2)
        st = m.small[:, 0:64]
        ptc = m.p[:, 2 * T:4 * T].rearrange("p (s t) -> p s t", s=2)
        mask = m.con("mask_c", W).rearrange("p (o w) -> p o w", o=1).to_broadcast([P, 4, W])
        rows = lambda ap: ap.rearrange("p (r j) -> p r j", j=NCMP)
        each = lambda ap: ap.rearrange("p (r o) -> p r o", o=1).to_broadcast([P, 4 * TT, NCMP])

        @block.gpsimd
        def _(pool):
            n = 0
            for b in range(2):
                for half in (0, 64):
                    nc.gpsimd.tensor_copy(m.swapped[64 - half:128 - half, b, :], m.raw[half:half + 64, 9 + b, :]).then_inc(swap_done, 1)
                    n += 1
                    pool.wait_ge(swap_done, n)

        @block.scalar
        def _(act):
            nc.scalar.activation(m.kcmp[64:128, :], m.kcmp[0:64, :], ACT.Copy).then_inc(dup, 1)
            for g in range(2):
                act.wait_ge(centred, g + 1)
                nc.scalar.activation(sc[:, g, :], sc[:, g, :], ACT.Exp).then_inc(exped, 1)
            for i in range(NH):
                act.wait_ge(transposed, i + 1)
                if i >= 2:
                    act.wait_ge(pv_done, i - 1)
                nc.scalar.activation(ptc[0:NCMP, i % 2, :], m.ps[0:NCMP, 2 + i % 2, :], ACT.Copy).then_inc(copied, 1)

        @block.tensor
        def _(pe):
            pe.wait_ge(dup, 1)
            for i, h in enumerate(heads):
                r0 = 64 * (h % 2)
                for t in range(TT):
                    mm = nc.tensor.matmul(m.ps[:, i // 4, (i % 4) * W + t * NCMP:(i % 4) * W + (t + 1) * NCMP],
                                          m.raw[r0:r0 + 64, 5 + h // 2, t * P:(t + 1) * P],
                                          m.kcmp[r0:r0 + 64, (h // 4) * NCMP:(h // 4 + 1) * NCMP], start=True, stop=True)
                if i % 4 == 3:
                    mm.then_inc(scores, 1)

            def product(i):
                h = heads[i]
                r0 = 64 * (h % 2)
                pe.wait_ge(copied, i + 1)
                nc.tensor.matmul(m.ps[r0:r0 + 64, 4 + h // 2, :], m.vcmp[0:NCMP, h // 4, :], ptc[0:NCMP, i % 2, :],
                                 start=True, stop=True).then_inc(pv_done, 1)

            for i in range(NH):
                if i % 4 == 0:
                    pe.wait_ge(scaled, i // 4 + 1)
                if i >= 2:
                    pe.wait_ge(copied, i - 1)
                for t in range(TT):
                    at = (i % 4) * W + t * NCMP
                    mm = nc.tensor.transpose(m.ps[0:NCMP, 2 + i % 2, t * P:(t + 1) * P], sc[:, i // 4, at:at + NCMP], m.ident)
                mm.then_inc(transposed, 1)
                if i:
                    product(i - 1)
            product(NH - 1)

        @block.vector
        def _(dve):
            for g in range(2):
                s, a = sc[:, g, :], st[:, 32 * g:32 * g + 32]
                top, total = a[:, 0:16], a[:, 16:32]
                dve.wait_ge(scores, g + 1)
                nc.vector.tensor_tensor(s.rearrange("p (h w) -> p h w", h=4), m.ps[:, g, 0:4 * W].rearrange("p (h w) -> p h w", h=4),
                                        mask, ALU.add).then_inc(masked, 1)
                dve.wait_ge(masked, g + 1)
                nc.vector.tensor_reduce(top, rows(s), AX, ALU.max).then_inc(maxed, 1)
                dve.wait_ge(maxed, g + 1)
                nc.vector.tensor_tensor(rows(s), rows(s), each(top), ALU.subtract).then_inc(centred, 1)
            for g in range(2):
                s, a = sc[:, g, :], st[:, 32 * g:32 * g + 32]
                top, total = a[:, 0:16], a[:, 16:32]
                dve.wait_ge(exped, g + 1)
                nc.vector.tensor_reduce(total, rows(s), AX, ALU.add).then_inc(summed, 1)
                dve.wait_ge(summed, g + 1)
                nc.vector.reciprocal(top, total).then_inc(inverted, 1)
                dve.wait_ge(inverted, g + 1)
                gate = m.gcmp.rearrange("p (t h) -> p h t", t=TT)[:, g:NH:2, :]
                head_rows = lambda ap: ap.rearrange("p (h t) -> p h t", h=4)
                nc.vector.tensor_tensor(head_rows(total), head_rows(top), gate, ALU.mult).then_inc(weighted, 1)
                dve.wait_ge(weighted, g + 1)
                nc.vector.tensor_tensor(rows(s), rows(s), each(total), ALU.mult).then_inc(scaled, 1)
            for pair in range(4):
                dve.wait_ge(pv_done, 5 + pair)
                nc.vector.tensor_copy(m.o_nsa[:, pair, :], m.ps[:, 4 + pair, :])


def conv_padded(m):
    return m.p[:, 0:CCH * 544].rearrange("p (c t) -> p c t", c=CCH)


def glu_stage(m):
    up = conv_padded(m)
    bias = m.param("b_glu", 8)

    def gate(c):
        return "act", lambda e, bank, n, act_evac: m.nc.scalar.activation(m.glu[:, c, :], bank, ACT.Sigmoid,
                                                                          bias=bias[:, 4 + c:5 + c])

    def half(c):
        def emit(e, bank, n, act_evac):
            e.wait_ge(act_evac, CCH + c + 1)
            return m.nc.vector.scalar_tensor_tensor(up[:, c, TAPS - 1:TAPS - 1 + T], bank, bias[:, c:c + 1], m.glu[:, c, :],
                                                    ALU.add, ALU.mult)
        return "dve", emit

    def pad(dve):
        for c in range(CCH):
            m.nc.vector.memset(up[:, c, 0:TAPS - 1], 0.0)

    linear_stage(m, C1["glu"], 1, 8, [f(c) for c in range(CCH) for f in (gate, half)], dve_side=pad)


def conv_taps(m, dve, tapped):
    nc = m.nc
    up = conv_padded(m)
    w = m.param("w_dw", CCH * TAPS).rearrange("p (c w) -> p c w", c=CCH)
    for c in range(CCH):
        nc.vector.tensor_scalar(m.conv[:, c, :], up[:, c, 0:T], w[:, c, 0:1], m.param("b_dw", 4)[:, c:c + 1],
                                ALU.mult, ALU.add).then_inc(tapped, 1)
    with dve.Fori(1, TAPS) as i:
        for c in range(CCH):
            dve.wait_ge(tapped, i * CCH + (c + 1 - CCH))
            nc.vector.scalar_tensor_tensor(m.conv[:, c, :], up[:, c, bass.ds(i, T)], w[:, c, bass.ds(i, 1)], m.conv[:, c, :],
                                           ALU.mult, ALU.add).then_inc(tapped, 1)
    dve.wait_ge(tapped, CCH * TAPS)


def first_layer(m, par):
    nc = m.nc

    def copy_act(dst):
        return "act", lambda eng, bank, n, _: m.nc.scalar.activation(dst(n), bank, ACT.Copy)

    def copy_dve(dst):
        return "dve", lambda eng, bank, n, _: m.nc.vector.tensor_copy(dst(n), bank)

    X = lambda k: m.x[:, k, :]
    raw = lambda n: m.raw[:, n, :]
    scratch = lambda k: m.p[:, k * T:(k + 1) * T]
    g_mix, g_ffn, g_cq, g_ckv = (lambda k, g=g: m.param(g, 1 + k)[:, k:k + 1] for g in ("g_mix", "g_ffn", "g_cq", "g_ckv"))
    norm_stage(m, X, KD, D, params=par)
    linear_stage(m, C1["raw"], 3, 4, [copy_act(raw), copy_dve(raw)] * 2, source=scratch, make=normed_tiles(m, scratch, g_mix))
    misc1_stage(m)
    compress_stage(m, [([raw(k) for k in range(3)], g_cq, QRANK), ([raw(3 + k) for k in range(2)], g_ckv, KVRANK)])
    mla_project_stage(m)
    one, two = m.con("select1", 16), m.con("select2", 26)
    row = lambda rows, i, width: m.ident[0:rows, i:i + 1].to_broadcast([rows, width])

    def latent(tile, gain):
        return [(tile[0:MQK, i, :], one[0:MQK, 8 - i:16 - i], [row(NH, i, MQK)], m.param(gain, 1)[0:MQK],
                 m.con("cos_m", T)[0:MQK], m.con("sin_m", T)[0:MQK], SWAP32) for i in range(NH)]

    sparse = [(raw(5 + i), two[:, 12 - 2 * i:25 - 2 * i], [row(13, 2 * i, DH), row(13, 2 * i + 1, DH)],
               m.param("gq_nsa" if i < 4 else "gk_nsa", 1), m.con("cos_n", T), m.con("sin_n", T), SWAP16) for i in range(6)]
    compressed = [(m.kcmp[0:64, :], two[0:64, 0:13], [row(13, 12, DH)], m.param("gk_nsa", 1)[0:64],
                   m.con("cos_c", 62)[0:64], m.con("sin_c", 62)[0:64], SWAP16)]
    rotate_stage(m, [(latent(m.q_mla, "gq_mla"), NH, 1.0, m.con("eps_mla", 1)[0:NH]),
                     (latent(m.k_mla, "gk_mla"), NH, 1.0 / MQK, m.eps[0:NH]),
                     (sparse + compressed, 13, m.con("sum_scale", 1)[0:13], m.con("sum_eps", 1)[0:13])])
    causal = lambda b, qt: (m.causal_bf, qt * P)
    attention_stage(m, 1, lambda j: m.q_mla[0:MQK, j, :], lambda j, b: m.k_mla[0:MQK, j, :],
                    lambda j, b: m.v_mla[:, :, j * DH:(j + 1) * DH], causal, lambda j, b: None, lambda pair: m.o_mla[:, pair, :])
    compressed_attention_stage(m)
    gates = m.gn.rearrange("p (t c) -> p t c", t=TT)
    attention_stage(m, 2, lambda j: m.raw[64 * (j % 2):64 * (j % 2) + 64, 5 + j // 2, :],
                    lambda j, b: (raw(9 + b) if j % 2 == j // 4 else m.swapped[:, b, :])[64 * (j % 2):64 * (j % 2) + 64, :],
                    lambda j, b: m.v_nsa[:, :, b * 128 + (j // 4) * 64:b * 128 + (j // 4) * 64 + 64], causal,
                    lambda j, b: gates[:, :, 3 * j + 1 + b], lambda pair: m.o_nsa[:, pair, :], add=True)
    glu_stage(m)
    linear_stage(m, C1["gate"], 6, 4, [("act", lambda e, bank, n, _: nc.scalar.activation(m.g[:, n, :], bank, ACT.Sigmoid))] * 4,
                 extra="tapped", dve_side=lambda dve, *s: conv_taps(m, dve, *s))
    merge_stage(m, C1["merge"], [(lambda k: m.o_mla[:, k, :], lambda n: m.g[:, n, :], None),
                                 (lambda k: m.o_nsa[:, k, :], lambda n: m.g[:, 16 + n, :], None),
                                 (lambda k: m.conv[:, k, :], lambda n: m.g[:, 8 + n, :],
                                  lambda n: m.param("b_out", 8)[:, n:n + 1])], conv=True)
    add_x = lambda eng, bank, n, _=None: nc.vector.tensor_tensor(m.x[:, n, :], m.x[:, n, :], bank, ALU.add)
    linear_stage(m, C1["wout"], 1, 8, [("dve", add_x)] * 8, source=scratch, extra="squared added", squares=True)
    norm_stage(m, X, KD, D, squared_before=True)
    linear_stage(m, C1["ff_up"], 8, 4, [("act", lambda e, bank, n, _: nc.scalar.activation(m.hidden[:, n, :], bank, ACT.Relu))] * 4,
                 source=scratch, make=normed_tiles(m, scratch, g_ffn),
                 post=lambda dve, n: nc.vector.tensor_tensor(m.hidden[:, n, :], m.hidden[:, n, :], m.hidden[:, n, :], ALU.mult))
    down_stage(m, C1["ff_down"], FF1 // P // 2, lambda n, bank: add_x(None, bank, n), m.layer, 0)


def position_stage(m, tri, pos):
    nc = m.nc
    turn = 2 * np.pi
    c1 = 6.28125
    c2 = float(np.round((turn - c1) * 2.0 ** 21) / 2.0 ** 21)
    c3 = float(turn - c1 - c2)
    magic = 1.5 * 2.0 ** 23
    lim = 3.1415925
    ang, n_, r, rc = (m.p[:, k * T:(k + 1) * T] for k in range(4))
    posi = m.p[:, 4 * T:5 * T].bitcast(I32)
    cos, sin = m.con("cos_n", T), m.con("sin_n", T)
    with stage(m, "pos_loaded step args lut") as (block, (pos_loaded, step, args, lut)):
        @block.sync
        def _(sp):
            sp.dma_start(posi, pos.to_broadcast([P, T])).then_inc(pos_loaded, 16)
            sp.dma_start(m.con("cos_m", T), tri).then_inc(pos_loaded, 16)
            sp.wait_ge(pos_loaded, 32)

        @block.vector
        def _(dve):
            done = 0

            def then(ins):
                nonlocal done
                ins.then_inc(step, 1)
                done += 1
                dve.wait_ge(step, done)

            dve.wait_ge(pos_loaded, 32)
            then(nc.vector.tensor_copy(ang, posi))
            then(nc.vector.tensor_scalar(ang, ang, m.con("invf", 1), None, ALU.mult))
            then(nc.vector.tensor_scalar(n_, ang, 1.0 / turn, magic, ALU.mult, ALU.add))
            then(nc.vector.tensor_scalar(n_, n_, magic, None, ALU.subtract))
            then(nc.vector.scalar_tensor_tensor(r, n_, -c1, ang, ALU.mult, ALU.add))
            then(nc.vector.scalar_tensor_tensor(r, n_, -c2, r, ALU.mult, ALU.add))
            then(nc.vector.scalar_tensor_tensor(r, n_, -c3, r, ALU.mult, ALU.add))
            then(nc.vector.tensor_scalar(rc, r, np.pi / 2, None, ALU.add))
            then(nc.vector.tensor_scalar(ang, rc, np.pi, -turn, ALU.is_gt, ALU.mult))
            then(nc.vector.tensor_tensor(rc, rc, ang, ALU.add))
            then(nc.vector.tensor_scalar(rc, rc, lim, -lim, ALU.min, ALU.max))
            then(nc.vector.tensor_scalar(r, r, lim, -lim, ALU.min, ALU.max))
            nc.vector.tensor_scalar(r, r, 1.0, None, ALU.mult).then_inc(args, 1)
            dve.wait_ge(lut, 2)
            then(nc.vector.tensor_scalar(sin, sin, m.con("sgn", 1), None, ALU.mult))
            then(nc.vector.tensor_scalar(cos, cos, m.con("rotm", 1), m.con("unrot", 1), ALU.mult, ALU.add))

        @block.scalar
        def _(act):
            act.wait_ge(args, 1)
            nc.scalar.activation(sin, r, ACT.Sin).then_inc(lut, 1)
            nc.scalar.activation(cos, rc, ACT.Sin).then_inc(lut, 1)



def column(w, f):
    return w[:, f:f + 1] if isinstance(f, int) else w[:, bass.ds(f, 1)]


def add_modulation(m, dve, acc, weights, k, c, mod_added):
    dve.wait_ge(mod_added, c + 1)
    m.nc.vector.scalar_tensor_tensor(acc, weights, column(m.con("cvec", KD), k), acc, ALU.mult, ALU.add).then_inc(mod_added, 1)


def over_partitions(m, accs, bank):
    for q, acc in enumerate(accs):
        for n in range(KD):
            mm = m.nc.tensor.matmul(m.ps[:, bank, KD * q + n:KD * q + n + 1], unit_tile(acc, n), m.ones[:, 0:1], start=True, stop=True)
    return mm


def bias_modulation(m, dve, first, count, bank, gain, scale, mod_summed, mod_biased):
    nc = m.nc
    dve.wait_ge(mod_summed, 1)
    mod = m.mod[:, KD * first:KD * (first + count)]
    nc.vector.tensor_tensor(mod, m.ps[:, bank, 0:KD * count], m.param("mod_b", 48)[:, KD * first:KD * (first + count)], ALU.add)\
        .then_inc(mod_biased, 1)
    dve.wait_ge(mod_biased, 1)
    a = 0 if gain == "g1" else 1
    nc.vector.scalar_tensor_tensor(m.gains[:, KD * a:KD * (a + 1)], m.mod[:, KD * scale:KD * (scale + 1)], 1.0, m.param(gain, KD),
                                   ALU.add, ALU.mult).then_inc(mod_biased, 1)


def rest_sync(m, sp, i, j, mod_added):
    for s in range(2):
        slot = (2 * j + s) % 4
        sp.wait_ge(mod_added, i * 8 + 2 * j + s + 1)
        sp.dma_start(m.mod_slots[:, slot, :], m.modw[m.layer * (4 * KD) + i * 8 + (2 * j + s)]).then_inc(m.mod_landed[slot], 16)


def rest_vector(m, dve, mod_added, *_):
    for q in range(4):
        m.nc.vector.memset(m.mod_accs[:, q, :], 0.0).then_inc(mod_added, 1)
    with dve.Fori(0, 4) as i:
        for c in range(8):
            dve.wait_ge(m.mod_landed[c % 4], m.layer * (16 * 8) + i * 32 + (c // 4) * 16 + 16)
            add_modulation(m, dve, m.mod_accs[:, c % 4, :], m.mod_slots[:, c % 4, :], i * 2 + c // 4, i * 8 + c, mod_added)


def misc2_stage(m):
    nc = m.nc
    base = C2["misc"]
    W = DH + 2 * NH
    rows = m.p[0:W, 0:T]
    with stage(m, "chunk_done hi_ready lo_ready rows_out turned") as (block, (chunk_done, hi_ready, lo_ready, rows_out, turned)):
        @block.sync
        def _(sp):
            load_ahead_loop(sp, m, base, lo_ready, 1, 2)

        @block.gpsimd
        def _(pool):
            weights_lo_loop(pool, m, base, hi_ready, lo_ready, 1, 2)

        @block.tensor
        def _(pe):
            pe.sem_inc(chunk_done, 1)
            split_products(pe, m, base, 0, 1, 2, m.ps[:, 1, :], hi_ready, lo_ready).then_inc(chunk_done, 1)
            split_products(pe, m, base, 0, 0, 2, m.ps[:, 0, :], hi_ready, lo_ready).then_inc(chunk_done, 1)
            pe.wait_ge(rows_out, 1)
            for t in range(TT):
                tr = nc.tensor.transpose(m.ps[:, 2, t * W:(t + 1) * W], rows[:, t * P:(t + 1) * P], m.ident[0:W, 0:W])
            tr.then_inc(turned, 1)

        @block.scalar
        def _(act):
            for j in range(2):
                weights_hi(act, m, base, 0, j, 2, chunk_done, hi_ready)
            act.wait_ge(chunk_done, 2)
            nc.scalar.activation(rows, m.ps[0:W, 1, :], ACT.Copy).then_inc(rows_out, 1)
            act.wait_ge(chunk_done, 3)
            for half in (0, 64):
                nc.scalar.activation(m.raw[half:half + 64, 8, :], m.ps[0:64, 0, :], ACT.Copy)
                nc.scalar.activation(m.raw[half:half + 64, 9, :], m.ps[64:128, 0, :], ACT.Copy)

        @block.vector
        def _(dve):
            dve.wait_ge(turned, 1)
            out = m.ps[:, 2, 0:TT * W].rearrange("p (t w) -> p t w", t=TT)
            tokens = lambda a: a.rearrange("p (t w) -> p t w", t=TT)
            nc.vector.tensor_copy(tokens(m.va), out[:, :, 0:DH])
            nc.vector.tensor_tensor(tokens(m.logf), out[:, :, DH:DH + NH], tokens(m.param("fbias", 32)), ALU.add)
            nc.vector.tensor_scalar(tokens(m.wi), out[:, :, DH + NH:W], float(NH) ** -0.5, None, ALU.mult)


def index_stage(m):
    nc = m.nc
    relu = m.p[:, 0:4 * T].rearrange("p (s t) -> p s t", s=4)
    cum = m.p[:, 4 * T:6 * T].rearrange("p (s t) -> p s t", s=2)
    neg, absx, low, ex = (m.small[:, 192 + 16 * 0:224], m.small[:, 224:256], m.small[:, 0:32], m.small[:, 32:64])
    work = m.work
    order = [(h, qt) for h in range(NH) for qt in range(1, TT)]
    CUM = 3
    with stage(m, "step log_exp logf_done summed cum_done filled rows_set started scored rectified") as (block, (
            step, log_exp, logf_done, summed, cum_done, filled, rows_set, started, scored, rectified)):
        @block.gpsimd
        def _(pool):
            nc.gpsimd.memset(m.qf[64:96, :, :], 0.0).then_inc(filled, 1)
            nc.gpsimd.memset(m.qf[96:97, :, :], 1.0).then_inc(filled, 1)
            nc.gpsimd.memset(m.kf[64:96, :, :], 0.0).then_inc(filled, 1)
            pool.wait_ge(filled, 3)
            nc.gpsimd.memset(m.kf[64:65, :, :], 1.0).then_inc(filled, 1)

        @block.sync
        def _(sp):
            sp.wait_ge(cum_done, 2)
            sp.wait_ge(filled, 4)
            for h in range(NH):
                sp.dma_start(m.qf[64:65, h, :], cum[h:h + 1, 0, :]).then_inc(rows_set, 16)
                sp.dma_start(m.kf[96:97, h, :], cum[h:h + 1, 1, :]).then_inc(rows_set, 16)
            sp.wait_ge(rows_set, 16 * 2 * NH)

        @block.scalar
        def _(act):
            use_log_exp(m)
            act.wait_ge(step, 2)
            nc.scalar.activation(ex, absx, ACT.Exp, scale=-1.0).then_inc(log_exp, 1)
            act.wait_ge(log_exp, 1)
            nc.scalar.activation(ex, ex, ACT.Ln, bias=1.0).then_inc(log_exp, 1)
            for n_, (h, qt) in enumerate(order):
                w = P * (qt + 1)
                act.wait_ge(scored, n_ + 1)
                if n_ >= 4:
                    act.wait_ge(started, 3 + n_ - 3)
                nc.scalar.activation(relu[:, n_ % 4, 0:w], m.ps[:, n_ % 4, 0:w], ACT.Relu, scale=float(DH) ** -0.5)\
                    .then_inc(rectified, 1)
                if n_ == CUM + 2:
                    act.wait_ge(summed, 1)
                    nc.scalar.activation(cum[0:NH, 0, :], m.ps[0:NH, 4, :], ACT.Copy).then_inc(cum_done, 1)
                    nc.scalar.activation(cum[0:NH, 1, :], m.ps[0:NH, 4, :], ACT.Copy, scale=-1.0).then_inc(cum_done, 1)

        @block.vector
        def _(dve):
            nc.vector.tensor_scalar(neg, m.logf, -1.0, None, ALU.mult).then_inc(step, 1)
            dve.wait_ge(step, 1)
            nc.vector.tensor_tensor(absx, neg, m.logf, ALU.max).then_inc(step, 1)
            nc.vector.tensor_scalar(low, neg, 0.0, None, ALU.max).then_inc(step, 1)
            dve.wait_ge(log_exp, 2)
            dve.wait_ge(step, 3)
            nc.vector.tensor_tensor(low, low, ex, ALU.add).then_inc(step, 1)
            dve.wait_ge(step, 4)
            nc.vector.tensor_scalar(m.logf, low, -1.0, None, ALU.mult).then_inc(logf_done, 1)
            for qt in range(1, TT):
                nc.vector.memset(work[qt][:, 0:qt * P], 0.0)
                nc.vector.tensor_copy(work[qt][:, qt * P:(qt + 1) * P], m.con("chunkmask", P)).then_inc(started, 1)
            for n_, (h, qt) in enumerate(order):
                w = P * (qt + 1)
                dve.wait_ge(rectified, n_ + 1)
                dve.wait_ge(started, n_ + 1)
                nc.vector.scalar_tensor_tensor(work[qt], relu[:, n_ % 4, 0:w], m.wi[:, qt * NH + h:qt * NH + h + 1], work[qt],
                                               ALU.mult, ALU.add).then_inc(started, 1)

        @block.tensor
        def _(pe):
            for n_, (h, qt) in enumerate(order):
                w, r0 = P * (qt + 1), 64 * (h % 2)
                if n_ >= 4:
                    pe.wait_ge(rectified, n_ - 3)
                nc.tensor.matmul(m.ps[:, n_ % 4, 0:w], m.raw[r0:r0 + 64, 4 + h // 2, qt * P:(qt + 1) * P],
                                 m.raw[r0:r0 + 64, 9, 0:w], start=True, stop=True).then_inc(scored, 1)
                if n_ == CUM:
                    pe.wait_ge(logf_done, 1)
                    for t in range(TT):
                        mm = nc.tensor.matmul(m.ps[0:NH, 4, t * P:T], m.logf[:, t * NH:(t + 1) * NH], m.tri[:, 0:T - t * P],
                                              start=(t == 0), stop=(t == TT - 1))
                    mm.then_inc(summed, 1)


TAKEN = -3e38


def select_topk(m, dve, rounds, last, top8, replaced, marked):
    nc = m.nc
    best = m.small[:, 0:24]
    dve.sem_inc(replaced, 3)
    with dve.Fori(0, rounds) as r:
        dve.wait_ge(replaced, r * 3 + 3)
        hold(dve, m)
        for qt in range(1, TT):
            nc.vector.max(best[:, 8 * (qt - 1):8 * qt], m.work[qt]).then_inc(top8, 1)
        dve.wait_ge(top8, r * 3 + 3)
        hold(dve, m)
        for qt in range(1, TT):
            nc.vector.match_replace(m.work[qt], best[:, 8 * (qt - 1):8 * qt], m.work[qt], TAKEN).then_inc(replaced, 1)
    dve.wait_ge(replaced, 3 * rounds + 3)
    if not last:
        return
    nc.vector.tensor_copy(m.select_bf[0], m.con("chunkmask", P)).then_inc(marked, 1)
    for qt in range(1, TT):
        nc.vector.tensor_scalar(m.select_bf[qt], m.work[qt], TAKEN / 2, NEG, ALU.is_ge, ALU.mult).then_inc(marked, 1)


def forget_values_stage(m, turned):
    nc = m.nc
    base = C2["fox"] + 8
    cos, sin = m.con("cos_n", T), m.con("sin_n", T)
    swap = [m.p[:, k * T:(k + 1) * T] for k in range(len(turned))]
    with stage(m, "chunk_done hi_ready lo_ready swapped cos_done sin_done top8 replaced marked") as (block, (
            chunk_done, hi_ready, lo_ready, swapped, cos_done, sin_done, *select)):
        @block.vector
        def _(dve):
            for k, tile in enumerate(turned):
                nc.vector.stream_shuffle(swap[k], tile, SWAP16).then_inc(swapped, 1)
                nc.vector.tensor_tensor(tile, tile, cos, ALU.mult).then_inc(cos_done, 1)
            select_topk(m, dve, 5, True, *select)
            for k, tile in enumerate(turned):
                dve.wait_ge(cos_done, k + 1)
                dve.wait_ge(sin_done, k + 1)
                nc.vector.tensor_tensor(tile, tile, swap[k], ALU.add)

        @block.sync
        def _(sp):
            load_ahead_loop(sp, m, base, lo_ready, 1, 4)

        @block.gpsimd
        def _(pool):
            for j in range(4):
                weights_lo(pool, m, base, 0, j, 4, hi_ready, lo_ready)
                for k in range(2 * j - 1, min(2 * j + 1, len(turned))):
                    if k >= 0:
                        pool.wait_ge(swapped, k + 1)
                        nc.gpsimd.tensor_tensor(swap[k], swap[k], sin, ALU.mult).then_inc(sin_done, 1)

        @block.tensor
        def _(pe):
            pe.sem_inc(chunk_done, 1)
            for c in range(4):
                pe.wait_ge(lo_ready, c + 1)
                for t in range(TT):
                    mm = token_major(m, m.ps[:, t, :], t, c % 2, (2 * c, 2 * c + 1), T,
                                     lambda w, k: w[:, (k % 2) * T:(k % 2 + 1) * T], c == 0, c == 3)
                mm.then_inc(chunk_done, 1)

        @block.scalar
        def _(act):
            for j in range(4):
                weights_hi(act, m, base, 0, j, 4, chunk_done, hi_ready)
            act.wait_ge(chunk_done, 5)
            for t in range(TT):
                nc.scalar.activation(m.v_fox[:, t, :], m.ps[:, t, :], ACT.Copy)


def gated_up_stage(m, source, make):
    nc = m.nc
    base = C2["ff_up"]
    W = T + 2
    u = m.scratch[:, 0:4 * W].rearrange("p (s t) -> p s t", s=4)
    acc = m.scratch[:, 4 * W:4 * W + 4 * T].rearrange("p (s t) -> p s t", s=4)
    sig = m.scratch[:, 4 * W + 4 * T:4 * W + 6 * T].rearrange("p (s t) -> p s t", s=2)
    cw = m.param("conv_w", 132)
    cb = m.param("conv_b", 44)
    with stage(m, "chunk_done hi_ready lo_ready made src_hi src_lo zeroed copied tap1 tap2 tap3 sig_done half_done pair_done") as (block, (
            chunk_done, hi_ready, lo_ready, made, src_hi, src_lo, zeroed, copied, tap1, tap2, tap3, sig_done, half_done, pair_done)):
        @block.sync
        def _(sp):
            load_ahead_loop(sp, m, base, lo_ready, 11, 4)

        @block.gpsimd
        def _(pool):
            weights_lo_loop(pool, m, base, hi_ready, lo_ready, 11, 4)

        @block.tensor
        def _(pe):
            pe.sem_inc(chunk_done, 1)
            with pe.Fori(0, 11) as i:
                for s in range(4):
                    pe.wait_ge(copied, i * 4 + s + 1)
                    split_products(pe, m, base, i, s, 4, m.ps[:, s, :], hi_ready, lo_ready,
                                   (src_hi, src_lo) if s == 0 else None).then_inc(chunk_done, 1)

        @block.scalar
        def _(act):
            weights_hi(act, m, base, 0, 0, 4, chunk_done, hi_ready)
            split_source_hi(act, m, source, make, made, src_hi)
            act.sem_inc(copied, 4)
            act.wait_ge(zeroed, 1)

            def sigmoid(i, p):
                act.wait_ge(tap3, i * 4 + 2 * p + 5)
                nc.scalar.activation(sig[:, p, :], acc[:, 2 * p, :], ACT.Sigmoid).then_inc(sig_done, 1)

            def turn(i, first):
                for s in range(4):
                    weights_hi(act, m, base, i, s + 1, 4, chunk_done, hi_ready)
                    act.wait_ge(chunk_done, i * 4 + s + 2)
                    act.wait_ge(tap3, i * 4 + s + 1)
                    nc.scalar.activation(u[:, s, 2:W], m.ps[:, s, :], ACT.Copy).then_inc(copied, 1)
                    if s == 1 and not first:
                        sigmoid(i - 1, 1)
                    if s == 3:
                        sigmoid(i, 0)

            turn(0, True)
            with act.Fori(1, 11) as i:
                turn(i, False)
            sigmoid(10, 1)

        @block.vector
        def _(dve):
            dve.sem_inc(tap3, 4)
            nc.vector.memset(u[:, :, 0:2], 0.0).then_inc(zeroed, 1)
            split_source_lo(dve, m, source, make, made, src_hi, src_lo)

            def out(i, p):
                if isinstance(i, int):
                    return m.hidden[:, 2 * i + p, :]
                return m.hidden[:, bass.ds(i * 2 + p, 1), :].rearrange("p o t -> p (o t)")

            def finish(i, p):
                dve.wait_ge(sig_done, i * 2 + p + 1)
                dve.wait_ge(half_done, i * 2 + p + 1)
                nc.vector.tensor_tensor(out(i, p), out(i, p), sig[:, p, :], ALU.mult).then_inc(pair_done, 1)

            def turn(i, first):
                for p in range(2):
                    for s in (2 * p, 2 * p + 1):
                        f = i * 2 + (p + NF2 * (s % 2))
                        if s % 2 == 0 and not first:
                            dve.wait_ge(sig_done, i * 2 + p - 1)
                        dve.wait_ge(copied, i * 4 + s + 5)
                        nc.vector.tensor_scalar(acc[:, s, :], u[:, s, 2:W], column(cw, f + 88), column(cb, f),
                                                ALU.mult, ALU.add).then_inc(tap1, 1)
                    for s in (2 * p, 2 * p + 1):
                        f = i * 2 + (p + NF2 * (s % 2))
                        dve.wait_ge(tap1, i * 4 + s + 1)
                        nc.vector.scalar_tensor_tensor(acc[:, s, :], u[:, s, 1:W - 1], column(cw, f + 44), acc[:, s, :],
                                                       ALU.mult, ALU.add).then_inc(tap2, 1)
                    for s in (2 * p, 2 * p + 1):
                        f = i * 2 + (p + NF2 * (s % 2))
                        dve.wait_ge(tap2, i * 4 + s + 1)
                        nc.vector.scalar_tensor_tensor(acc[:, s, :], u[:, s, 0:T], column(cw, f), acc[:, s, :],
                                                       ALU.mult, ALU.add).then_inc(tap3, 1)
                    dve.wait_ge(tap3, i * 4 + 2 * p + 6)
                    nc.vector.tensor_tensor(out(i, p), acc[:, 2 * p, :], acc[:, 2 * p + 1, :], ALU.mult).then_inc(half_done, 1)
                    if p:
                        finish(i, 0)
                    elif not first:
                        finish(i - 1, 1)

            turn(0, True)
            with dve.Fori(1, 11) as i:
                turn(i, False)
            finish(10, 1)


def second_layer(m, par):
    nc = m.nc
    X = lambda k: m.x[:, k, :]
    scratch = lambda k: m.p[:, k * T:(k + 1) * T]
    spare = lambda k: m.o[:, k, :]
    raw = lambda n: m.raw[:, n, :]
    mod = lambda part: lambda k: m.mod[:, 8 * part + k:8 * part + k + 1]
    gain = lambda a: lambda k: m.gains[:, 8 * a + k:8 * a + k + 1]

    def gated_add(part):
        return lambda e, bank, n, _=None: nc.vector.scalar_tensor_tensor(m.x[:, n, :], bank, column(m.mod, n + 8 * part), m.x[:, n, :],
                                                                 ALU.mult, ALU.add)

    norm_stage(m, X, KD, D, modulate=True, params=par)
    linear_stage(m, C2["raw"], 1, 8,
                 [("act", lambda e, bank, n, _: nc.scalar.activation(raw(n), bank, ACT.Copy, scale=float(DH) ** -0.5 if n < 4 else 1.0)),
                  ("dve", lambda e, bank, n, _: (nc.vector.tensor_scalar(raw(n), bank, float(DH) ** -0.5, None, ALU.mult) if n < 4
                                                 else nc.vector.tensor_copy(raw(n), bank)))] * 4,
                 source=scratch, make=normed_tiles(m, scratch, gain(0), mod(0)))
    misc2_stage(m)
    rotate_stage(m, [([(raw(t), None, None, None, m.con("cos_n", T), m.con("sin_n", T), SWAP16) for t in (4, 5, 6, 7, 9)],
                      None, None, None)])
    index_stage(m)

    def split_heads(n):
        dst = m.qf if n < 4 else m.kf

        def emit(eng, bank, n_, act_evac):
            for half in range(2):
                r = nc.scalar.activation(dst[0:DH, 2 * (n % 4) + half, :], bank[64 * half:64 * half + 64, :], ACT.Copy,
                                         scale=float(DH) ** -0.5 if n < 4 else 1.0)
            return r
        return ("act", emit)

    linear_stage(m, C2["fox"], 1, 8, [split_heads(n) for n in range(8)],
                 extra="top8 replaced marked", dve_side=lambda dve, *s: select_topk(m, dve, TOPK // 8 - 5, False, *s))
    forget_values_stage(m, [raw(t) for t in (0, 1, 2, 3, 8)])
    attention_stage(m, 1, lambda j: m.raw[64 * (j % 2):64 * (j % 2) + 64, j // 2, :],
                    lambda j, b: m.raw[64 * (j % 2):64 * (j % 2) + 64, 8, :],
                    lambda j, b: m.va.rearrange("p (t d) -> p t d", t=TT), lambda b, qt: (m.select_bf[qt], 0),
                    lambda j, b: None, lambda pair: m.o_mla[:, pair, :])
    attention_stage(m, 1, lambda j: m.qf[0:97, j, :], lambda j, b: m.kf[0:97, j, :],
                    lambda j, b: m.v_fox[:, :, j * DH:(j + 1) * DH], lambda b, qt: (m.causal_bf, qt * P),
                    lambda j, b: None, lambda pair: m.o_nsa[:, pair, :])

    def rest_tensor(pe, mod_added, mod_summed, mod_biased):
        pe.wait_ge(mod_added, 4 + 4 * KD)
        over_partitions(m, [m.mod_accs[:, q, :] for q in range(4)], 4).then_inc(mod_summed, 1)

    linear_stage(m, C2["gate"], 4, 4, [("act", lambda e, bank, n, _: nc.scalar.activation(m.gates2[:, n, :], bank, ACT.Sigmoid))] * 4,
                 extra="mod_added mod_summed mod_biased", dve_side=lambda dve, *side: rest_vector(m, dve, *side),
                 sync_side=lambda sp, i, j, mod_added, *_: rest_sync(m, sp, i, j, mod_added), pe_last=rest_tensor,
                 dve_last=lambda dve, _, mod_summed, mod_biased: bias_modulation(m, dve, 2, 4, 4, "g2", 4, mod_summed, mod_biased))
    merge_stage(m, C2["merge"], [(lambda k: m.o_mla[:, k, :], lambda n: m.gates2[:, n, :], None),
                                 (lambda k: m.o_nsa[:, k, :], lambda n: m.gates2[:, 8 + n, :], None)])
    linear_stage(m, C2["wout"], 1, 8, [("dve", gated_add(2))] * 8, source=scratch, extra="squared added", squares=True)
    norm_stage(m, X, KD, D, squared_before=True)
    gated_up_stage(m, spare, normed_tiles(m, spare, gain(1), mod(3)))
    down_stage(m, C2["ff_down"], NF2 // 2, lambda n, bank: gated_add(5)(None, bank, n), m.layer + DEPTH, m.layer * (2 * KD) + 2 * KD)


def second_stack(m, par, tri, pos, view, tiles):
    m.param = lambda name, w: view("par", PAR2[name], w)
    m.per_layer, m.stream_base = NC2, BASE2
    m.tri = m.con("cos_m", T)
    m.va = view("vs", 1024, 256)
    m.mod, m.gains = view("small", 64, 48), view("small", 112, 16)
    m.wi, m.logf = view("small", 128, 32), view("small", 160, 32)
    m.raw = tiles("body", 0, 10)
    m.qf, m.kf = tiles("body", 10 * T, 8), tiles("body", 18 * T, 8)
    m.v_fox = tiles("body", 4 * T, TT)
    m.gates2 = tiles("body", 0, 16)
    m.work = {1: view("o", 0, 256), 2: view("o", T, 384), 3: view("o", 2 * T, 512)}
    bits = view("extra", 0, 640).bitcast(BF16)
    m.select_bf = {0: bits[:, 0:128], 1: bits[:, 128:384], 2: bits[:, 384:768], 3: bits[:, 768:1280]}
    position_stage(m, tri, pos)
    zero_used(m)
    with m.nc.Fori(0, DEPTH) as layer:
        m.layer = layer
        second_layer(m, par)
        zero_used(m)
    norm_stage(m, lambda k: m.x[:, k, :], KD, D, lambda k: m.hidden[:, k, :], lambda k: m.con("final_g", 8)[:, k:k + 1])


def build(nc, wstream, modw_first, modw, par1, par2, con, causal, tri, vecs, pos, xT, outT, upto=None):
    with ExitStack() as ctx:
        arena = ctx.enter_context(nc.sbuf_tensor("arena", [P, NARENA], F32))
        w_hi, w_lo = (ctx.enter_context(nc.sbuf_tensor(n_, [P, 2, CHUNK], F32R)) for n_ in ("weights_hi", "weights_lo"))
        a_hi, a_lo = (ctx.enter_context(nc.sbuf_tensor(n_, [P, KD, T], F32R)) for n_ in ("moving_hi", "moving_lo"))
        ps = ctx.enter_context(nc.psum_tensor("ps", [P, 8, T], F32))
        landed = [ctx.enter_context(nc.semaphore(f"weights_landed{s}")) for s in range(RING)]
        mod_landed = [ctx.enter_context(nc.semaphore(f"modulation_landed{s}")) for s in range(4)]
        mod_first_landed = [ctx.enter_context(nc.semaphore(f"first_modulation_landed{s}")) for s in range(2)]
        loaded = ctx.enter_context(nc.semaphore("inputs_loaded"))
        cast = ctx.enter_context(nc.semaphore("masks_cast"))
        passed = ctx.enter_context(nc.semaphore("waits_passed"))
        stored = ctx.enter_context(nc.semaphore("output_stored"))

        def view(name, off, w):
            return arena[:, AR[name] + off:AR[name] + off + w]

        def tiles(name, off, n, w=T):
            return view(name, off, n * w).rearrange("p (k t) -> p k t", t=w)

        m = Program()
        m.nc, m.wstream, m.landed, m.passed = nc, wstream, landed, passed
        m.modw, m.mod_landed = modw, mod_landed
        m.modw_first, m.mod_first_landed = modw_first, mod_first_landed
        m.used, m.parity = None, 0
        m.mod_slots, m.mod_accs = tiles("p", 0, 4, CHUNK), tiles("qs", 0, 4, CHUNK)
        m.ps = ps[:, :, :]
        m.ring = tiles("ring", 0, RING, CHUNK)
        m.x = tiles("x", 0, KD)
        m.hidden = tiles("body", 0, 36)
        m.w_hi, m.w_lo, m.a_hi, m.a_lo = w_hi[:, :, :], w_lo[:, :, :], a_hi[:, :, :], a_lo[:, :, :]
        m.p, m.pt = view("p", 0, 8 * T), view("pt", 0, 1280)
        m.par = view("par", 0, NPAR)
        m.con = lambda name, w: view("con", CON[name], w)
        m.ident, m.ones, m.bd64 = m.con("ident", P), m.con("ones", P), m.con("bd64", P)
        m.eps = m.con("eps", 1)
        m.ident_bf = view("idb", 0, 64).bitcast(BF16)
        m.causal_bf = view("caub", 0, 64).bitcast(BF16)
        m.small = view("small", 0, 256)

        m.scratch = view("p", 0, 8 * T + 1280)
        m.rstd = ps[:, 7, :]
        m.spare4 = view("qs", 0, 8 * T)
        m.param = lambda name, w: view("par", PAR1[name], w)
        at = AR["body"] - 5 * T
        m.raw = arena[:, at:at + 13 * T].rearrange("p (k t) -> p k t", t=T)
        m.q_mla, m.k_mla = tiles("body", 6 * T, 8), tiles("body", 14 * T, 8)
        m.v_mla, m.v_nsa = tiles("body", 22 * T, TT), tiles("body", 26 * T, TT, 256)
        m.g, m.conv = tiles("body", 0, 24), tiles("body", 24 * T, CCH)
        m.glu = tiles("qs", 0, CCH)
        m.swapped = tiles("qs", 0, 2)
        m.o = tiles("o", 0, 8)
        m.o_mla, m.o_nsa = tiles("o", 0, 4), tiles("o", 4 * T, 4)
        m.gn, m.gcmp = view("small", 64, 96), view("small", 160, 32)
        m.hid, m.hsig = tiles("extra", 0, 2, 62), tiles("extra", 124, 2, 62)
        m.kcmp, m.vcmp = view("extra", 248, 62), tiles("extra", 310, 2, 64)
        m.krope = view("o", 0, T)

        with nc.Block() as block:
            @block.sync
            def _(sp):
                sp.dma_start(m.x, xT.rearrange("(k p) t -> p k t", p=P)).then_inc(loaded, 16)
                sp.dma_start(view("con", 0, NCON - 2 * KD), con[:, 0:NCON - 2 * KD]).then_inc(loaded, 16)
                sp.dma_start(m.con("final_g", 2 * KD), vecs).then_inc(loaded, 16)
                sp.dma_start(m.pt[:, 0:P], causal).then_inc(loaded, 16)
                for c in range(RING):
                    sp.dma_start(m.ring[:, c, :], wstream[c]).then_inc(landed[c], 16)

            @block.vector
            def _(dve):
                dve.wait_ge(loaded, 64)
                nc.vector.tensor_copy(m.ident_bf, m.ident).then_inc(cast, 1)
                nc.vector.tensor_copy(m.causal_bf, m.pt[:, 0:P]).then_inc(cast, 1)
                dve.wait_ge(cast, 2)

        m.per_layer, m.stream_base = NC1, 0
        with nc.Fori(0, DEPTH) as layer:
            m.layer = layer
            first_layer(m, par1)
            zero_used(m)
        if upto != "first":
            second_stack(m, par2, tri, pos, view, tiles)
        zero_used(m)
        with nc.Block() as block:
            @block.sync
            def _(sp):
                res = m.x if upto == "first" else m.hidden[:, 0:KD, :]
                sp.dma_start(outT.rearrange("(k p) t -> p k t", p=P), res).then_inc(stored, 16)
                sp.wait_ge(stored, 16)
                for s in range(RING):
                    if upto != "first":
                        sp.wait_ge(landed[s], 16 * (NCHUNKS // RING + 1))


def constants():
    f = np.float32
    c = np.zeros((P, NCON), f)

    def put(name, a):
        a = np.asarray(a, f)
        c[:a.shape[0], CON[name]:CON[name] + a.shape[1]] = a

    put("ident", np.eye(P))
    put("ones", np.ones((P, P)))
    put("bd64", np.kron(np.eye(2), np.ones((64, 64))))
    s = np.arange(P)[:, None]
    put("chunkmask", np.where(np.arange(P)[None, :] // 64 <= s // 64, 0.0, NEG))

    def table(rot, pos):
        half = rot // 2
        inv = np.power(f(500000.0), -np.arange(half, dtype=f) * f(2.0 / rot)).astype(f)
        ang = (pos.astype(f)[:, None] * inv).astype(f)
        return np.cos(ang).T, np.sin(ang).T

    def rows(head, at, rot, pos):
        co, si = np.ones((head, len(pos)), f), np.zeros((head, len(pos)), f)
        a, b = table(rot, pos)
        h = rot // 2
        co[at:at + h], co[at + h:at + rot] = a, a
        si[at:at + h], si[at + h:at + rot] = -b, b
        return co, si

    co, si = rows(MQK, MNOPE, MROPE, np.arange(T))
    put("cos_m", co)
    put("sin_m", si)
    co, si = rows(DH, 0, 16, np.arange(T))
    put("cos_n", np.tile(co, (2, 1)))
    put("sin_n", np.tile(si, (2, 1)))
    cpos = np.arange(NCMP) * CSTRIDE + CBLOCK - 1
    co, si = rows(DH, 0, 16, cpos)
    put("cos_c", np.tile(co, (1, 2)))
    put("sin_c", np.tile(si, (1, 2)))
    q = np.arange(TT)[None, :, None] * P + np.arange(P)[:, None, None]
    put("mask_c", np.where(cpos[None, None, :] <= q, 0.0, NEG).reshape(P, -1))
    put("rowok", (q[:, :, 0] >= CBLOCK - 1))
    r = np.arange(P) % 64
    inv = np.power(f(500000.0), -np.arange(0, 16, 2, dtype=f) / f(16)).astype(f)
    put("invf", np.where(r < 16, inv[r % 8], 0.0)[:, None])
    put("sgn", np.where(r < 8, -1.0, np.where(r < 16, 1.0, 0.0))[:, None])
    put("rotm", (r < 16)[:, None])
    put("unrot", (r >= 16)[:, None])
    put("eps", np.full((P, 1), EPS))
    put("eps_mla", np.full((P, 1), MQK * EPS))
    put("select1", np.tile(np.arange(16) == 8, (P, 1)))
    side = np.arange(P)[:, None] // 64
    put("select2", np.arange(26)[None, :] == 12 + side)
    put("sum_scale", np.where(np.arange(13) < 8, 1.0, 1.0 / DH)[:, None])
    put("sum_eps", np.where(np.arange(13) < 8, DH * EPS, EPS)[:, None])
    put("eps_nsa", np.full((P, 1), DH * EPS))
    return c


def causal_bias():
    return np.where(np.arange(P)[None, :] <= np.arange(P)[:, None], 0.0, NEG).astype(np.float32)


def col_tiles(w, n0, count, kt=KD):
    k = w.shape[0]
    a = w[:, n0:n0 + count * P].reshape(k // P, P, count, P).transpose(2, 1, 0, 3)
    return a.reshape(count, P, (k // P) * P)


def put_chunks(stream, at, a):
    stream[at:at + a.shape[0], :, 0:a.shape[2]] = a


def pair_tiles(w):
    return w.reshape(4, P, 4, 2, P).transpose(2, 1, 3, 0, 4).reshape(4, P, -1)


def down_tiles(w):
    k = w.shape[0]
    return w.reshape(k // (2 * P), 2, P, 2, 4, P).transpose(0, 3, 2, 4, 1, 5).reshape(k // P, P, -1)


def by_rows(w, c0, width):
    k = w.shape[0]
    return w[:, c0:c0 + width].reshape(k // P, P, width).transpose(1, 0, 2)


def pack_first(stream, at, i, l):
    w = i["w_in"][l]
    o = np.cumsum([0, QRANK, KVRANK, MROPE, 2 * CONV_CH, 512, 768, 24])
    cq, ckv, kr, u2, qn, kvn, gn, gm = o
    b = at + C1["raw"]
    put_chunks(stream, b, col_tiles(w, cq, 3))
    put_chunks(stream, b + 3, col_tiles(w, ckv, 2))
    put_chunks(stream, b + 5, col_tiles(w, qn, 4))
    put_chunks(stream, b + 9, col_tiles(w, kvn + 256, 1))
    put_chunks(stream, b + 10, col_tiles(w, kvn + 512, 1))
    put_chunks(stream, b + 11, col_tiles(w, kvn, 1))
    b = at + C1["glu"]
    for c in range(CCH):
        put_chunks(stream, b + 2 * c, col_tiles(w, u2 + CONV_CH + c * P, 1))
        put_chunks(stream, b + 2 * c + 1, col_tiles(w, u2 + c * P, 1))
    b = at + C1["misc"]
    put_chunks(stream, b, col_tiles(w, kvn + 128, 1))
    s = stream[b + 1].reshape(P, 8, P)
    s[:, :, 64:96] = by_rows(w, kr, 32)
    s[:, :, 0:24] = by_rows(w, gn, 24)
    vv = np.concatenate([by_rows(w, kvn + 384, 128), by_rows(w, kvn + 640, 128)], axis=2)
    stream[b + 2] = vv[:, 0:4].reshape(P, -1)
    stream[b + 3] = vv[:, 4:8].reshape(P, -1)
    b = at + C1["mla"]
    uq = i["w_uq"][l].reshape(QRANK, NH, MQK)
    uq = np.concatenate([uq[:, :, MROPE:], uq[:, :, :MROPE]], axis=2)
    for h in range(NH):
        s = stream[b + h // 2].reshape(P, 8, P)
        s[:, (h % 2) * 3:(h % 2) * 3 + 3, 0:MQK] = uq[:, h].reshape(3, P, MQK).transpose(1, 0, 2)
    ukv = i["w_ukv"][l].reshape(KVRANK, NH, 128)
    nope = np.ascontiguousarray(ukv[:, :, :64]).reshape(2, P, 4, P)
    stream[b + 4] = nope.transpose(1, 2, 0, 3).reshape(P, -1)
    v = np.ascontiguousarray(ukv[:, :, 64:]).reshape(2, P, T)
    stream[b + 5] = v.transpose(1, 0, 2).reshape(P, -1)
    b = at + C1["cmp"]
    for n_, name in enumerate(("w_cmp_k", "w_cmp_v")):
        a = i[name + "1"][l].reshape(2, 8, P, P).transpose(0, 2, 1, 3).reshape(2, P, -1)
        stream[b + 2 * n_:b + 2 * n_ + 2] = a
        stream[b + 4 + n_, :, 0:64] = i[name + "2"][l]
    put_chunks(stream, at + C1["gate"], col_tiles(w, gm, 24))
    b = at + C1["merge"]
    for n_, name in enumerate(("w_o_mla", "w_o_nsa", "w_conv_out")):
        stream[b + 4 * n_:b + 4 * n_ + 4] = pair_tiles(i[name][l])
    put_chunks(stream, at + C1["wout"], col_tiles(i["w_out"][l], 0, 8))
    put_chunks(stream, at + C1["ff_up"], col_tiles(i["w_ff1"][l], 0, 32))
    stream[at + C1["ff_down"]:at + C1["ff_down"] + 32] = down_tiles(i["w_ff2"][l])


def pack_par1(i, l):
    c = np.zeros((P, NPAR), np.float32)

    def put(name, a):
        a = a.reshape(a.shape[0], -1)
        c[:a.shape[0], PAR1[name]:PAR1[name] + a.shape[1]] = a

    vec = lambda a: a.reshape(-1, P).T
    turned = lambda a: np.concatenate([a[MROPE:], a[:MROPE]])[:, None]
    for name, key in (("g_mix", "g_mix"), ("g_ffn", "g_ffn"), ("g_cq", "g_cq"), ("g_ckv", "g_ckv"), ("b_glu", "b_glu"),
                      ("b_dw", "b_dw"), ("g_ln", "g_conv_ln"), ("b_ln", "b_conv_ln"), ("b_out", "b_conv_out")):
        put(name, vec(i[key][l]))
    put("gq_mla", turned(i["g_q_mla"][l]))
    put("gk_mla", turned(i["g_k_mla"][l]))
    put("gq_nsa", np.concatenate([i["g_q_nsa"][l]] * 2)[:, None])
    put("gk_nsa", np.concatenate([i["g_k_nsa"][l]] * 2)[:, None])
    put("w_dw", i["w_dw"][l].reshape(TAPS, CCH, P).transpose(2, 1, 0))
    for n_, name in (("pe_k", "pe_cmp_k"), ("pe_v", "pe_cmp_v")):
        put(n_, i[name][l].reshape(16, P).T)
    return c


def modulation_chunks(w, first, count):
    return w.reshape(KD, P, 6, D)[:, :, first:first + count].transpose(0, 2, 1, 3).reshape(KD * count, P, D)


def pack_second(stream, at, i, l):
    w = i["w_in_2"][l]
    qa, ka, va, qi, ki, wi, qf, kf, vf, ff, gates = np.cumsum([0, 512, 64, 64, 512, 64, 8, 512, 512, 512, 8])
    b = at + C2["raw"]
    put_chunks(stream, b, col_tiles(w, qa, 4))
    put_chunks(stream, b + 4, col_tiles(w, qi, 4))
    b = at + C2["misc"]
    s = stream[b].reshape(P, 8, P)
    s[:, :, 0:64], s[:, :, 64:128] = by_rows(w, ka, 64), by_rows(w, ki, 64)
    s = stream[b + 1].reshape(P, 8, P)
    s[:, :, 0:64], s[:, :, 64:72], s[:, :, 72:80] = by_rows(w, va, 64), by_rows(w, ff, 8), by_rows(w, wi, 8)
    b = at + C2["fox"]
    put_chunks(stream, b, col_tiles(w, qf, 4))
    put_chunks(stream, b + 4, col_tiles(w, kf, 4))
    v = by_rows(w, vf, 512)
    for c in range(4):
        stream[b + 8 + c] = v[:, 2 * c:2 * c + 2].reshape(P, -1)
    put_chunks(stream, at + C2["gate"], col_tiles(w, gates, 16))
    for n_, name in enumerate(("w_branch_a_2", "w_branch_b_2")):
        b = at + C2["merge"] + 4 * n_
        stream[b:b + 4] = pair_tiles(i[name][l])
    put_chunks(stream, at + C2["wout"], col_tiles(i["w_out_2"][l], 0, 8))
    a = col_tiles(i["w_up_2"][l], 0, 44)
    put_chunks(stream, at + C2["ff_up"], a.reshape(2, NF2, P, -1).transpose(1, 0, 2, 3).reshape(44, P, -1))
    stream[at + C2["ff_down"]:at + C2["ff_down"] + NF2] = down_tiles(i["w_down_2"][l])


def pack_par2(i, l):
    c = np.zeros((P, NPAR), np.float32)

    def put(name, a):
        a = a.reshape(a.shape[0], -1)
        c[:, PAR2[name]:PAR2[name] + a.shape[1]] = a

    vec = lambda a: a.reshape(-1, P).T
    put("mod_b", vec(i["mod_b_2"][l]))
    put("g1", vec(i["norm1_g_2"][l]))
    put("g2", vec(i["norm2_g_2"][l]))
    put("fbias", np.tile(i["forget_bias_2"][l][None, :], (P, TT)))
    put("conv_w", i["conv_w_2"][l].reshape(3, 44, P).transpose(2, 0, 1))
    put("conv_b", vec(i["conv_b_2"][l]))
    return c


def triangle():
    return (np.arange(T)[None, :] >= np.arange(P)[:, None]).astype(np.float32)


def host_arrays(i):
    stream = np.zeros((NCHUNKS + RING, P, CHUNK), np.float32)
    for l in range(DEPTH):
        pack_first(stream, l * NC1, i, l)
        pack_second(stream, BASE2 + l * NC2, i, l)
    vecs = np.concatenate([i["final_g_2"].reshape(KD, P).T, i["c_2"].reshape(KD, P).T], axis=1)
    first = [modulation_chunks(i["mod_w_2"][l], 0, 2) for l in range(DEPTH)]
    return {"wstream": stream, "modw_first": np.concatenate(first + [np.zeros_like(first[0])]), "modw": np.concatenate([modulation_chunks(i["mod_w_2"][l], 2, 4) for l in range(DEPTH)]),
            "par1": np.stack([pack_par1(i, l) for l in range(DEPTH)]),
            "par2": np.stack([pack_par2(i, l) for l in range(DEPTH)]),
            "con": constants(), "causal": causal_bias(), "tri": triangle(), "vecs": np.ascontiguousarray(vecs),
            "pos": np.ascontiguousarray(i["positions_2"].reshape(1, T)), "xT": np.ascontiguousarray(i["x"][0].T)}


def kernel(**inputs):
    import concourse.bacc as bacc
    from concourse.bass_utils import run_bass_kernel_spmd

    i = {name: np.asarray(a) for name, a in inputs.items()}
    arrays = host_arrays(i)
    nc = bacc.Bacc("TRN2", target_bir_lowering=False, num_devices=1)
    args = [nc.dram_tensor(n_, a.shape, mybir.dt.from_np(a.dtype), kind="ExternalInput").ap() for n_, a in arrays.items()]
    out = nc.dram_tensor("outT", (D, T), F32, kind="ExternalOutput").ap()
    build(nc, *args, out)
    r = run_bass_kernel_spmd(nc, [arrays], core_ids=[0])
    return np.ascontiguousarray(np.asarray(r.results[0]["outT"]).T).reshape(1, T, D)
```
